# Optimizing a Trainium2 kernel written in Bass

```python
import math
import jax, jax.numpy as jnp
from jax import lax
import numpy as np

D_MODEL = 1024
BATCH = 1
SEQ = 512
DEPTH = 2
DEC_BATCH = 8
DEC_SEQ = 1
PAST_LEN = 256
PAGE_SIZE = 128

H_A = 4
DK_A = 128
DV_A = 128
RET_CHUNK = 128
ROPE_BASE = 10000.0
H_B = 4
DH_B = 64
DV_B = 2 * DH_B
Q_BLOCK = 128
N_BUCKETS = 32
MAX_DISTANCE = 128
H_C = 8
DH_C = 64
R_DECAY = 64
R_A = 64
R_V = 32
R_G = 160
LNX_EPS = 64e-5
W_AQ = H_A * DK_A
W_A = H_A * DV_A
W_BQK = H_B * 2 * DH_B
W_B = H_B * DV_B
W_C = H_C * DH_C
D_FF = 4 * D_MODEL
RET_COLS = 2 * W_AQ + 2 * W_A
DIFF_COLS = 2 * W_BQK + W_B
RWKV_COLS = 3 * W_C + R_DECAY + R_A + R_G
GATE_COLS = 3 * D_MODEL
IN_COLS = RET_COLS + DIFF_COLS + RWKV_COLS + GATE_COLS
EPS = 1e-6

kernel_name = 'hybrid_retention_diffattn_rwkv7_decoder_step'

def rms_norm(x, gain=None):
    xf = x.astype(jnp.float32)
    y = xf * lax.rsqrt(jnp.mean(xf * xf, axis=-1, keepdims=True) + EPS)
    if gain is not None:
        y = y * gain.astype(jnp.float32)
    return y.astype(x.dtype)

def rope(x, pos):
    half = x.shape[-1] // 2
    inv = ROPE_BASE ** (-jnp.arange(half, dtype=jnp.float32) / half)
    ang = pos.astype(jnp.float32)[:, None] * inv[None, :]
    cos = jnp.cos(ang)[None, :, None, :]
    sin = jnp.sin(ang)[None, :, None, :]
    x1, x2 = x[..., :half], x[..., half:]
    return jnp.concatenate([x1 * cos - x2 * sin, x1 * sin + x2 * cos], axis=-1)

def retention_chunked(q, k, v, s0):
    B, L = q.shape[0], q.shape[1]
    C = math.gcd(L, RET_CHUNK)
    n = L // C
    log_g = jnp.log1p(-jnp.exp2(-5.0 - jnp.arange(H_A, dtype=jnp.float32)))
    i = jnp.arange(C, dtype=jnp.float32)
    dist = i[:, None] - i[None, :]
    causal = dist >= 0
    inner = jnp.where(causal[None], jnp.exp(jnp.where(causal, dist, 0.0)[None] * log_g[:, None, None]), 0.0)
    cross = jnp.exp((i[:, None] + 1.0) * log_g[None, :])
    tail = jnp.exp((C - 1.0 - i)[:, None] * log_g[None, :])
    chunk = jnp.exp(C * log_g)

    def split(t):
        return t.reshape(B, n, C, *t.shape[2:]).swapaxes(0, 1)

    def step(S, blk):
        qc, kc, vc = blk
        sc = jnp.einsum('bihd,bjhd->bhij', qc, kc) * inner
        o = (jnp.einsum('bhij,bjhe->bihe', sc, vc)
             + jnp.einsum('bihd,bhde->bihe', qc, S) * cross[None, :, :, None])
        S = S * chunk[None, :, None, None] + jnp.einsum('bjhd,bjhe->bhde', kc * tail[None, :, :, None], vc)
        return S, o

    S, o = lax.scan(step, s0, (split(q), split(k), split(v)))
    return o.swapaxes(0, 1).reshape(B, L, H_A, DV_A), S

def t5_bias(table, q_pos, k_pos):
    n = jnp.maximum(q_pos[:, None] - k_pos[None, :], 0)
    max_exact = N_BUCKETS // 2
    nf = jnp.maximum(n, 1).astype(jnp.float32)
    large = max_exact + (jnp.log(nf / max_exact) / math.log(MAX_DISTANCE / max_exact)
                         * (N_BUCKETS - max_exact)).astype(jnp.int32)
    large = jnp.minimum(large, N_BUCKETS - 1)
    bucket = jnp.where(n < max_exact, n, large)
    return jnp.moveaxis(table[bucket], -1, 0)

def diff_attend(q, k, v, q_pos, k_pos, bias_table, lam):
    s = jnp.einsum('bqhcd,bkhcd->bhcqk', q, k).astype(jnp.float32)
    s = s + t5_bias(bias_table, q_pos, k_pos).astype(jnp.float32)[None, :, None]
    s = jnp.where((k_pos[None, :] <= q_pos[:, None])[None, None, None], s, -jnp.inf)
    p = jax.nn.softmax(s, axis=-1)
    a = p[:, :, 0] - lam * p[:, :, 1]
    return jnp.einsum('bhqk,bkhe->bqhe', a.astype(v.dtype), v)

def diff_attend_blocked(q, k, v, pos, bias_table, lam):
    B, L = q.shape[0], q.shape[1]
    bq = math.gcd(L, Q_BLOCK)
    nb = L // bq
    qb = q.reshape(B, nb, bq, H_B, 2, DH_B).swapaxes(0, 1)
    pb = pos.reshape(nb, bq)
    out = lax.map(lambda a: diff_attend(a[0], k, v, a[1], pos, bias_table, lam), (qb, pb))
    return out.swapaxes(0, 1).reshape(B, L, H_B, DV_B)

def rwkv7_scan(r, w, k, v, a_vec, b_vec, s0):
    def step(S, inp):
        rt, wt, kt, vt, at, bt = inp
        sa = jnp.einsum('bhij,bhj->bhi', S, at)
        S = S * wt[:, :, None, :] + sa[..., None] * bt[:, :, None, :] + vt[..., None] * kt[:, :, None, :]
        return S, jnp.einsum('bhij,bhj->bhi', S, rt)
    xs = tuple(t.swapaxes(0, 1) for t in (r, w, k, v, a_vec, b_vec))
    S, y = lax.scan(step, s0, xs)
    return y.swapaxes(0, 1), S

def trunk(x, c, pos, ret_s0, rwkv_s0, shift0, paged, p):
    B, L, _ = x.shape
    dt = x.dtype
    f32 = jnp.float32
    k_rows, v_rows, ret_out, rwkv_out, shift_out = [], [], [], [], []
    v_first = None
    for l in range(DEPTH):
        mod = jnp.einsum('bd,de->be', jax.nn.silu(c), p['w_ada'][l]) + p['b_ada'][l]
        sh1, sc1, gt1, sh2, sc2, gt2 = jnp.split(mod[:, None, :], 6, axis=-1)
        h = rms_norm(x, p['norm1'][l]) * (1 + sc1) + sh1
        z = jnp.einsum('bld,de->ble', h, p['w_in'][l])
        z_ret, z_diff, z_rwkv, z_gate = jnp.split(
            z, [RET_COLS, RET_COLS + DIFF_COLS, RET_COLS + DIFF_COLS + RWKV_COLS], axis=-1)

        qa, ka, va, ga = jnp.split(z_ret, [W_AQ, 2 * W_AQ, 2 * W_AQ + W_A], axis=-1)
        qa = rope(qa.reshape(B, L, H_A, DK_A).astype(f32), pos)
        ka = rope(ka.reshape(B, L, H_A, DK_A).astype(f32), pos) * (DK_A ** -0.5)
        oa, s_ret = retention_chunked(qa, ka, va.reshape(B, L, H_A, DV_A).astype(f32), ret_s0[l].astype(f32))
        ya = rms_norm(oa).reshape(B, L, W_A).astype(dt) * jax.nn.silu(ga)

        qb, kb, vb = jnp.split(z_diff, [W_BQK, 2 * W_BQK], axis=-1)
        qb = rms_norm(qb.reshape(B, L, H_B, 2, DH_B), p['qk_norm_q'][l]) * (DH_B ** -0.5)
        kb = rms_norm(kb.reshape(B, L, H_B, 2, DH_B), p['qk_norm_k'][l])
        vb = vb.reshape(B, L, H_B, DV_B)
        lam_init = 0.8 - 0.6 * math.exp(-0.3 * l)
        lam = (jnp.exp(jnp.sum(p['lambda_q1'][l].astype(f32) * p['lambda_k1'][l].astype(f32)))
               - jnp.exp(jnp.sum(p['lambda_q2'][l].astype(f32) * p['lambda_k2'][l].astype(f32))) + lam_init)
        if paged is None:
            ob = diff_attend_blocked(qb, kb, vb, pos, p['rel_bias'], lam)
        else:
            ck, cv, pt = paged
            nbd, npg = pt.shape
            k_past = ck[l, pt].reshape(nbd, npg * PAGE_SIZE, H_B, 2, DH_B).astype(dt)
            v_past = cv[l, pt].reshape(nbd, npg * PAGE_SIZE, H_B, DV_B).astype(dt)
            k_all = jnp.concatenate([k_past, kb], axis=1)
            v_all = jnp.concatenate([v_past, vb], axis=1)
            k_pos = jnp.arange(npg * PAGE_SIZE + L)
            ob = diff_attend(qb, k_all, v_all, pos, k_pos, p['rel_bias'], lam)
        yb = (rms_norm(ob, p['subln_diff'][l]) * (1.0 - lam_init)).reshape(B, L, W_B)
        k_rows.append(kb.reshape(B, L, H_B, 2 * DH_B))
        v_rows.append(vb)

        zprev = jnp.concatenate([shift0[l].astype(dt), z_rwkv[:, :-1]], axis=1)
        zs = z_rwkv + (zprev - z_rwkv) * p['mu_shift'][l]
        shift_out.append(z_rwkv[:, -1:])
        rc, kc, vc, wd, ad, gd = jnp.split(
            zs, [W_C, 2 * W_C, 3 * W_C, 3 * W_C + R_DECAY, 3 * W_C + R_DECAY + R_A], axis=-1)
        w = -jax.nn.softplus(-(p['w0'][l] + jnp.tanh(wd) @ p['w_decay_up'][l]).astype(f32)) - 0.5
        decay = jnp.exp(-jnp.exp(w))
        if l == 0:
            v_first = vc
        else:
            vgate = jax.nn.sigmoid(p['v0'][l - 1] + (vc @ p['w_v_down'][l - 1]) @ p['w_v_up'][l - 1])
            vc = vc + (v_first - vc) * vgate
        a = jax.nn.sigmoid((p['a0'][l] + ad @ p['w_a_up'][l]).astype(f32))
        gg = jax.nn.sigmoid(gd) @ p['w_g_up'][l]
        kk = (kc * p['k_k'][l]).astype(f32).reshape(B, L, H_C, DH_C)
        kk = kk / jnp.maximum(jnp.sqrt(jnp.sum(kk * kk, axis=-1, keepdims=True)), 1e-12)
        kc = kc.astype(f32) * (1.0 + (a - 1.0) * p['k_a'][l].astype(f32))
        hs = (B, L, H_C, DH_C)
        r_h = rc.astype(f32).reshape(hs)
        k_h = kc.reshape(hs)
        v_h = vc.astype(f32).reshape(hs)
        a_h = a.reshape(hs)
        yc, s_rwkv = rwkv7_scan(r_h, decay.reshape(hs), k_h, v_h, -kk, kk * a_h, rwkv_s0[l].astype(f32))
        mu_c = jnp.mean(yc, axis=-1, keepdims=True)
        var_c = jnp.mean(jnp.square(yc - mu_c), axis=-1, keepdims=True)
        yc = ((yc - mu_c) * lax.rsqrt(var_c + LNX_EPS)).reshape(B, L, W_C) * p['lnx_g'][l] + p['lnx_b'][l]
        yc = yc + (jnp.sum(r_h * k_h * p['r_k'][l].astype(f32), axis=-1, keepdims=True) * v_h).reshape(B, L, W_C)
        yc = yc.astype(dt) * gg

        gate_a, gate_b, gate_c = jnp.split(jax.nn.sigmoid(z_gate), 3, axis=-1)
        merged = (gate_a * (ya @ p['w_up_a'][l]) + gate_b * (yb @ p['w_up_b'][l])
                  + gate_c * (yc @ p['w_up_c'][l]))
        x = x + gt1 * (merged @ p['w_out'][l])

        h2 = rms_norm(x, p['norm2'][l]) * (1 + sc2) + sh2
        x = x + gt2 * (jnp.square(jax.nn.relu(h2 @ p['w_ff1'][l])) @ p['w_ff2'][l])

        ret_out.append(s_ret.astype(dt))
        rwkv_out.append(s_rwkv.astype(dt))
    return (x, jnp.stack(k_rows), jnp.stack(v_rows), jnp.stack(ret_out),
            jnp.stack(rwkv_out), jnp.stack(shift_out))

def setup_inputs(seed: int = 0) -> dict:
    key = jax.random.key(seed)
    keys = jax.random.split(key, 64)
    ctr = [0]
    f32 = jnp.float32

    def nk():
        ctr[0] += 1
        return keys[ctr[0] - 1]

    def nrm(shape, scale=1.0):
        return jax.random.normal(nk(), shape, f32) * scale

    def gain(shape):
        return 1.0 + 0.02 * jax.random.normal(nk(), shape, f32)

    D = D_MODEL
    n_pages = PAST_LEN // PAGE_SIZE
    n_pool = (DEC_BATCH * n_pages * 5) // 4
    x_prompt = nrm((BATCH, SEQ, D))
    x_sample = nrm((DEC_BATCH, DEC_SEQ, D))
    c_prompt = nrm((BATCH, D))
    c_sample = nrm((DEC_BATCH, D))
    cache_k_diff = nrm((DEPTH, n_pool, PAGE_SIZE, H_B, 2 * DH_B))
    cache_v_diff = nrm((DEPTH, n_pool, PAGE_SIZE, H_B, DV_B))
    page_table = jax.random.permutation(nk(), n_pool)[:DEC_BATCH * n_pages].reshape(
        DEC_BATCH, n_pages).astype(jnp.int32)
    state_ret = nrm((DEPTH, DEC_BATCH, H_A, DK_A, DV_A), 0.3)
    state_rwkv = nrm((DEPTH, DEC_BATCH, H_C, DH_C, DH_C), 0.1)
    state_shift = nrm((DEPTH, DEC_BATCH, 1, RWKV_COLS))
    return {
        'x_prompt': x_prompt, 'x_sample': x_sample, 'c_prompt': c_prompt, 'c_sample': c_sample,
        'cache_k_diff': cache_k_diff, 'cache_v_diff': cache_v_diff, 'page_table': page_table,
        'state_ret': state_ret, 'state_rwkv': state_rwkv, 'state_shift': state_shift,
        'rel_bias': nrm((N_BUCKETS, H_B), 0.5),
        'w_ada': nrm((DEPTH, D, 6 * D), 0.5 * D ** -0.5),
        'b_ada': nrm((DEPTH, 6 * D), 0.02),
        'norm1': gain((DEPTH, D)),
        'norm2': gain((DEPTH, D)),
        'w_in': nrm((DEPTH, D, IN_COLS), D ** -0.5),
        'qk_norm_q': gain((DEPTH, DH_B)),
        'qk_norm_k': gain((DEPTH, DH_B)),
        'lambda_q1': nrm((DEPTH, DH_B), 0.1),
        'lambda_k1': nrm((DEPTH, DH_B), 0.1),
        'lambda_q2': nrm((DEPTH, DH_B), 0.1),
        'lambda_k2': nrm((DEPTH, DH_B), 0.1),
        'subln_diff': gain((DEPTH, DV_B)),
        'mu_shift': jax.random.uniform(nk(), (DEPTH, RWKV_COLS), f32, 0.0, 1.0),
        'w0': jax.random.uniform(nk(), (DEPTH, W_C), f32, -6.0, -1.0),
        'w_decay_up': nrm((DEPTH, R_DECAY, W_C), 0.1),
        'a0': nrm((DEPTH, W_C), 0.1),
        'w_a_up': nrm((DEPTH, R_A, W_C), 0.1),
        'w_g_up': nrm((DEPTH, R_G, W_C), R_G ** -0.5),
        'v0': nrm((DEPTH - 1, W_C), 0.1),
        'w_v_down': nrm((DEPTH - 1, W_C, R_V), W_C ** -0.5),
        'w_v_up': nrm((DEPTH - 1, R_V, W_C), 0.1),
        'k_k': 0.85 + 0.02 * jax.random.normal(nk(), (DEPTH, W_C), f32),
        'k_a': gain((DEPTH, W_C)),
        'r_k': nrm((DEPTH, H_C, DH_C), 0.1),
        'lnx_g': gain((DEPTH, W_C)),
        'lnx_b': nrm((DEPTH, W_C), 0.02),
        'w_up_a': nrm((DEPTH, W_A, D), W_A ** -0.5),
        'w_up_b': nrm((DEPTH, W_B, D), W_B ** -0.5),
        'w_up_c': nrm((DEPTH, W_C, D), W_C ** -0.5),
        'w_out': nrm((DEPTH, D, D), D ** -0.5),
        'w_ff1': nrm((DEPTH, D, D_FF), D ** -0.5),
        'w_ff2': nrm((DEPTH, D_FF, D), D_FF ** -0.5),
    }

def reference(x_prompt, x_sample, c_prompt, c_sample, cache_k_diff, cache_v_diff, page_table,
              state_ret, state_rwkv, state_shift, rel_bias, w_ada, b_ada, norm1, norm2, w_in,
              qk_norm_q, qk_norm_k, lambda_q1, lambda_k1, lambda_q2, lambda_k2, subln_diff,
              mu_shift, w0, w_decay_up, a0, w_a_up, w_g_up, v0, w_v_down, w_v_up, k_k, k_a, r_k,
              lnx_g, lnx_b, w_up_a, w_up_b, w_up_c, w_out, w_ff1, w_ff2):
    p = dict(rel_bias=rel_bias, w_ada=w_ada, b_ada=b_ada, norm1=norm1, norm2=norm2, w_in=w_in,
             qk_norm_q=qk_norm_q, qk_norm_k=qk_norm_k, lambda_q1=lambda_q1, lambda_k1=lambda_k1,
             lambda_q2=lambda_q2, lambda_k2=lambda_k2, subln_diff=subln_diff, mu_shift=mu_shift,
             w0=w0, w_decay_up=w_decay_up, a0=a0, w_a_up=w_a_up, w_g_up=w_g_up, v0=v0,
             w_v_down=w_v_down, w_v_up=w_v_up, k_k=k_k, k_a=k_a, r_k=r_k, lnx_g=lnx_g, lnx_b=lnx_b,
             w_up_a=w_up_a, w_up_b=w_up_b, w_up_c=w_up_c, w_out=w_out, w_ff1=w_ff1, w_ff2=w_ff2)
    bp, lp = x_prompt.shape[0], x_prompt.shape[1]
    dtp = x_prompt.dtype
    pos_p = jnp.arange(lp)
    past = page_table.shape[1] * PAGE_SIZE
    pos_s = past + jnp.arange(x_sample.shape[1])
    ret0 = jnp.zeros((DEPTH, bp, H_A, DK_A, DV_A), dtp)
    rwkv0 = jnp.zeros((DEPTH, bp, H_C, DH_C, DH_C), dtp)
    shift_init = jnp.zeros((DEPTH, bp, 1, RWKV_COLS), dtp)
    y_prompt, k_p, v_p, ret_p, rwkv_p, shift_p = trunk(
        x_prompt, c_prompt, pos_p, ret0, rwkv0, shift_init, None, p)
    y_sample, k_s, v_s, ret_s, rwkv_s, shift_s = trunk(
        x_sample, c_sample, pos_s, state_ret, state_rwkv, state_shift,
        (cache_k_diff, cache_v_diff, page_table), p)
    return (y_prompt, y_sample, k_p, v_p, k_s, v_s, ret_p, ret_s, rwkv_p, rwkv_s, shift_p, shift_s)


_drawn_inputs = setup_inputs


def setup_inputs(seed=0):
    import zlib

    import numpy as np

    out = dict(_drawn_inputs(seed))
    spreads = {}
    factors = {'norm2': 4.364,
     'qk_norm_q': 8.0,
     'qk_norm_k': 2.845,
     'lambda_q1': 5.257,
     'lambda_k1': 32.497,
     'lambda_q2': 8.0,
     'subln_diff': 27.368,
     'lnx_g': 37.618,
     'lnx_b': 35.61}
    for name, (base, spread) in spreads.items():
        noise = np.random.default_rng([zlib.crc32(name.encode()), seed]).standard_normal(out[name].shape)
        drawn = base * np.exp(spread * noise) if base else spread * noise
        out[name] = __import__('jax').numpy.asarray(drawn.astype(out[name].dtype))
    for name, factor in factors.items():
        out[name] = (out[name] * factor).astype(out[name].dtype)
    return out
```

```python
import math
from contextlib import ExitStack

import numpy as np

import concourse.bass as bass
from concourse import mybir

F32 = mybir.dt.float32
I32 = mybir.dt.int32
ALU = mybir.AluOpType
ACT = mybir.ActivationFunctionType
AX = mybir.AxisListType

P = 128
D = 1024
KD = D // P
SEQ = 512
MT = SEQ // P
DEC = 8
T = SEQ + DEC
DEPTH = 2
PAST, PAGE = 256, 128
NPG = PAST // PAGE
NB = 32
HA, DA = 4, 128
HB, DB, DVB = 4, 64, 128
HC, DC = 8, 64
HP = HC // 2
W = 512
CH = 64
RW = 3 * W + 64 + 64 + 160
RT = 15
RET0, DIFF0, RW0 = 0, 2048, 3584
GATE0 = RW0 + RW
DFF = 4096
KF = DFF // P
EPS = 1e-6
LNX_EPS = 64e-5
MASKED = -1e30
TOE = 640

_c = 0
COL = {}
for _n, _w in (("ident", P), ("ones", P), ("blk", P), ("inner", HA * P), ("cross", HA * P), ("keep", 2 * P),
               ("level", 6 * P), ("cosq", 320), ("sinq", 320), ("cosk", 320), ("sink", 320), ("tail", HA),
               ("chunk", HA), ("gamma", HA), ("scan", T), ("c0", HB * DEC), ("c1", HB * DEC), ("selb", DEC),
               ("pair", 2), ("laminit", 2 * DEPTH), ("vmix", DEPTH), ("toe", TOE), ("past", NPG * P)):
    COL[_n] = (_c, _w)
    _c += _w
NCONST = _c
NKEPT = COL["toe"][0]

PROW = {}
_r = 0
for _n, _w in (("b_ada", 48), ("norm1", 8), ("norm2", 8), ("mu", 15), ("w0", 4), ("a0", 4), ("v0", 4),
               ("k_k", 4), ("k_a", 4), ("r_k", 4)):
    PROW[_n] = (_r, _w)
    _r += _w
NPAR = _r

BROW = {}
_b = 0
for _n, _w in (("qn", 64), ("kn", 64), ("lq1", 64), ("lk1", 64), ("lq2", 64), ("lk2", 64), ("subln", 128),
               ("lnx_g", 512), ("lnx_b", 512)):
    BROW[_n] = (_b, _w)
    _b += _w
NROW = _b


def shape_constants():
    t = np.zeros((P, NCONST), np.float32)

    def put(name, a):
        o, w = COL[name]
        a = np.asarray(a, np.float32)
        a = a.reshape(a.shape[0], -1)
        assert a.shape[1] == w, (name, a.shape)
        t[:a.shape[0], o:o + w] = a

    i = np.arange(P)
    put("ident", np.eye(P))
    put("ones", np.ones((P, P)))
    put("blk", (i[:, None] // 64) == (i[None, :] // 64))
    log_g = np.log1p(-np.exp2(-5.0 - np.arange(HA, dtype=np.float32))).astype(np.float32)
    dist = i[None, :] - i[:, None]
    put("inner", np.stack([np.where(dist >= 0, np.exp(np.maximum(dist, 0) * g), 0.0) for g in log_g], 1))
    put("cross", np.broadcast_to(np.stack([np.exp((i + 1.0) * g) for g in log_g])[None], (P, HA, P)))
    put("tail", np.exp((P - 1.0 - i)[:, None] * log_g[None]))
    put("chunk", np.broadcast_to(np.exp(P * log_g)[None], (P, HA)))
    put("gamma", np.broadcast_to(np.exp(log_g)[None], (P, HA)))
    same = (i[:, None] // CH) == (i[None, :] // CH)
    before = same & (i[:, None] < i[None, :])
    upto = same & (i[:, None] <= i[None, :])
    put("keep", np.stack([before, upto], 1))
    lv = []
    for k in range(6):
        m = 1 << k
        lv.append((i[:, None] // (2 * m) == i[None, :] // (2 * m)) & (i[:, None] % (2 * m) < m)
                  & (i[None, :] % (2 * m) >= m))
    put("level", np.stack(lv, 1))
    half = DA // 2
    inv = (np.float32(10000.0) ** (-np.arange(half, dtype=np.float32) / np.float32(half))).astype(np.float32)
    pos = np.zeros((P, 5), np.float32)
    for m in range(MT):
        pos[:, m] = m * P + i
    pos[:, 4] = PAST
    ang = (pos[:, :, None] * inv[None, None, :]).astype(np.float32)
    cs, sn = np.cos(ang), np.sin(ang)
    sc = DA ** -0.5
    put("cosq", cs)
    put("sinq", sn)
    put("cosk", cs * sc)
    put("sink", sn * sc)
    scan = np.ones(T)
    scan[0:SEQ:CH] = 0
    scan[SEQ:] = 0
    put("scan", np.broadcast_to(scan[None], (P, T)))

    def bucket(n):
        n = np.maximum(n, 0)
        nf = np.maximum(n, 1).astype(np.float32)
        large = 16 + (np.log(nf / np.float32(16)).astype(np.float32) / np.float32(math.log(128 / 16))
                      * np.float32(16)).astype(np.int32)
        return np.where(n < 16, n, np.minimum(large, NB - 1))

    n = 511 - np.arange(TOE)
    toe = np.zeros((NB + 1, TOE), np.float32)
    toe[bucket(n), np.arange(TOE)] = (n >= 0)
    toe[NB] = np.where(n >= 0, 0.0, 1.0)
    put("toe", toe)
    n = PAST - np.arange(PAST)
    past = np.zeros((NB, PAST), np.float32)
    past[bucket(n), np.arange(PAST)] = 1
    put("past", past)
    r = np.arange(DEC * 8)
    bb, hh, cc = r // 8, (r // 2) % 4, r % 2
    col = np.arange(HB * DEC)
    hit = (bb[:, None] == col[None] % DEC) & (hh[:, None] == col[None] // DEC)
    put("c0", hit & (cc[:, None] == 0))
    put("c1", hit & (cc[:, None] == 1))
    put("selb", bb[:, None] == np.arange(DEC)[None])
    put("pair", (i[:, None] // 64) == np.arange(2)[None])
    li = [0.8 - 0.6 * math.exp(-0.3 * l) for l in range(DEPTH)]
    put("laminit", np.broadcast_to(np.array([[x, 1.0 - x] for x in li])[None], (P, DEPTH, 2)))
    put("vmix", np.broadcast_to((np.arange(DEPTH) > 0)[None], (P, DEPTH)))
    return t


class Count:

    def __init__(self, sem):
        self.sem, self.base, self.i, self.per, self.j = sem, 0, None, 0, 0

    def next(self, by=1):
        self.j += by
        if self.i is None:
            self.base, self.j = self.base + self.j, 0
            return self.base
        return self.i * self.per + (self.base + self.j)

    def skip(self, n):
        assert self.i is None
        self.base += n

    def enter(self, i, per):
        self.i, self.per = i, per

    def leave(self, n):
        assert self.j == self.per, (self.j, self.per)
        self.base, self.i, self.j = self.base + n * self.per, None, 0


class Chain(Count):

    def __init__(self, eng, sem):
        super().__init__(sem)
        self.eng = eng

    def __call__(self, ins):
        ins.then_inc(self.sem, 1)
        self.eng.wait_ge(self.sem, self.next())


def build(nc, a, consts, outs):
    (y_p, y_s, k_p, v_p, k_s, v_s, ret_p, ret_s, rwkv_p, rwkv_s, shift_p, shift_s) = outs
    skew = nc.dram_tensor("skew_dram", (HB, P, TOE), F32, kind="Internal").ap()
    V, S, G, PE = nc.vector, nc.scalar, nc.gpsimd, nc.tensor
    with ExitStack() as ctx:
        def sb(name, n, dt=F32, p=P):
            return ctx.enter_context(nc.sbuf_tensor(name, [p, n], dt))

        xT = sb("xT", KD * T)[:, :].rearrange("p (k t) -> p k t", k=KD)
        hT = sb("hT", KD * T)[:, :].rearrange("p (k t) -> p k t", k=KD)
        ring = [sb("ring0", 4096)[:, :], sb("ring1", 4096)[:, :]]
        vfirst = sb("vfirst", HP * T)[:, :].rearrange("p (k t) -> p k t", k=HP)
        y_raw = sb("yT", 12 * T)[:, :]
        yT = y_raw.rearrange("p (k t) -> p k t", k=12)
        modT = sb("modT", 48 * 9)[:, :].rearrange("p (k s) -> p k s", k=48)
        coef = sb("coef", KD * 9)[:, :].rearrange("p (k s) -> p k s", k=KD)
        csT = sb("csT", KD * 9)[:, :].rearrange("p (k s) -> p k s", k=KD)
        par = sb("par", NPAR)[:, :]
        rows = sb("rows", NROW)[:, :]
        cst = sb("cst", NKEPT)[:, :]
        biasD = sb("biasD", NPG * HB)[:, :].rearrange("p (g h) -> p g h", g=NPG)
        bias0 = sb("bias0", HB)[:, :]
        tab = sb("tab", HB)[:, :]
        rstd = sb("rstd", T)[:, :]
        small = sb("small", 512)[:, :]
        pages = sb("pages", DEC * NPG, I32, 1)[:, :]
        AR = 20720
        arena = sb("arena", AR)[:, :]
        pb = [ctx.enter_context(nc.psum_tensor(f"pb{i}", [P, 512], F32))[:, :] for i in range(8)]

        def at(base, off, *dims):
            n = 1
            for d in dims:
                n *= d
            ap = base[:, off:off + n]
            if len(dims) == 2:
                return ap.rearrange("p (a b) -> p a b", a=dims[0])
            if len(dims) == 3:
                return ap.rearrange("p (a b c) -> p a b c", a=dims[0], b=dims[1])
            if len(dims) == 4:
                return ap.rearrange("p (a b c d) -> p a b c d", a=dims[0], b=dims[1], c=dims[2])
            return ap

        def C(name, *dims):
            return at(cst, COL[name][0], *(dims or (COL[name][1],)))

        def PR(name):
            return par[:, PROW[name][0]:PROW[name][0] + PROW[name][1]]

        def BR(name):
            return rows[:, BROW[name][0]:BROW[name][0] + BROW[name][1]]

        ident, ones, blk = C("ident"), C("ones"), C("blk")
        eps = small[:, 0:1]
        eps_ln = small[:, 1:2]
        lam = small[:, 2:3]

        def sem(name):
            return ctx.enter_context(nc.semaphore(name))

        sems = {n: sem(n) for n in (
            "slot0_full", "slot1_full", "slot0_free", "slot1_free", "loaded", "loaded_act", "stored",
            "pe_for_dve", "dve_for_pe", "pe_for_act", "act_for_pe", "dve_for_act", "act_for_dve",
            "dve_done", "act_done", "sp_for_dve", "dve_for_sp", "page_full", "page_free")}
        pe_for_dve, dve_for_pe = sems["pe_for_dve"], sems["dve_for_pe"]
        pe_for_act, act_for_pe = sems["pe_for_act"], sems["act_for_pe"]
        dve_for_act, act_for_dve = sems["dve_for_act"], sems["act_for_dve"]
        loaded, stored = sems["loaded"], sems["stored"]
        dve_for_sp = sems["dve_for_sp"]
        page_full, page_free = sems["page_full"], sems["page_free"]
        slot_full = [sems["slot0_full"], sems["slot1_full"]]
        slot_free = [sems["slot0_free"], sems["slot1_free"]]

        def counts():
            c = {
                "pe_full": [Count(s) for s in slot_full], "sp_free": [Count(s) for s in slot_free],
                "dve_from_pe": Count(pe_for_dve), "pe_from_dve": Count(dve_for_pe),
                "act_from_pe": Count(pe_for_act), "pe_from_act": Count(act_for_pe),
                "act_from_dve": Count(dve_for_act), "dve_from_act": Count(act_for_dve),
                "dve": Chain(V, sems["dve_done"]), "act": Chain(S, sems["act_done"]),
                "loaded": Count(loaded), "stored": Count(stored),
                "sp_from_dve": Count(dve_for_sp), "dve_page": Count(page_full), "pe_page": Count(page_full),
                "sp_page": Count(page_free),
            }
            return c

        def clear():
            with nc.Block() as block:
                @block.gpsimd
                def _(g):
                    for s in sems.values():
                        g.sem_clear(s)

        def mm(out, lhsT, rhs, start=True, stop=True):
            return PE.matmul(out, lhsT, rhs, start=start, stop=stop, skip_group_check=True)

        def tr(out, in_):
            return PE.transpose(out, in_, ident[0:in_.shape[0], 0:in_.shape[0]])

        def bc(ap, shape, *dims):
            for d in dims:
                ap = ap.unsqueeze(d)
            return ap.broadcast_to(shape)

        mult, add, sub, amax = ALU.mult, ALU.add, ALU.subtract, ALU.max

        c = counts()
        dist_rows = arena[:, 11000:11000 + NCONST - NKEPT]
        toe, past = dist_rows[:, 0:TOE], dist_rows[:, TOE:TOE + NPG * P]
        with nc.Block() as block:
            @block.vector
            def _(v):
                c["dve"](V.memset(arena[:, 4096:6144], 0.0))
        with nc.Block() as block:
            @block.sync
            def _(sp):
                sp.dma_start(cst, consts[:, 0:NKEPT]).then_inc(loaded, 16)
                sp.dma_start(dist_rows, consts[:, NKEPT:NCONST]).then_inc(loaded, 16)
                sp.dma_start(at(arena, 0, MT, D), a["x_prompt"].rearrange("o (m p) d -> p (o m) d", p=P)).then_inc(loaded, 16)
                sp.dma_start(arena[0:DEC, 4096:5120], a["x_sample"].rearrange("b o d -> b (o d)")).then_inc(loaded, 16)
                sp.dma_start(arena[0:1, 5120:6144], a["c_prompt"]).then_inc(loaded, 16)
                sp.dma_start(arena[1:9, 5120:6144], a["c_sample"]).then_inc(loaded, 16)
                sp.dma_start(tab[0:NB, :], a["rel_bias"]).then_inc(loaded, 16)
                sp.dma_start(bias0, a["rel_bias"][0].partition_broadcast(P)).then_inc(loaded, 16)
                sp.dma_start(pages, a["page_table"].rearrange("(o b) g -> o (b g)", o=1)).then_inc(loaded, 16)
                sp.wait_ge(loaded, 9 * 16)

            @block.vector
            def _(v):
                dv = c["dve"]
                dv(V.memset(arena[:, 6144:11000], 0.0))
                dv(V.memset(arena[:, 11000 + NCONST - NKEPT:AR], 0.0))
                dv(V.memset(tab[NB:NB + 1, :], MASKED))
                dv(V.memset(small, 0.0))
                dv(V.memset(eps, EPS))
                dv(V.memset(eps_ln, LNX_EPS))
                dv(V.memset(vfirst, 0.0))
                dv(V.memset(ring[1], 0.0))
                dv(V.memset(y_raw, 0.0))
        c["loaded"].skip(9 * 16)
        with nc.Block() as block:
            @block.scalar
            def _(s):
                c["act"](S.activation(arena[0:9, 6144:7168], arena[0:9, 5120:6144], ACT.Sigmoid))
                S.sem_inc(act_for_dve, 1)

            @block.tensor
            def _(pe):
                for k in range(KD):
                    if k >= 4:
                        pe.wait_ge(dve_for_pe, c["pe_from_dve"].next())
                    for m in range(MT):
                        tr(pb[k % 4][:, m * P:(m + 1) * P], arena[:, m * D + k * P:m * D + (k + 1) * P])
                    tr(pb[4 + k % 4][:, 0:DEC], arena[0:DEC, 4096 + k * P:4096 + (k + 1) * P]).then_inc(pe_for_dve, 1)
                pe.wait_ge(dve_for_pe, c["pe_from_dve"].next(5))
                for k in range(KD):
                    t = tr(pb[0][:, k * 9:k * 9 + 9], arena[0:9, 6144 + k * P:6144 + (k + 1) * P])
                t.then_inc(pe_for_dve, 1)
                pe.wait_ge(dve_for_pe, c["pe_from_dve"].next())
                for h in range(HB):
                    mm(pb[h], tab[0:NB + 1, h:h + 1].broadcast_to([NB + 1, P]), toe[0:NB + 1, 0:512])
                    mm(pb[4 + h][:, 0:128], tab[0:NB + 1, h:h + 1].broadcast_to([NB + 1, P]),
                       toe[0:NB + 1, 512:640])
                for g in range(NPG):
                    t = mm(pb[4][:, 256 + g * HB:256 + (g + 1) * HB], past[0:NB, g * P:(g + 1) * P], tab[0:NB, :])
                t.then_inc(pe_for_dve, 1)

            @block.vector
            def _(v):
                dv = c["dve"]
                for k in range(KD):
                    v.wait_ge(pe_for_dve, c["dve_from_pe"].next())
                    V.tensor_copy(xT[:, k, 0:SEQ], pb[k % 4])
                    dv(V.tensor_copy(xT[:, k, SEQ:T], pb[4 + k % 4][:, 0:DEC]))
                    V.sem_inc(dve_for_pe, 1)
                v.wait_ge(act_for_dve, c["dve_from_act"].next())
                dv(V.tensor_tensor(arena[0:9, 6144:7168], arena[0:9, 6144:7168], arena[0:9, 5120:6144], mult))
                V.sem_inc(dve_for_pe, 1)
                v.wait_ge(pe_for_dve, c["dve_from_pe"].next())
                dv(V.tensor_copy(csT.rearrange("p k s -> p (k s)"), pb[0][:, 0:72]))
                V.sem_inc(dve_for_pe, 1)
                v.wait_ge(pe_for_dve, c["dve_from_pe"].next())
                for h in range(HB):
                    V.tensor_copy(at(arena, 8192, HB, TOE)[:, h, 0:512], pb[h])
                    V.tensor_copy(at(arena, 8192, HB, TOE)[:, h, 512:640], pb[4 + h][:, 0:128])
                dv(V.tensor_copy(biasD.rearrange("p g h -> p (g h)"), pb[4][:, 256:256 + NPG * HB]))
                V.sem_inc(dve_for_sp, 1)

            @block.sync
            def _(sp):
                sp.wait_ge(dve_for_sp, c["sp_from_dve"].next())
                sp.dma_start(skew.rearrange("h p u -> p h u"), at(arena, 8192, HB, TOE)).then_inc(loaded, 16)
                sp.wait_ge(loaded, c["loaded"].next(16))
        clear()

        with nc.Fori(0, DEPTH) as l:
            c = counts()

            def L(name):
                ap = a[name][bass.ds(l, 1)]
                dims = "abcdef"[:len(ap.shape) - 1]
                return ap.rearrange("o " + " ".join(dims) + " -> (o " + dims[0] + ") " + " ".join(dims[1:]))

            def Lo(ap):
                ap = ap[bass.ds(l, 1)]
                dims = "abcdef"[:len(ap.shape) - 1]
                return ap.rearrange("o " + " ".join(dims) + " -> (o " + dims[0] + ") " + " ".join(dims[1:]))

            def load_w(sp, slot, src, k=8):
                sp.wait_ge(slot_free[slot], c["sp_free"][slot].next())
                n = src.shape[1]
                sp.dma_start(at(ring[slot], 0, k, 4096 // k)[:, :, 0:n],
                             src.rearrange("(k p) n -> p k n", p=P)).then_inc(slot_full[slot], 16)

            def wslot(slot, k=8):
                return at(ring[slot], 0, k, 4096 // k)

            def fm_tiles(pe, w, k0, src, n_tiles, cnt_free, done, nk=8, first=True, last=True, wk=0):
                for ct in range(n_tiles):
                    if first:
                        pe.wait_ge(cnt_free.sem, cnt_free.next())
                    mc = min(P, w.shape[2] - ct * P)
                    for k in range(nk):
                        mm(pb[ct][0:mc, :], w[:, wk + k, ct * P:ct * P + mc], src[:, k0 + k, 0:SEQ],
                           start=first and k == 0, stop=last and k == nk - 1)
                    for k in range(nk):
                        t = mm(pb[4 + ct][0:mc, 0:DEC], w[:, wk + k, ct * P:ct * P + mc], src[:, k0 + k, SEQ:T],
                               start=first and k == 0, stop=last and k == nk - 1)
                    if last:
                        t.then_inc(done, 1)
                return t

            with nc.Block() as block:
                @block.sync
                def _(sp):
                    n = 0
                    for name in PROW:
                        r0, nr = PROW[name]
                        if name == "v0":
                            src = a["v0"].rearrange("o (r c) -> (o r) c", c=P)
                        elif name == "mu":
                            mu = L("mu_shift")
                            sp.dma_start(arena[r0 + 14:r0 + 15, 0:32], mu[14 * P:RW].rearrange("(o c) -> o c", o=1)).then_inc(loaded, 16)
                            src = mu[0:14 * P].rearrange("(r c) -> r c", c=P)
                            n += 1
                        elif name == "r_k":
                            src = L("r_k").rearrange("(r h) d -> r (h d)", h=2)
                        else:
                            src = L(name).rearrange("(r c) -> r c", c=P)
                        sp.dma_start(arena[r0:r0 + src.shape[0], 0:P], src).then_inc(loaded, 16)
                        n += 1
                    for name, key in (("qn", "qk_norm_q"), ("kn", "qk_norm_k"), ("lq1", "lambda_q1"), ("lk1", "lambda_k1"),
                                      ("lq2", "lambda_q2"), ("lk2", "lambda_k2"), ("subln", "subln_diff"),
                                      ("lnx_g", "lnx_g"), ("lnx_b", "lnx_b")):
                        sp.dma_start(BR(name), L(key).partition_broadcast(P)).then_inc(loaded, 16)
                        n += 1
                    sp.wait_ge(loaded, 16 * n)
                    c["loaded"].skip(16 * n)

                @block.tensor
                def _(pe):
                    pe.sem_inc(slot_free[0], 1)
                    pe.sem_inc(slot_free[1], 1)
            with nc.Block() as block:
                @block.tensor
                def _(pe):
                    tr(pb[0][:, 0:NPAR], arena[0:NPAR, 0:P]).then_inc(pe_for_dve, 1)

                @block.vector
                def _(v):
                    dv = c["dve"]
                    v.wait_ge(pe_for_dve, c["dve_from_pe"].next())
                    dv(V.tensor_copy(par, pb[0][:, 0:NPAR]))
                    dv(V.tensor_tensor(small[:, 16:80], BR("lq1"), BR("lk1"), mult))
                    dv(V.tensor_tensor(small[:, 80:144], BR("lq2"), BR("lk2"), mult))
                    dv(V.tensor_reduce(small[:, 4:6], at(small, 16, 2, 64), AX.X, add))
                    V.sem_inc(dve_for_act, 1)
                    v.wait_ge(act_for_dve, c["dve_from_act"].next())
                    dv(V.tensor_tensor(lam, small[:, 6:7], small[:, 7:8], sub))
                    li = C("laminit", DEPTH, 2)
                    dv(V.tensor_tensor(lam, lam, li[:, bass.ds(l, 1), 0:1].rearrange("p a b -> p (a b)"), add))
                    dv(V.tensor_scalar(BR("subln"), BR("subln"), li[:, bass.ds(l, 1), 1:2].rearrange("p a b -> p (a b)"), None, mult))

                @block.scalar
                def _(s):
                    s.wait_ge(dve_for_act, c["act_from_dve"].next())
                    c["act"](S.activation(small[:, 6:8], small[:, 4:6], ACT.Exp))
                    S.sem_inc(act_for_dve, 1)

            with nc.Block() as block:
                @block.sync
                def _(sp):
                    wa = L("w_ada")
                    with sp.Fori(0, 6) as i:
                        for s in range(2):
                            c["sp_free"][s].enter(i, 1)
                            load_w(sp, s, wa[:, bass.ds(i * 1024 + s * 512, 512)])
                    for s in range(2):
                        c["sp_free"][s].leave(6)

                @block.tensor
                def _(pe):
                    with pe.Fori(0, 6) as i:
                        c["pe_from_dve"].enter(i, 2)
                        for s in range(2):
                            c["pe_full"][s].enter(i, 16)
                            pe.wait_ge(dve_for_pe, c["pe_from_dve"].next())
                            pe.wait_ge(slot_full[s], c["pe_full"][s].next(16))
                            w = wslot(s)
                            for ct in range(4):
                                for k in range(KD):
                                    t = mm(pb[s][:, ct * 9:ct * 9 + 9], w[:, k, ct * P:(ct + 1) * P], csT[:, k, :],
                                           start=(k == 0), stop=(k == KD - 1))
                            t.then_inc(pe_for_dve, 1)
                    for s in range(2):
                        c["pe_full"][s].leave(6)
                    c["pe_from_dve"].leave(6)
                    c["pe_from_dve"].skip(2)

                @block.vector
                def _(v):
                    V.sem_inc(dve_for_pe, 2)
                    with v.Fori(0, 6) as i:
                        c["dve_from_pe"].enter(i, 2)
                        c["dve"].enter(i, 2)
                        for s in range(2):
                            v.wait_ge(pe_for_dve, c["dve_from_pe"].next())
                            c["dve"](V.tensor_tensor(
                                modT[:, bass.ds(i * 8 + s * 4, 4), :], pb[s][:, 0:36].rearrange("p (c s) -> p c s", c=4),
                                bc(PR("b_ada")[:, bass.ds(i * 8 + s * 4, 4)], [P, 4, 9], 2), add))
                            V.sem_inc(dve_for_pe, 1)
                            V.sem_inc(slot_free[s], 1)
                    c["dve_from_pe"].leave(6)
                    c["dve"].leave(6)

            def norm_stage(gain, shift0, scale0):
                with nc.Block() as block:
                    @block.vector
                    def _(v):
                        dv = c["dve"]
                        sq = at(arena, 0, KD, T)
                        dv(V.tensor_tensor(sq, xT, xT, mult))
                        V.sem_inc(dve_for_pe, 1)
                        dv(V.tensor_scalar(coef, modT[:, scale0:scale0 + KD, :], 1.0, None, add))
                        dv(V.tensor_tensor(coef, coef, bc(PR(gain), [P, KD, 9], 2), mult))
                        v.wait_ge(act_for_dve, c["dve_from_act"].next())
                        dv(V.reciprocal(rstd, rstd))
                        dv(V.tensor_tensor(hT, xT, bc(rstd, [P, KD, T], 1), mult))
                        for k in range(KD):
                            V.tensor_scalar(hT[:, k, 0:SEQ], hT[:, k, 0:SEQ], coef[:, k, 0:1],
                                            modT[:, shift0 + k, 0:1], mult, add)
                        dv(V.tensor_tensor(hT[:, :, SEQ:T], hT[:, :, SEQ:T], coef[:, :, 1:9], mult))
                        dv(V.tensor_tensor(hT[:, :, SEQ:T], hT[:, :, SEQ:T], modT[:, shift0:shift0 + KD, 1:9], add))

                    @block.tensor
                    def _(pe):
                        sq = at(arena, 0, KD, T)
                        pe.wait_ge(dve_for_pe, c["pe_from_dve"].next())
                        for k in range(KD):
                            mm(pb[0], ones, sq[:, k, 0:SEQ], start=(k == 0), stop=(k == KD - 1))
                        for k in range(KD):
                            t = mm(pb[1][:, 0:DEC], ones, sq[:, k, SEQ:T], start=(k == 0), stop=(k == KD - 1))
                        t.then_inc(pe_for_act, 1)

                    @block.scalar
                    def _(s):
                        s.wait_ge(pe_for_act, c["act_from_pe"].next())
                        S.activation(rstd[:, 0:SEQ], pb[0], ACT.Sqrt, bias=eps, scale=1.0 / D)
                        c["act"](S.activation(rstd[:, SEQ:T], pb[1][:, 0:DEC], ACT.Sqrt, bias=eps, scale=1.0 / D))
                        S.sem_inc(act_for_dve, 1)

            norm_stage("norm1", 0, 8)

            w_in = L("w_in")

            def token_major(col0, n_blocks):
                with nc.Block() as block:
                    @block.sync
                    def _(sp):
                        for b in range(n_blocks):
                            load_w(sp, b % 2, w_in[:, col0 + 512 * b:col0 + 512 * (b + 1)])

                    @block.tensor
                    def _(pe):
                        for b in range(n_blocks):
                            pe.wait_ge(slot_full[b % 2], c["pe_full"][b % 2].next(16))
                            w = wslot(b % 2)
                            for m in range(5):
                                pe.wait_ge(act_for_pe, c["pe_from_act"].next())
                                r = P if m < MT else DEC
                                for k in range(KD):
                                    t = mm(pb[m][0:r, :], hT[:, k, m * P:m * P + r], w[:, k, :],
                                           start=(k == 0), stop=(k == KD - 1))
                                t.then_inc(pe_for_act, 1)
                        c["pe_from_act"].skip(5)

                    @block.scalar
                    def _(s):
                        S.sem_inc(act_for_pe, 5)
                        for b in range(n_blocks):
                            for m in range(5):
                                r = P if m < MT else DEC
                                s.wait_ge(pe_for_act, c["act_from_pe"].next())
                                c["act"](S.activation(arena[0:r, (b * 5 + m) * 512:(b * 5 + m + 1) * 512],
                                                      pb[m][0:r, :], ACT.Copy))
                                S.sem_inc(act_for_pe, 1)
                            S.sem_inc(slot_free[b % 2], 1)

            def heads_to_columns(block_fns, srcs, dst, heads=4, m_tiles=5):
                def pe_part(pe):
                    for n, src in enumerate(srcs):
                        pe.wait_ge(dve_for_pe, c["pe_from_dve"].next())
                        for h in range(heads):
                            for m in range(MT):
                                tr(pb[h][:, m * P:(m + 1) * P], src[:, m, h * P:(h + 1) * P])
                            t = tr(pb[4 + h][:, 0:DEC], src[0:DEC, MT, h * P:(h + 1) * P])
                        t.then_inc(pe_for_dve, 1)

                def dve_part(v):
                    for n, src in enumerate(srcs):
                        V.sem_inc(dve_for_pe, 1)
                        v.wait_ge(pe_for_dve, c["dve_from_pe"].next())
                        for h in range(heads):
                            V.tensor_copy(dst[:, 4 * n + h, 0:SEQ], pb[h])
                            c["dve"](V.tensor_copy(dst[:, 4 * n + h, SEQ:T], pb[4 + h][:, 0:DEC]))
                return pe_part, dve_part

            token_major(RET0, 4)
            Z = lambda b: at(arena, b * 2560, 5, 512)
            rot = [at(arena, 10240, 5, 512), at(arena, 12800, 5, 512)]
            qkT = at(arena, 0, 8, T)
            with nc.Block() as block:
                pe_part, dve_part = heads_to_columns(None, rot, qkT)
                vmask = at(ring[0], 0, DEC, 512)
                dstate = at(y_raw, 4 * T, 2, 4, HA, P)
                qc = at(arena, 10240, HA, SEQ)
                sc = at(arena, 15360, HA, P)
                st = at(arena, 15872, HA, P)
                od = at(arena, 16384, HA, DEC)
                oa = at(arena, 16640, 5, 512)

                @block.vector
                def _(v):
                    dv = c["dve"]
                    tmp = at(arena, 15360, 5, HA, 64)
                    for n, (cn, sn) in enumerate((("cosq", "sinq"), ("cosk", "sink"))):
                        x = at(arena, n * 2560, 20, 2, 64).rearrange("p (m h) t d -> p m h t d", m=5)
                        o = at(arena, 10240 + n * 2560, 20, 2, 64).rearrange("p (m h) t d -> p m h t d", m=5)
                        cs = bc(C(cn, 5, 64), [P, 5, HA, 64], 2)
                        sn_ = bc(C(sn, 5, 64), [P, 5, HA, 64], 2)
                        x1, x2, o1, o2 = x[:, :, :, 0, :], x[:, :, :, 1, :], o[:, :, :, 0, :], o[:, :, :, 1, :]
                        dv(V.tensor_tensor(o1, x1, cs, mult))
                        dv(V.tensor_tensor(tmp, x2, sn_, mult))
                        dv(V.tensor_tensor(o1, o1, tmp, sub))
                        dv(V.tensor_tensor(o2, x1, sn_, mult))
                        dv(V.tensor_tensor(tmp, x2, cs, mult))
                        dv(V.tensor_tensor(o2, o2, tmp, add))
                    dve_part(v)
                    kt = at(arena, 12800, MT, HA, P)
                    dv(V.tensor_tensor(kt, kt, bc(C("tail"), [P, MT, HA, P], 1, 3), mult))
                    q4 = at(arena, 0, HA, T)[:, :, 0:SEQ].rearrange("p h (n i) -> p h n i", n=MT)
                    dv(V.tensor_tensor(qc.rearrange("p h (n i) -> p h n i", n=MT), q4,
                                       bc(C("cross", HA, P), [P, HA, MT, P], 2), mult))
                    V.sem_inc(dve_for_pe, 1)
                    for n in range(MT):
                        v.wait_ge(pe_for_dve, c["dve_from_pe"].next())
                        dv(V.tensor_tensor(sc, at(pb[0], 0, HA, P), C("inner", HA, P), mult))
                        V.sem_inc(dve_for_pe, 1)
                        v.wait_ge(pe_for_dve, c["dve_from_pe"].next())
                        dv(V.tensor_copy(oa[:, n, :], pb[1]))
                        if n == 0:
                            dv(V.tensor_copy(st, at(pb[2], 0, HA, P)))
                        else:
                            dv(V.tensor_tensor(st, st, bc(C("chunk"), [P, HA, P], 2), mult))
                            dv(V.tensor_tensor(st, st, at(pb[2], 0, HA, P), add))
                        V.sem_inc(dve_for_pe, 1)
                    V.sem_inc(dve_for_sp, 1)
                    dv(V.tensor_tensor(vmask[0:DEC], bc(Z(2)[0:DEC, MT, :], [DEC, DEC, 512], 1),
                                       bc(ident[0:DEC, 0:DEC], [DEC, DEC, 512], 2), mult))
                    V.sem_inc(dve_for_pe, 1)
                    v.wait_ge(loaded, c["loaded"].base + 16 * DEC)
                    for hf in range(2):
                        v.wait_ge(pe_for_dve, c["dve_from_pe"].next())
                        for h in range(HA):
                            dv(V.scalar_tensor_tensor(dstate[:, hf, :, h, :], dstate[:, hf, :, h, :],
                                                      C("gamma")[:, h:h + 1], at(pb[4 * hf + h], 0, 4, P), mult, add))
                    V.sem_inc(dve_for_pe, 1)
                    V.sem_inc(dve_for_sp, 1)
                    v.wait_ge(pe_for_dve, c["dve_from_pe"].next())
                    dv(V.tensor_copy(od, at(pb[0], 0, HA, DEC)))
                    V.sem_inc(dve_for_pe, 1)
                    v.wait_ge(pe_for_dve, c["dve_from_pe"].next())
                    dv(V.tensor_copy(oa[0:DEC, MT, :], pb[1][0:DEC, :]))

                @block.tensor
                def _(pe):
                    pe_part(pe)
                    pe.wait_ge(dve_for_pe, c["pe_from_dve"].next())
                    for n in range(MT):
                        tok = slice(n * P, (n + 1) * P)
                        for h in range(HA):
                            t = mm(pb[0][:, h * P:(h + 1) * P], qkT[:, 4 + h, tok], qkT[:, h, tok])
                        t.then_inc(pe_for_dve, 1)
                        pe.wait_ge(dve_for_pe, c["pe_from_dve"].next())
                        for h in range(HA):
                            hs = slice(h * P, (h + 1) * P)
                            mm(pb[1][:, hs], sc[:, h, :], Z(2)[:, n, hs], stop=(n == 0))
                            if n:
                                mm(pb[1][:, hs], qc[:, h, tok], st[:, h, :], start=False)
                            t = mm(pb[2][:, hs], rot[1][:, n, hs], Z(2)[:, n, hs])
                        t.then_inc(pe_for_dve, 1)
                        pe.wait_ge(dve_for_pe, c["pe_from_dve"].next())
                    pe.wait_ge(dve_for_pe, c["pe_from_dve"].next())
                    for hf in range(2):
                        for h in range(HA):
                            hs = slice(h * P, (h + 1) * P)
                            t = mm(pb[4 * hf + h], rot[1][0:DEC, MT, hs], vmask[0:DEC, 4 * hf:4 * hf + 4, hs])
                        t.then_inc(pe_for_dve, 1)
                    pe.wait_ge(dve_for_pe, c["pe_from_dve"].next())
                    for b in range(DEC):
                        for h in range(HA):
                            t = mm(pb[0][:, h * DEC + b:h * DEC + b + 1], dstate[:, b // 4, b % 4, h, :],
                                   qkT[:, h, SEQ + b:SEQ + b + 1])
                    t.then_inc(pe_for_dve, 1)
                    pe.wait_ge(dve_for_pe, c["pe_from_dve"].next())
                    for h in range(HA):
                        t = tr(pb[1][0:DEC, h * P:(h + 1) * P], od[:, h, :])
                    t.then_inc(pe_for_dve, 1)

                @block.sync
                def _(sp):
                    sr = L("state_ret").rearrange("b h d e -> d b h e")
                    so = Lo(ret_s).rearrange("b h d e -> d b h e")
                    for b in range(DEC):
                        sp.dma_start(dstate[:, b // 4, b % 4], sr[:, b]).then_inc(loaded, 16)
                    sp.wait_ge(dve_for_sp, c["sp_from_dve"].next())
                    sp.dma_start(Lo(ret_p).rearrange("o h d e -> d (o h) e"), st).then_inc(stored, 16)
                    sp.wait_ge(dve_for_sp, c["sp_from_dve"].next())
                    for b in range(DEC):
                        sp.dma_start(so[:, b], dstate[:, b // 4, b % 4]).then_inc(stored, 16)
                    sp.wait_ge(stored, c["stored"].next(16 + 16 * DEC))
            c["loaded"].skip(16 * DEC)

            def head_rms(v, dv, o, sq, ms, groups, width):
                dv(V.tensor_tensor(sq, o, o, mult))
                dv(V.tensor_reduce(ms, sq.rearrange("p m (g d) -> p (m g) d", d=width), AX.X, add))
                V.sem_inc(dve_for_act, 1)
                v.wait_ge(act_for_dve, c["dve_from_act"].next())
                dv(V.reciprocal(ms, ms))
                og = o.rearrange("p m (g d) -> p (m g) d", d=width)
                dv(V.tensor_tensor(og, og, bc(ms, [P, groups, width], 2), mult))

            def act_root(s, ms, width):
                s.wait_ge(dve_for_act, c["act_from_dve"].next())
                c["act"](S.activation(ms, ms, ACT.Sqrt, bias=eps, scale=1.0 / width))
                S.sem_inc(act_for_dve, 1)

            with nc.Block() as block:
                oa = at(arena, 16640, 5, 512)
                sg = at(arena, 10240, 5, 512)
                sq = at(arena, 12800, 5, 512)
                ms = small[:, 160:180]
                pe_part, dve_part = heads_to_columns(None, [oa], yT)

                @block.scalar
                def _(s):
                    c["act"](S.activation(sg, Z(3), ACT.Sigmoid))
                    act_root(s, ms, DA)

                @block.vector
                def _(v):
                    dv = c["dve"]
                    head_rms(v, dv, oa, sq, ms, 20, DA)
                    dv(V.tensor_tensor(sg, sg, Z(3), mult))
                    dv(V.tensor_tensor(oa, oa, sg, mult))
                    dve_part(v)

                @block.tensor
                def _(pe):
                    pe_part(pe)

            token_major(DIFF0, 3)
            zq, zk, zv = Z(0), Z(1), Z(2)
            qkT2 = at(arena, 10240, 8, T)
            biasT = at(arena, 14912, HB, SEQ)
            with nc.Block() as block:
                sq = at(arena, 7680, 5, 512)
                ms = [small[:, 160:200], small[:, 200:240]]
                pe_part, dve_part = heads_to_columns(None, [zq, zk], qkT2)

                @block.vector
                def _(v):
                    dv = c["dve"]
                    dv(V.tensor_scalar(BR("qn"), BR("qn"), DB ** -0.5, None, mult))
                    for n, (z, g) in enumerate(((zq, "qn"), (zk, "kn"))):
                        head_rms(v, dv, z, sq, ms[n], 40, DB)
                        zg = z.rearrange("p m (g d) -> p (m g) d", d=DB)
                        dv(V.tensor_tensor(zg, zg, bc(BR(g), [P, 40, DB], 1), mult))
                    V.sem_inc(dve_for_sp, 1)
                    dve_part(v)

                @block.scalar
                def _(s):
                    for n in range(2):
                        act_root(s, ms[n], DB)

                @block.tensor
                def _(pe):
                    pe_part(pe)

                @block.sync
                def _(sp):
                    sp.dma_start(biasT, bass.AP(tensor=skew.tensor, offset=P - 1,
                                                ap=[[TOE - 1, P], [P * TOE, HB], [1, SEQ]])).then_inc(loaded, 16)
                    sp.wait_ge(loaded, c["loaded"].next(16))
                    sp.wait_ge(dve_for_sp, c["sp_from_dve"].next())
                    for z, op, os in ((zk, k_p, k_s), (zv, v_p, v_s)):
                        sp.dma_start(Lo(op).rearrange("o (m p) h d -> p (o m) (h d)", p=P), z[:, 0:MT, :]).then_inc(stored, 16)
                        sp.dma_start(Lo(os).rearrange("b o h d -> b (o h d)"), z[0:DEC, MT, :]).then_inc(stored, 16)
                    sp.wait_ge(stored, c["stored"].next(64))

            ob = at(arena, 0, 5, 512)
            with nc.Block() as block:
                s_ = at(arena, 7680, 2, SEQ)
                p_ = at(arena, 8704, 2, SEQ)
                aw = at(arena, 9728, SEQ)
                aT = at(arena, 14400, MT, P)
                st8 = small[:, 160:168]

                @block.vector
                def _(v):
                    dv = c["dve"]
                    for h in range(HB):
                        for qb in range(MT):
                            kw = (qb + 1) * P
                            v.wait_ge(pe_for_dve, c["dve_from_pe"].next())
                            for cc in range(2):
                                dv(V.tensor_tensor(s_[:, cc, 0:kw], pb[cc][:, 0:kw], biasT[:, h, SEQ - kw:SEQ], add))
                            dv(V.tensor_reduce(st8[:, 0:2], s_[:, :, 0:kw], AX.X, amax))
                            dv(V.tensor_scalar(st8[:, 2:4], st8[:, 0:2], -1.0, None, mult))
                            V.sem_inc(dve_for_act, 1)
                            v.wait_ge(act_for_dve, c["dve_from_act"].next())
                            dv(V.reciprocal(st8[:, 6:8], st8[:, 4:6]))
                            dv(V.tensor_tensor(st8[:, 7:8], st8[:, 7:8], lam, mult))
                            dv(V.tensor_scalar(p_[:, 1, 0:kw], p_[:, 1, 0:kw], st8[:, 7:8], None, mult))
                            dv(V.scalar_tensor_tensor(aw[:, 0:kw], p_[:, 0, 0:kw], st8[:, 6:7], p_[:, 1, 0:kw], mult, sub))
                            V.sem_inc(dve_for_pe, 1)
                            v.wait_ge(pe_for_dve, c["dve_from_pe"].next())
                            dv(V.tensor_copy(aT[:, 0:qb + 1, :], at(pb[2], 0, MT, P)[:, 0:qb + 1, :]))
                            V.sem_inc(dve_for_pe, 1)
                            v.wait_ge(pe_for_dve, c["dve_from_pe"].next())
                            dv(V.tensor_copy(ob[:, qb, h * P:(h + 1) * P], pb[3][:, 0:P]))

                @block.scalar
                def _(s):
                    for h in range(HB):
                        for qb in range(MT):
                            kw = (qb + 1) * P
                            s.wait_ge(dve_for_act, c["act_from_dve"].next())
                            for cc in range(2):
                                c["act"](S.activation(p_[:, cc, 0:kw], s_[:, cc, 0:kw], ACT.Exp,
                                                      bias=st8[:, 2 + cc:3 + cc], accum_out=st8[:, 4 + cc:5 + cc]))
                            S.sem_inc(act_for_dve, 1)

                @block.tensor
                def _(pe):
                    for h in range(HB):
                        for qb in range(MT):
                            kw = (qb + 1) * P
                            for cc in range(2):
                                r = slice(cc * DB, (cc + 1) * DB)
                                t = mm(pb[cc][:, 0:kw], qkT2[r, h, qb * P:(qb + 1) * P], qkT2[r, 4 + h, 0:kw])
                            t.then_inc(pe_for_dve, 1)
                            pe.wait_ge(dve_for_pe, c["pe_from_dve"].next())
                            for kb in range(qb + 1):
                                t = tr(pb[2][:, kb * P:(kb + 1) * P], aw[:, kb * P:(kb + 1) * P])
                            t.then_inc(pe_for_dve, 1)
                            pe.wait_ge(dve_for_pe, c["pe_from_dve"].next())
                            for kb in range(qb + 1):
                                t = mm(pb[3][:, 0:P], aT[:, kb, :], zv[:, kb, h * P:(h + 1) * P],
                                       start=(kb == 0), stop=(kb == qb))
                            t.then_inc(pe_for_dve, 1)

            with nc.Block() as block:
                pg = [at(arena, 16384, NPG, 512), at(arena, 17408, NPG, 512)]
                prod = at(arena, 18432, NPG, 512)
                scr = at(arena, 19456, NPG, DEC, 8)
                sown = at(arena, 19584, DEC, 8)
                srow = at(arena, 19648, PAST + 1)
                comb = at(arena, 19920, HB * DEC)
                comb2 = at(arena, 19952, HB * DEC)
                ap_ = at(arena, 19984, NPG, HB * DEC)
                aown = at(arena, 20048, HB * DEC)
                odT = at(arena, 20080, HB * DEC)
                zqd = at(arena, 20112, 512)
                st4 = small[:, 160:164]
                own = arena[0:DEC, 20624:20632]

                @block.sync
                def _(sp):
                    n = 0
                    for src in (a["cache_k_diff"], a["cache_v_diff"]):
                        for b in range(DEC):
                            if n >= 2:
                                sp.wait_ge(page_free, c["sp_page"].next())
                            for g in range(NPG):
                                pid = sp.value_load(pages[0:1, b * NPG + g:b * NPG + g + 1], min_val=0,
                                                    max_val=a["cache_k_diff"].shape[1] - 1)
                                sp.dma_start(pg[b % 2][:, g, :], src[bass.ds(l, 1), bass.ds(pid, 1)]
                                             .rearrange("o g p h d -> p (o g h d)")).then_inc(page_full, 16)
                            sp.wait_ge(page_full, 32 * (n + 1))
                            n += 1
                    c["sp_page"].skip(2)

                @block.vector
                def _(v):
                    dv = c["dve"]
                    dv(V.tensor_copy(zqd[0:DEC, :], zq[0:DEC, MT, :]))
                    V.sem_inc(dve_for_pe, 1)
                    for b in range(DEC):
                        v.wait_ge(pe_for_dve, c["dve_from_pe"].next())
                        v.wait_ge(page_full, c["dve_page"].next(32))
                        dv(V.tensor_tensor(prod, pg[b % 2], bc(pb[b % 2], [P, NPG, 512], 1), mult))
                        dv(V.tensor_reduce(scr[:, :, b, :], prod.rearrange("p g (x d) -> p g x d", d=DB), AX.X, add))
                        V.sem_inc(page_free, 1)
                        V.sem_inc(dve_for_pe, 1)
                    for g in range(NPG):
                        sg_ = scr[:, g].rearrange("p b (h c) -> p b h c", c=2)
                        dv(V.tensor_tensor(sg_, sg_, bc(biasD[:, g, :], [P, DEC, HB, 2], 1, 3), add))
                    dv(V.tensor_tensor(prod[0:DEC, 0, :], zqd[0:DEC, :], zk[0:DEC, MT, :], mult))
                    dv(V.tensor_reduce(own, prod[0:DEC, 0, :].rearrange("p (x d) -> p x d", d=DB), AX.X, add))
                    ow = own.rearrange("p (h c) -> p h c", c=2)
                    dv(V.tensor_tensor(ow, ow, bc(bias0[0:DEC], [DEC, HB, 2], 2), add))
                    dv(V.tensor_tensor(sown[0:DEC], bc(own, [DEC, DEC, 8], 1), bc(ident[0:DEC, 0:DEC], [DEC, DEC, 8], 2), mult))
                    V.sem_inc(dve_for_pe, 1)
                    v.wait_ge(pe_for_dve, c["dve_from_pe"].next())
                    dv(V.tensor_copy(srow[0:64], pb[0][0:64, 0:PAST + 1]))
                    dv(V.tensor_reduce(st4[0:64, 0:1], srow[0:64], AX.X, amax))
                    dv(V.tensor_scalar(st4[0:64, 1:2], st4[0:64, 0:1], -1.0, None, mult))
                    V.sem_inc(dve_for_act, 1)
                    v.wait_ge(act_for_dve, c["dve_from_act"].next())
                    dv(V.reciprocal(st4[0:64, 3:4], st4[0:64, 2:3]))
                    dv(V.tensor_scalar(srow[0:64], srow[0:64], st4[0:64, 3:4], None, mult))
                    dv(V.tensor_scalar(comb[0:64], C("c1")[0:64], lam[0:64], None, mult))
                    dv(V.tensor_tensor(comb[0:64], C("c0")[0:64], comb[0:64], sub))
                    dv(V.tensor_scalar(comb2[0:64], comb[0:64], srow[0:64, PAST:PAST + 1], None, mult))
                    V.sem_inc(dve_for_pe, 1)
                    v.wait_ge(pe_for_dve, c["dve_from_pe"].next())
                    dv(V.tensor_copy(ap_.rearrange("p g c -> p (g c)"), pb[1][:, 0:64]))
                    dv(V.tensor_copy(aown[0:DEC], pb[1][0:DEC, 64:96]))
                    V.sem_inc(dve_for_pe, 1)
                    for b in range(DEC):
                        v.wait_ge(pe_for_dve, c["dve_from_pe"].next())
                        V.sem_inc(page_free, 1)
                    dv(V.tensor_copy(odT, pb[2][:, 0:32]))
                    V.sem_inc(dve_for_pe, 1)
                    v.wait_ge(pe_for_dve, c["dve_from_pe"].next())
                    dv(V.tensor_copy(ob[0:DEC, MT, :], pb[3][0:DEC, :]))

                @block.scalar
                def _(s):
                    s.wait_ge(dve_for_act, c["act_from_dve"].next())
                    c["act"](S.activation(srow[0:64], srow[0:64], ACT.Exp, bias=st4[0:64, 1:2],
                                          accum_out=st4[0:64, 2:3]))
                    S.sem_inc(act_for_dve, 1)

                @block.tensor
                def _(pe):
                    pe.wait_ge(dve_for_pe, c["pe_from_dve"].next())
                    for b in range(DEC):
                        if b >= 2:
                            pe.wait_ge(dve_for_pe, c["pe_from_dve"].next())
                        mm(pb[b % 2], ident[0:DEC, b:b + 1].broadcast_to([DEC, P]), zqd[0:DEC, :]).then_inc(pe_for_dve, 1)
                    pe.wait_ge(dve_for_pe, c["pe_from_dve"].next(3))
                    for g in range(NPG):
                        tr(pb[0][0:64, g * P:(g + 1) * P], scr[:, g].rearrange("p b x -> p (b x)"))
                    mm(pb[0][0:64, PAST:PAST + 1], sown[0:DEC].rearrange("p b x -> p (b x)"),
                       ones[0:DEC, 0:1]).then_inc(pe_for_dve, 1)
                    pe.wait_ge(dve_for_pe, c["pe_from_dve"].next())
                    for g in range(NPG):
                        mm(pb[1][:, g * 32:(g + 1) * 32], srow[0:64, g * P:(g + 1) * P], comb[0:64])
                    mm(pb[1][0:DEC, 64:96], C("selb")[0:64], comb2[0:64]).then_inc(pe_for_dve, 1)
                    pe.wait_ge(dve_for_pe, c["pe_from_dve"].next())
                    for h in range(HB):
                        mm(pb[2][:, h * DEC:(h + 1) * DEC], zv[0:DEC, MT, h * P:(h + 1) * P],
                           aown[0:DEC, h * DEC:(h + 1) * DEC], start=(h == 0), stop=False)
                    c["pe_page"].skip(32 * DEC)
                    for b in range(DEC):
                        pe.wait_ge(page_full, c["pe_page"].next(32))
                        for h in range(HB):
                            for g in range(NPG):
                                t = mm(pb[2][:, h * DEC + b:h * DEC + b + 1], pg[b % 2][:, g, h * P:(h + 1) * P],
                                       ap_[:, g, h * DEC + b:h * DEC + b + 1], start=False, stop=(b == DEC - 1))
                        t.then_inc(pe_for_dve, 1)
                    pe.wait_ge(dve_for_pe, c["pe_from_dve"].next())
                    for h in range(HB):
                        t = tr(pb[3][0:DEC, h * P:(h + 1) * P], odT[:, h * DEC:(h + 1) * DEC])
                    t.then_inc(pe_for_dve, 1)
            c["dve_page"].skip(32 * DEC)

            with nc.Block() as block:
                sq = at(arena, 7680, 5, 512)
                ms = small[:, 160:180]
                pe_part, dve_part = heads_to_columns(None, [ob], yT[:, 4:8, :])

                @block.scalar
                def _(s):
                    act_root(s, ms, DVB)

                @block.vector
                def _(v):
                    dv = c["dve"]
                    head_rms(v, dv, ob, sq, ms, 20, DVB)
                    og = ob.rearrange("p m (g d) -> p (m g) d", d=DVB)
                    dv(V.tensor_tensor(og, og, bc(BR("subln"), [P, 20, DVB], 1), mult))
                    dve_part(v)

                @block.tensor
                def _(pe):
                    pe_part(pe)

            z = at(arena, 0, RT, T)
            zs = at(arena, 7800, RT, T)
            slab = [at(arena, n * 2080, HP, T) for n in range(3)]
            z0, z1, z2 = slab
            y3 = yT[:, 8:12, :]
            r_, k_, v_ = zs[:, 0:4, :], zs[:, 4:8, :], zs[:, 8:12, :]
            wdad, gd = zs[:, 12, :], zs[:, 13:15, :]
            w_up2 = ring[1][:, 0:512]
            w_g1, w_g2 = ring[1][:, 512:1024], ring[1][0:32, 1024:1536]
            w_vu = ring[1][0:32, 1536:2048]
            w_vd = at(ring[1], 2048, HP, 32)
            with nc.Block() as block:
                @block.sync
                def _(sp):
                    for b in range(4):
                        c0 = RW0 + 512 * b
                        load_w(sp, b % 2, w_in[:, c0:min(c0 + 512, GATE0)])

                @block.tensor
                def _(pe):
                    for b in range(4):
                        pe.wait_ge(slot_full[b % 2], c["pe_full"][b % 2].next(16))
                        n = 4 if b < 3 else 3
                        w = wslot(b % 2) if b < 3 else wslot(1)[:, :, 0:RW - 3 * W]
                        fm_tiles(pe, w, 0, hT, n, c["pe_from_act"], pe_for_act)
                    c["pe_from_act"].skip(4)

                @block.scalar
                def _(s):
                    S.sem_inc(act_for_pe, 4)
                    for b in range(4):
                        for ct in range(4 if b < 3 else 3):
                            mc = 32 if b == 3 and ct == 2 else P
                            s.wait_ge(pe_for_act, c["act_from_pe"].next())
                            S.activation(z[0:mc, 4 * b + ct, 0:SEQ], pb[ct][0:mc, :], ACT.Copy)
                            c["act"](S.activation(z[0:mc, 4 * b + ct, SEQ:T], pb[4 + ct][0:mc, 0:DEC], ACT.Copy))
                            S.sem_inc(act_for_pe, 1)
                        S.sem_inc(slot_free[b % 2], 1)

            with nc.Block() as block:
                prev_rows = arena[0:DEC, 15600:15600 + RT * P]
                prevT = at(arena, 17520, RT, DEC)
                last_rows = arena[0:9, 17664:17664 + RT * P]

                @block.sync
                def _(sp):
                    sp.dma_start(prev_rows[:, 0:RW], L("state_shift").rearrange("b o c -> b (o c)")).then_inc(loaded, 16)
                    sp.dma_start(w_up2[0:64, :], L("w_decay_up")).then_inc(loaded, 16)
                    sp.dma_start(w_up2[64:128, :], L("w_a_up")).then_inc(loaded, 16)
                    wg = L("w_g_up")
                    sp.dma_start(w_g1, wg[0:P, :]).then_inc(loaded, 16)
                    sp.dma_start(w_g2, wg[P:160, :]).then_inc(loaded, 16)
                    sp.dma_start(w_vu, a["w_v_up"][0]).then_inc(loaded, 16)
                    sp.dma_start(w_vd, a["w_v_down"][0].rearrange("(k p) n -> p k n", p=P)).then_inc(loaded, 16)
                    sp.wait_ge(loaded, c["loaded"].base + 112)
                    sp.wait_ge(dve_for_sp, c["sp_from_dve"].next())
                    sp.dma_start(Lo(shift_p).rearrange("b o c -> b (o c)"), last_rows[0:1, 0:RW]).then_inc(stored, 16)
                    sp.dma_start(Lo(shift_s).rearrange("b o c -> b (o c)"), last_rows[1:9, 0:RW]).then_inc(stored, 16)
                    sp.wait_ge(stored, c["stored"].next(32))

                @block.tensor
                def _(pe):
                    pe.wait_ge(loaded, c["loaded"].base + 112)
                    for t in range(RT):
                        mc = P if t < 14 else 32
                        tr(pb[0][0:mc, t * DEC:(t + 1) * DEC], prev_rows[:, t * P:t * P + mc])
                    for t in range(RT):
                        mc = P if t < 14 else 32
                        i = tr(pb[1 + t // 4][0:9, (t % 4) * P:(t % 4) * P + mc], z[0:mc, t, SEQ - 1:T])
                    i.then_inc(pe_for_dve, 1)

                @block.vector
                def _(v):
                    dv = c["dve"]
                    v.wait_ge(pe_for_dve, c["dve_from_pe"].next())
                    for g in range(4):
                        w_ = 512 if g < 3 else RW - 1536
                        dv(V.tensor_copy(last_rows[:, g * 512:g * 512 + w_], pb[1 + g][0:9, 0:w_]))
                    V.sem_inc(dve_for_sp, 1)
                    dv(V.tensor_copy(prevT[:, 0:14], at(pb[0], 0, 14, DEC)))
                    dv(V.tensor_copy(prevT[0:32, 14], pb[0][0:32, 14 * DEC:15 * DEC]))
                    for lo, hi, mc in ((0, 14, P), (14, 15, 32)):
                        dv(V.tensor_tensor(zs[0:mc, lo:hi, 1:SEQ], z[0:mc, lo:hi, 0:SEQ - 1], z[0:mc, lo:hi, 1:SEQ], sub))
                        dv(V.tensor_scalar(zs[0:mc, lo:hi, 0:1], z[0:mc, lo:hi, 0:1], -1.0, None, mult))
                        dv(V.tensor_tensor(zs[0:mc, lo:hi, SEQ:T], prevT[0:mc, lo:hi], z[0:mc, lo:hi, SEQ:T], sub))
                    for t in range(RT):
                        mc = P if t < 14 else 32
                        dv(V.scalar_tensor_tensor(zs[0:mc, t, :], zs[0:mc, t, :], PR("mu")[0:mc, t:t + 1], z[0:mc, t, :], mult, add))
            c["loaded"].skip(112)

            dvec = at(arena, 6760, 5, HP, DEC)
            tokv = at(arena, 18160, 5, 512)
            bonus = at(small, 200, 5, HC)
            dend = at(small, 256, HP, 8)
            yd = at(small, 288, HP, DEC)
            vdn = at(arena, 6240, T)
            with nc.Block() as block:
                def up(pe, lhs, rows_, rhs):
                    for ct in range(HP):
                        mm(pb[ct], lhs[rows_, ct * P:(ct + 1) * P], rhs[rows_, 0:SEQ])
                        t = mm(pb[4 + ct][:, 0:DEC], lhs[rows_, ct * P:(ct + 1) * P], rhs[rows_, SEQ:T])
                    return t

                @block.tensor
                def _(pe):
                    pe.wait_ge(act_for_pe, c["pe_from_act"].next())
                    up(pe, w_up2, slice(0, 64), wdad).then_inc(pe_for_act, 1)
                    pe.wait_ge(act_for_pe, c["pe_from_act"].next())
                    up(pe, w_up2, slice(64, 128), wdad).then_inc(pe_for_act, 1)
                    pe.wait_ge(act_for_pe, c["pe_from_act"].next())
                    for k in range(HP):
                        mm(pb[0][0:32, :], w_vd[:, k, :], v_[:, k, 0:SEQ], start=(k == 0), stop=(k == HP - 1))
                    for k in range(HP):
                        t = mm(pb[1][0:32, 0:DEC], w_vd[:, k, :], v_[:, k, SEQ:T], start=(k == 0), stop=(k == HP - 1))
                    t.then_inc(pe_for_act, 1)
                    pe.wait_ge(act_for_pe, c["pe_from_act"].next())
                    up(pe, w_vu, slice(0, 32), vdn).then_inc(pe_for_act, 1)
                    pe.wait_ge(dve_for_pe, c["pe_from_dve"].next())
                    for ct in range(HP):
                        mm(pb[ct], blk, y3[:, ct, 0:SEQ])
                        t = mm(pb[4 + ct][:, 0:DEC], blk, y3[:, ct, SEQ:T])
                    t.then_inc(pe_for_act, 1)
                    pe.wait_ge(dve_for_pe, c["pe_from_dve"].next())
                    for m in range(5):
                        r = P if m < MT else DEC
                        for hp in range(HP):
                            t = mm(pb[5][0:r, m * 8 + hp * 2:m * 8 + hp * 2 + 2], y3[:, hp, m * P:m * P + r], C("pair"))
                    t.then_inc(pe_for_dve, 1)
                    pe.wait_ge(dve_for_pe, c["pe_from_dve"].next())
                    for n in range(5):
                        for hp in range(HP):
                            t = tr(pb[n][0:DEC, hp * P:(hp + 1) * P], dvec[:, n, hp, :])
                    t.then_inc(pe_for_dve, 1)

                @block.scalar
                def _(s):
                    ac = c["act"]
                    ac(S.activation(wdad[0:64], wdad[0:64], ACT.Tanh))
                    S.sem_inc(act_for_pe, 1)
                    ac(S.activation(gd[:, 0], gd[:, 0], ACT.Sigmoid))
                    ac(S.activation(gd[0:32, 1], gd[0:32, 1], ACT.Sigmoid))

                    def bias_sigmoid(dst, name):
                        s.wait_ge(pe_for_act, c["act_from_pe"].next())
                        for ct in range(HP):
                            b_ = PR(name)[:, ct:ct + 1]
                            S.activation(dst[:, ct, 0:SEQ], pb[ct], ACT.Sigmoid, bias=b_)
                            ac(S.activation(dst[:, ct, SEQ:T], pb[4 + ct][:, 0:DEC], ACT.Sigmoid, bias=b_))

                    bias_sigmoid(z0, "w0")
                    S.sem_inc(act_for_pe, 1)
                    bias_sigmoid(z1, "a0")
                    S.sem_inc(act_for_pe, 1)
                    s.wait_ge(pe_for_act, c["act_from_pe"].next())
                    ac(S.activation(vdn[0:32, 0:SEQ], pb[0][0:32, :], ACT.Copy))
                    ac(S.activation(vdn[0:32, SEQ:T], pb[1][0:32, 0:DEC], ACT.Copy))
                    S.sem_inc(act_for_pe, 1)
                    bias_sigmoid(z2, "v0")
                    S.sem_inc(act_for_dve, 1)
                    s.wait_ge(pe_for_act, c["act_from_pe"].next())
                    for ct in range(HP):
                        S.activation(y3[:, ct, 0:SEQ], pb[ct], ACT.Sqrt)
                        ac(S.activation(y3[:, ct, SEQ:T], pb[4 + ct][:, 0:DEC], ACT.Sqrt))
                    S.sem_inc(act_for_dve, 1)
                    s.wait_ge(dve_for_act, c["act_from_dve"].next())
                    ac(S.activation(dvec[:, 0], z0[:, :, SEQ:T], ACT.Exp))
                    S.sem_inc(act_for_dve, 1)
                    s.wait_ge(dve_for_act, c["act_from_dve"].next())
                    ac(S.activation(z0, z0, ACT.Exp))
                    S.sem_inc(act_for_dve, 1)
                    s.wait_ge(dve_for_act, c["act_from_dve"].next())
                    ac(S.activation(z0, y3, ACT.Exp, scale=-1.0))
                    ac(S.activation(y3, y3, ACT.Exp))
                    S.sem_inc(act_for_dve, 1)

                @block.vector
                def _(v):
                    dv = c["dve"]
                    vm = C("vmix", DEPTH)[:, bass.ds(l, 1)]
                    v.wait_ge(act_for_dve, c["dve_from_act"].next())
                    dv(V.tensor_scalar(z0, z0, -math.exp(-0.5), None, mult))
                    dv(V.tensor_scalar(z2, z2, vm, None, mult))
                    dv(V.tensor_tensor(y3, vfirst, v_, sub))
                    dv(V.scalar_tensor_tensor(vfirst, y3, vm, v_, mult, add))
                    dv(V.tensor_tensor(y3, y3, z2, mult))
                    dv(V.tensor_tensor(v_, v_, y3, add))
                    for ct in range(HP):
                        dv(V.tensor_scalar(z2[:, ct], k_[:, ct], PR("k_k")[:, ct:ct + 1], None, mult))
                    dv(V.tensor_tensor(y3, z2, z2, mult))
                    V.sem_inc(dve_for_pe, 1)
                    v.wait_ge(act_for_dve, c["dve_from_act"].next())
                    dv(V.tensor_scalar(y3, y3, 1e-12, None, amax))
                    dv(V.reciprocal(y3, y3))
                    dv(V.tensor_tensor(z2, z2, y3, mult))
                    for ct in range(HP):
                        ka = PR("k_a")[:, ct:ct + 1]
                        dv(V.tensor_scalar(y3[:, ct], z1[:, ct], ka, ka, mult, sub))
                    dv(V.scalar_tensor_tensor(k_, y3, 1.0, k_, add, mult))
                    dv(V.tensor_tensor(z1, z1, z2, mult))
                    for ct in range(HP):
                        dv(V.scalar_tensor_tensor(y3[:, ct], r_[:, ct], PR("r_k")[:, ct:ct + 1], k_[:, ct], mult, mult))
                    V.sem_inc(dve_for_pe, 1)
                    v.wait_ge(pe_for_dve, c["dve_from_pe"].next())
                    dv(V.tensor_copy(bonus[:, 0:MT], at(pb[5], 0, MT, HC)))
                    dv(V.tensor_copy(bonus[0:DEC, MT], pb[5][0:DEC, MT * 8:MT * 8 + 8]))
                    V.sem_inc(dve_for_act, 1)
                    dv(V.tensor_copy(dvec[:, 1], k_[:, :, SEQ:T]))
                    dv(V.tensor_scalar(dvec[:, 2], z2[:, :, SEQ:T], -1.0, None, mult))
                    dv(V.tensor_copy(dvec[:, 3], z1[:, :, SEQ:T]))
                    dv(V.tensor_copy(dvec[:, 4], r_[:, :, SEQ:T]))
                    v.wait_ge(act_for_dve, c["dve_from_act"].next())
                    V.sem_inc(dve_for_pe, 1)
                    for ct in range(HP):
                        dv(V.tensor_tensor_scan(y3[:, ct], C("scan"), z0[:, ct], 0.0, mult, add))
                    dv(V.tensor_tensor(z0, y3, z0, sub))
                    V.sem_inc(dve_for_act, 1)
                    v.wait_ge(act_for_dve, c["dve_from_act"].next())
                    dv(V.scalar_tensor_tensor(z2, z2, -1.0, z0, mult, mult))
                    V.sem_inc(dve_for_act, 1)
                    v.wait_ge(act_for_dve, c["dve_from_act"].next())
                    dv(V.tensor_tensor(z1, z1, z0, mult))
                    dv(V.tensor_tensor(k_, k_, z0, mult))
                    dv(V.tensor_tensor(r_, r_, y3, mult))
                    dv(V.tensor_copy(dend, y3[:, :, CH - 1:SEQ:CH]))
                    v.wait_ge(pe_for_dve, c["dve_from_pe"].next())
                    for n in range(5):
                        dv(V.tensor_copy(tokv[0:DEC, n], pb[n][0:DEC, :]))

            ytok = at(arena, 18160, 5, 512)
            with nc.Block() as block:
                ds_ = at(arena, 15600, DEC, HP, DC)
                t1 = at(arena, 17648, 2, HP, DC)
                u = at(small, 320, 2, HP)

                @block.sync
                def _(sp):
                    sr = L("state_rwkv").rearrange("b (q g) i j -> g i b q j", g=2)
                    so = Lo(rwkv_s).rearrange("b (q g) i j -> g i b q j", g=2)
                    for g in range(2):
                        for b in range(DEC):
                            sp.dma_start(ds_[g * 64:(g + 1) * 64, b], sr[g, :, b]).then_inc(loaded, 16)
                    sp.wait_ge(dve_for_sp, c["sp_from_dve"].next())
                    for g in range(2):
                        for b in range(DEC):
                            sp.dma_start(so[g, :, b], ds_[g * 64:(g + 1) * 64, b]).then_inc(stored, 16)
                    sp.wait_ge(stored, c["stored"].next(256))

                @block.tensor
                def _(pe):
                    for q in range(4):
                        if q:
                            pe.wait_ge(dve_for_pe, c["pe_from_dve"].next())
                        for n in range(5):
                            x = tokv[0:DEC, n, :].rearrange("b (q g j) -> b g q j", g=2, j=DC)
                            for b2 in range(2):
                                for g in range(2):
                                    b = 2 * q + b2
                                    t = mm(pb[n][g * 64:(g + 1) * 64, b2 * 256:(b2 + 1) * 256],
                                           ident[0:DEC, b:b + 1].broadcast_to([DEC, 64]), x[:, g])
                        t.then_inc(pe_for_dve, 1)
                    pe.wait_ge(dve_for_pe, c["pe_from_dve"].next())
                    for hp in range(HP):
                        t = tr(pb[5][0:DEC, hp * P:(hp + 1) * P], yd[:, hp, :])
                    t.then_inc(pe_for_dve, 1)

                @block.vector
                def _(v):
                    dv = c["dve"]
                    v.wait_ge(loaded, c["loaded"].base + 256)
                    for q in range(4):
                        s2 = ds_[:, 2 * q:2 * q + 2]
                        sf, tf = s2.rearrange("p b q j -> p (b q) j"), t1.rearrange("p b q j -> p (b q) j")
                        w3, k3, a3, b3, r3 = (at(pb[n], 0, 8, DC) for n in range(5))
                        uf = u.rearrange("p b q -> p (b q)")
                        v.wait_ge(pe_for_dve, c["dve_from_pe"].next())
                        dv(V.tensor_tensor(tf, sf, a3, mult))
                        dv(V.tensor_reduce(uf, tf, AX.X, add))
                        dv(V.tensor_tensor(sf, sf, w3, mult))
                        dv(V.tensor_tensor(tf, b3, bc(uf, [P, 8, DC], 2), mult))
                        dv(V.tensor_tensor(sf, sf, tf, add))
                        vv = v_[:, :, SEQ + 2 * q:SEQ + 2 * q + 2].rearrange("p q b -> p b q")
                        dv(V.tensor_tensor(t1, at(pb[1], 0, 2, HP, DC), bc(vv, [P, 2, HP, DC], 3), mult))
                        dv(V.tensor_tensor(sf, sf, tf, add))
                        dv(V.tensor_tensor(tf, sf, r3, mult))
                        dv(V.tensor_reduce(yd[:, :, 2 * q:2 * q + 2].rearrange("p q b -> p b q"), t1, AX.X, add))
                        V.sem_inc(dve_for_pe, 1)
                    V.sem_inc(dve_for_sp, 1)
                    v.wait_ge(pe_for_dve, c["dve_from_pe"].next())
                    dv(V.tensor_copy(ytok[0:DEC, MT], pb[5][0:DEC, :]))
            c["loaded"].skip(256)

            vtok = at(arena, 15600, 5, 512)
            btok = at(arena, 0, MT, 512)
            ktok = at(arena, 11960, MT, 512)
            with nc.Block() as block:
                @block.tensor
                def _(pe):
                    for n, src in enumerate((v_, z1, k_)):
                        if n:
                            pe.wait_ge(dve_for_pe, c["pe_from_dve"].next())
                        for m in range(MT):
                            for hp in range(HP):
                                t = tr(pb[m][:, hp * P:(hp + 1) * P], src[:, hp, m * P:(m + 1) * P])
                        if n == 0:
                            for hp in range(HP):
                                t = tr(pb[4][0:DEC, hp * P:(hp + 1) * P], src[:, hp, SEQ:T])
                        t.then_inc(pe_for_dve, 1)

                @block.vector
                def _(v):
                    dv = c["dve"]
                    for n, dst in enumerate((vtok, btok, ktok)):
                        v.wait_ge(pe_for_dve, c["dve_from_pe"].next())
                        for m in range(MT):
                            dv(V.tensor_copy(dst[:, m], pb[m]))
                        if n == 0:
                            dv(V.tensor_copy(dst[0:DEC, MT], pb[4][0:DEC, :]))
                        V.sem_inc(dve_for_pe, 1)
            c["pe_from_dve"].skip(1)

            m_ba, m_br, m_ka, m_kr = (at(ring[0], n * 1024, 2, HP, P) for n in range(4))
            xt = at(arena, 6240, 2, HP, P)
            xm = at(y_raw, 8 * T, 2, HP, P)
            m1 = at(y_raw, 8 * T + 1024, 2, HP, P)
            lo_ = at(ring[1], 2176, 2, HP, P)
            rhs1 = ring[1][:, 3200:3712]
            uu = arena[:, 7264:7776]
            stb = at(arena, 14040, HP, P)
            with nc.Block() as block:
                @block.vector
                def _(v):
                    c["dve"](V.memset(stb, 0.0))
            keep = C("keep", 2, P)
            level = C("level", 6, P)
            with nc.Block() as block:
                @block.tensor
                def _(pe):
                    turn = c["pe_from_dve"]
                    for m in range(MT):
                        tok = slice(m * P, (m + 1) * P)
                        if m:
                            pe.wait_ge(dve_for_pe, turn.next())
                        for n, (left, right) in enumerate(((z1, z2), (z1, r_), (k_, z2), (k_, r_))):
                            for g in range(2):
                                gs = slice(g * 64, (g + 1) * 64)
                                for hp in range(HP):
                                    t = mm(pb[2 * n + g][:, hp * P:(hp + 1) * P], left[gs, hp, tok], right[gs, hp, tok])
                        t.then_inc(pe_for_dve, 1)
                        for lv in range(6):
                            for g in range(2):
                                pe.wait_ge(dve_for_pe, turn.next())
                                for hp in range(HP):
                                    t = mm(pb[g][:, hp * P:(hp + 1) * P], lo_[:, g, hp, :],
                                           ident if lv == 0 else xm[:, g, hp, :])
                                t.then_inc(pe_for_dve, 1)
                            if lv == 0:
                                continue
                            for g in range(2):
                                pe.wait_ge(dve_for_pe, turn.next())
                                for hp in range(HP):
                                    hs = slice(hp * P, (hp + 1) * P)
                                    if lv < 5:
                                        mm(pb[2 + g][:, hs], xt[:, g, hp, :], m1[:, g, hp, :])
                                    t = mm(pb[4 + g][:, hs], m1[:, g, hp, :], xt[:, g, hp, :])
                                t.then_inc(pe_for_dve, 1)
                        for cc in range(2):
                            r = slice(cc * 64, (cc + 1) * 64)
                            tk = slice(m * P + cc * 64, m * P + (cc + 1) * 64)
                            hsl = [slice(h * 64, (h + 1) * 64) for h in range(HC)]
                            pe.wait_ge(dve_for_pe, turn.next())
                            for hp in range(HP):
                                mm(pb[0][r, hp * P:(hp + 1) * P], z2[:, hp, tk], stb[:, hp, :], start=(hp == 0), stop=False)
                            for h in range(HC):
                                t = mm(pb[0][r, hsl[h]], m_ka[r, h % 2, h // 2, r], vtok[r, m, hsl[h]], start=False)
                            t.then_inc(pe_for_dve, 1)
                            pe.wait_ge(dve_for_pe, turn.next())
                            for h in range(HC):
                                t = mm(pb[1][r, hsl[h]], xt[r, h % 2, h // 2, r], rhs1[r, hsl[h]])
                            t.then_inc(pe_for_dve, 1)
                            pe.wait_ge(dve_for_pe, turn.next())
                            for hp in range(HP):
                                hs = slice(hp * P, (hp + 1) * P)
                                mm(pb[3][:, hs], btok[r, m, hs], uu[r, hs], stop=False)
                                mm(pb[3][:, hs], ktok[r, m, hs], vtok[r, m, hs], start=False)
                            for hp in range(HP):
                                mm(pb[2][r, hp * P:(hp + 1) * P], r_[:, hp, tk], stb[:, hp, :], start=(hp == 0), stop=False)
                            for h in range(HC):
                                mm(pb[2][r, hsl[h]], m_br[r, h % 2, h // 2, r], uu[r, hsl[h]], start=False, stop=False)
                                t = mm(pb[2][r, hsl[h]], m_kr[r, h % 2, h // 2, r], vtok[r, m, hsl[h]], start=False)
                            t.then_inc(pe_for_dve, 1)
                    pe.wait_ge(dve_for_pe, turn.next())
                    for hp in range(HP):
                        t = tr(pb[0][:, hp * P:(hp + 1) * P], stb[:, hp, :])
                    t.then_inc(pe_for_dve, 1)

                @block.vector
                def _(v):
                    dv = c["dve"]
                    done = c["dve_from_pe"]
                    for m in range(MT):
                        v.wait_ge(pe_for_dve, done.next())
                        for n, (dst, kp) in enumerate(((m_ba, 0), (m_br, 1), (m_ka, 0), (m_kr, 1))):
                            for g in range(2):
                                dv(V.tensor_tensor(dst[:, g], at(pb[2 * n + g], 0, HP, P), bc(keep[:, kp], [P, HP, P], 1), mult))
                        for lv in range(6):
                            for g in range(2):
                                dv(V.tensor_tensor(lo_[:, g], m_ba[:, g], bc(level[:, lv], [P, HP, P], 1), mult))
                                V.sem_inc(dve_for_pe, 1)
                            if lv == 0:
                                for g in range(2):
                                    dv(V.tensor_tensor(xt[:, g], lo_[:, g], bc(ident, [P, HP, P], 1), add))
                                    v.wait_ge(pe_for_dve, done.next())
                                    dv(V.tensor_tensor(xm[:, g], at(pb[g], 0, HP, P), bc(ident, [P, HP, P], 1), add))
                                continue
                            for g in range(2):
                                v.wait_ge(pe_for_dve, done.next())
                                dv(V.tensor_copy(m1[:, g], at(pb[g], 0, HP, P)))
                                V.sem_inc(dve_for_pe, 1)
                            for g in range(2):
                                v.wait_ge(pe_for_dve, done.next())
                                if lv < 5:
                                    dv(V.tensor_tensor(xm[:, g], xm[:, g], at(pb[2 + g], 0, HP, P), add))
                                dv(V.tensor_tensor(xt[:, g], xt[:, g], at(pb[4 + g], 0, HP, P), add))
                        for cc in range(2):
                            r = slice(cc * 64, (cc + 1) * 64)
                            V.sem_inc(dve_for_pe, 1)
                            v.wait_ge(pe_for_dve, done.next())
                            dv(V.tensor_copy(rhs1[r], pb[0][r]))
                            V.sem_inc(dve_for_pe, 1)
                            v.wait_ge(pe_for_dve, done.next())
                            dv(V.tensor_copy(uu[r], pb[1][r]))
                            V.sem_inc(dve_for_pe, 1)
                            v.wait_ge(pe_for_dve, done.next())
                            upd = at(m1.rearrange("p g q t -> p (g q t)"), 0, HP, P)
                            dv(V.tensor_tensor(upd, at(pb[3], 0, HP, P), bc(blk, [P, HP, P], 1), mult))
                            dv(V.tensor_tensor(stb, stb, upd, add))
                            dv(V.tensor_tensor(stb, stb, bc(dend[:, :, 2 * m + cc], [P, HP, P], 2), mult))
                            dv(V.tensor_copy(ytok[r, m], pb[2][r]))
                        V.sem_inc(dve_for_pe, 1)
                    v.wait_ge(pe_for_dve, done.next())
                    dv(V.tensor_copy(uu, pb[0]))
                    V.sem_inc(dve_for_sp, 1)

                @block.sync
                def _(sp):
                    sp.wait_ge(dve_for_sp, c["sp_from_dve"].next())
                    o = Lo(rwkv_p).rearrange("o (q g) i j -> g i (o q) j", g=2)
                    for g in range(2):
                        sp.dma_start(o[g], at(arena, 7264, HP, P)[g * 64:(g + 1) * 64, :, g * 64:(g + 1) * 64]).then_inc(stored, 16)
                    sp.wait_ge(stored, c["stored"].next(32))

            with nc.Block() as block:
                sq = at(arena, 0, 5, 512)
                ms = small[:, 160:200]
                mu_ = small[:, 330:370]
                pe_part, dve_part = heads_to_columns(None, [ytok], yT[:, 8:12, :])

                @block.scalar
                def _(s):
                    s.wait_ge(dve_for_act, c["act_from_dve"].next())
                    c["act"](S.activation(ms, ms, ACT.Sqrt, bias=eps_ln, scale=1.0 / DC))
                    S.sem_inc(act_for_dve, 1)

                @block.tensor
                def _(pe):
                    for m in range(5):
                        r = P if m < MT else DEC
                        mm(pb[m][0:r], gd[:, 0, m * P:m * P + r], w_g1, stop=False)
                        t = mm(pb[m][0:r], gd[0:32, 1, m * P:m * P + r], w_g2, start=False)
                    t.then_inc(pe_for_dve, 1)
                    pe_part(pe)

                @block.vector
                def _(v):
                    dv = c["dve"]
                    yg = ytok.rearrange("p m (g d) -> p (m g) d", d=DC)
                    vg = vtok.rearrange("p m (g d) -> p (m g) d", d=DC)
                    sg_ = sq.rearrange("p m (g d) -> p (m g) d", d=DC)
                    dv(V.tensor_reduce(mu_, yg, AX.X, add))
                    dv(V.tensor_scalar(mu_, mu_, 1.0 / DC, None, mult))
                    dv(V.tensor_tensor(yg, yg, bc(mu_, [P, 40, DC], 2), sub))
                    dv(V.tensor_tensor(sq, ytok, ytok, mult))
                    dv(V.tensor_reduce(ms, sg_, AX.X, add))
                    V.sem_inc(dve_for_act, 1)
                    v.wait_ge(act_for_dve, c["dve_from_act"].next())
                    dv(V.reciprocal(ms, ms))
                    dv(V.tensor_tensor(yg, yg, bc(ms, [P, 40, DC], 2), mult))
                    dv(V.tensor_tensor(ytok, ytok, bc(BR("lnx_g"), [P, 5, 512], 1), mult))
                    dv(V.tensor_tensor(ytok, ytok, bc(BR("lnx_b"), [P, 5, 512], 1), add))
                    dv(V.tensor_tensor(sg_, vg, bc(bonus.rearrange("p m h -> p (m h)"), [P, 40, DC], 2), mult))
                    dv(V.tensor_tensor(ytok, ytok, sq, add))
                    v.wait_ge(pe_for_dve, c["dve_from_pe"].next())
                    for m in range(5):
                        r = P if m < MT else DEC
                        dv(V.tensor_tensor(ytok[0:r, m], ytok[0:r, m], pb[m][0:r], mult))
                    dve_part(v)

            merged = at(arena, 0, KD, T)
            with nc.Block() as block:
                sgb = at(arena, 4160, 2, T)
                tmp = at(arena, 5200, 2, T)

                @block.sync
                def _(sp):
                    with sp.Fori(0, 2) as og:
                        for s in range(2):
                            c["sp_free"][s].enter(og, 3)
                        for n, name in enumerate(("w_up_a", "w_up_b", "w_up_c")):
                            load_w(sp, 0, w_in[:, bass.ds(og * 512 + (GATE0 + n * D), 512)])
                            load_w(sp, 1, L(name)[:, bass.ds(og * 512, 512)], k=4)
                    for s in range(2):
                        c["sp_free"][s].leave(2)

                @block.tensor
                def _(pe):
                    with pe.Fori(0, 2) as og:
                        c["pe_from_dve"].enter(og, 12)
                        for s in range(2):
                            c["pe_full"][s].enter(og, 48)
                        for n in range(3):
                            for s in range(2):
                                pe.wait_ge(slot_full[s], c["pe_full"][s].next(16))
                            for ct in range(4):
                                b = ct % 2
                                cs = slice(ct * P, (ct + 1) * P)
                                pe.wait_ge(dve_for_pe, c["pe_from_dve"].next())
                                wg, wu = wslot(0), wslot(1, 4)
                                for k in range(KD):
                                    mm(pb[b], wg[:, k, cs], hT[:, k, 0:SEQ], start=(k == 0), stop=(k == KD - 1))
                                for k in range(KD):
                                    mm(pb[4 + b][:, 0:DEC], wg[:, k, cs], hT[:, k, SEQ:T], start=(k == 0), stop=(k == KD - 1))
                                for k in range(4):
                                    mm(pb[2 + b], wu[:, k, cs], yT[:, 4 * n + k, 0:SEQ], start=(k == 0), stop=(k == 3))
                                for k in range(4):
                                    t = mm(pb[6 + b][:, 0:DEC], wu[:, k, cs], yT[:, 4 * n + k, SEQ:T], start=(k == 0), stop=(k == 3))
                                t.then_inc(pe_for_act, 1)
                    c["pe_from_dve"].leave(2)
                    c["pe_from_dve"].skip(2)
                    for s in range(2):
                        c["pe_full"][s].leave(2)

                @block.scalar
                def _(s):
                    with s.Fori(0, 2) as og:
                        c["act_from_pe"].enter(og, 12)
                        c["act"].enter(og, 24)
                        for n in range(3):
                            for ct in range(4):
                                b = ct % 2
                                s.wait_ge(pe_for_act, c["act_from_pe"].next())
                                c["act"](S.activation(sgb[:, b, 0:SEQ], pb[b], ACT.Sigmoid))
                                c["act"](S.activation(sgb[:, b, SEQ:T], pb[4 + b][:, 0:DEC], ACT.Sigmoid))
                                S.sem_inc(act_for_dve, 1)
                    c["act_from_pe"].leave(2)
                    c["act"].leave(2)

                @block.vector
                def _(v):
                    dv = c["dve"]
                    V.sem_inc(dve_for_pe, 2)
                    with v.Fori(0, 2) as og:
                        c["dve_from_act"].enter(og, 12)
                        dv.enter(og, 8 + 2 * 12)
                        for n in range(3):
                            for ct in range(4):
                                b = ct % 2
                                mg = merged[:, bass.ds(og * 4 + ct, 1), :].rearrange("p o t -> p (o t)")
                                dst = mg if n == 0 else tmp[:, b]
                                v.wait_ge(act_for_dve, c["dve_from_act"].next())
                                dv(V.tensor_tensor(dst[:, 0:SEQ], sgb[:, b, 0:SEQ], pb[2 + b], mult))
                                dv(V.tensor_tensor(dst[:, SEQ:T], sgb[:, b, SEQ:T], pb[6 + b][:, 0:DEC], mult))
                                V.sem_inc(dve_for_pe, 1)
                                if ct == 3:
                                    V.sem_inc(slot_free[0], 1)
                                    V.sem_inc(slot_free[1], 1)
                                if n:
                                    dv(V.tensor_tensor(mg, mg, tmp[:, b], add))
                        v.nop()
                    c["dve_from_act"].leave(2)
                    dv.leave(2)

            def residual(v, dv, kt, bank, gate0, tmp8):
                dv(V.scalar_tensor_tensor(xT[:, kt, 0:SEQ], pb[bank], modT[:, gate0 + kt, 0:1], xT[:, kt, 0:SEQ], mult, add))
                dv(V.tensor_tensor(tmp8, pb[4 + bank][:, 0:DEC], modT[:, gate0 + kt, 1:9], mult))
                V.sem_inc(dve_for_pe, 1)
                dv(V.tensor_tensor(xT[:, kt, SEQ:T], xT[:, kt, SEQ:T], tmp8, add))

            tmp8 = small[:, 400:408]
            with nc.Block() as block:
                @block.sync
                def _(sp):
                    for b in range(2):
                        load_w(sp, b, L("w_out")[:, b * 512:(b + 1) * 512])

                @block.tensor
                def _(pe):
                    for b in range(2):
                        pe.wait_ge(slot_full[b], c["pe_full"][b].next(16))
                        fm_tiles(pe, wslot(b), 0, merged, 4, c["pe_from_dve"], pe_for_dve)
                    c["pe_from_dve"].skip(4)

                @block.vector
                def _(v):
                    V.sem_inc(dve_for_pe, 4)
                    for b in range(2):
                        for ct in range(4):
                            v.wait_ge(pe_for_dve, c["dve_from_pe"].next())
                            residual(v, c["dve"], 4 * b + ct, ct, 16, tmp8)
                        V.sem_inc(slot_free[b], 1)

            norm_stage("norm2", 24, 32)

            ff = at(arena, 0, KF, T)
            with nc.Block() as block:
                @block.sync
                def _(sp):
                    w1 = L("w_ff1")
                    with sp.Fori(0, 4) as i:
                        for s in range(2):
                            c["sp_free"][s].enter(i, 1)
                            load_w(sp, s, w1[:, bass.ds(i * 1024 + s * 512, 512)])
                    for s in range(2):
                        c["sp_free"][s].leave(4)

                @block.tensor
                def _(pe):
                    with pe.Fori(0, 4) as i:
                        c["pe_from_dve"].enter(i, 8)
                        for s in range(2):
                            c["pe_full"][s].enter(i, 16)
                            pe.wait_ge(slot_full[s], c["pe_full"][s].next(16))
                            fm_tiles(pe, wslot(s), 0, hT, 4, c["pe_from_dve"], pe_for_act)
                    c["pe_from_dve"].leave(4)
                    c["pe_from_dve"].skip(4)
                    for s in range(2):
                        c["pe_full"][s].leave(4)

                @block.scalar
                def _(s):
                    with s.Fori(0, 4) as i:
                        c["act_from_pe"].enter(i, 8)
                        c["act"].enter(i, 16)
                        for sl in range(2):
                            for ct in range(4):
                                f = ff[:, bass.ds(i * 8 + sl * 4 + ct, 1), :].rearrange("p o t -> p (o t)")
                                s.wait_ge(pe_for_act, c["act_from_pe"].next())
                                c["act"](S.activation(f[:, 0:SEQ], pb[ct], ACT.Relu))
                                c["act"](S.activation(f[:, SEQ:T], pb[4 + ct][:, 0:DEC], ACT.Relu))
                                S.sem_inc(act_for_dve, 1)
                    c["act_from_pe"].leave(4)
                    c["act"].leave(4)

                @block.vector
                def _(v):
                    dv = c["dve"]
                    V.sem_inc(dve_for_pe, 4)
                    with v.Fori(0, 4) as i:
                        c["dve_from_act"].enter(i, 8)
                        dv.enter(i, 8)
                        for sl in range(2):
                            for ct in range(4):
                                f = ff[:, bass.ds(i * 8 + sl * 4 + ct, 1), :].rearrange("p o t -> p (o t)")
                                v.wait_ge(act_for_dve, c["dve_from_act"].next())
                                V.sem_inc(dve_for_pe, 1)
                                dv(V.tensor_tensor(f, f, f, mult))
                            V.sem_inc(slot_free[sl], 1)
                    c["dve_from_act"].leave(4)
                    dv.leave(4)

            with nc.Block() as block:
                @block.sync
                def _(sp):
                    w2 = L("w_ff2")
                    for og in range(2):
                        for kg in range(4):
                            load_w(sp, kg % 2, w2[kg * 1024:(kg + 1) * 1024, og * 512:(og + 1) * 512])

                @block.tensor
                def _(pe):
                    for og in range(2):
                        for kg in range(4):
                            pe.wait_ge(slot_full[kg % 2], c["pe_full"][kg % 2].next(16))
                            t = fm_tiles(pe, wslot(kg % 2), kg * 8, ff, 4, c["pe_from_dve"], pe_for_dve,
                                         first=(kg == 0), last=(kg == 3))
                            if kg < 3:
                                t.then_inc(slot_free[kg % 2], 1)
                    c["pe_from_dve"].skip(4)

                @block.vector
                def _(v):
                    V.sem_inc(dve_for_pe, 4)
                    for og in range(2):
                        for ct in range(4):
                            v.wait_ge(pe_for_dve, c["dve_from_pe"].next())
                            residual(v, c["dve"], 4 * og + ct, ct, 40, tmp8)
                        V.sem_inc(slot_free[1], 1)
            clear()

        c = counts()
        with nc.Block() as block:
            @block.tensor
            def _(pe):
                for m in range(5):
                    if m >= 3:
                        pe.wait_ge(dve_for_pe, c["pe_from_dve"].next())
                    r = P if m < MT else DEC
                    for k in range(KD):
                        t = tr(pb[2 * (m % 3) + k // 4][0:r, (k % 4) * P:(k % 4 + 1) * P], xT[:, k, m * P:m * P + r])
                    t.then_inc(pe_for_dve, 1)

            @block.vector
            def _(v):
                for m in range(5):
                    r = P if m < MT else DEC
                    v.wait_ge(pe_for_dve, c["dve_from_pe"].next())
                    for j in range(2):
                        c["dve"](V.tensor_copy(arena[0:r, m * D + j * 512:m * D + (j + 1) * 512], pb[2 * (m % 3) + j][0:r]))
                    V.sem_inc(dve_for_pe, 1)
                    V.sem_inc(dve_for_sp, 1)

            @block.sync
            def _(sp):
                for m in range(5):
                    sp.wait_ge(dve_for_sp, c["sp_from_dve"].next())
                    if m < MT:
                        sp.dma_start(y_p[0, m * P:(m + 1) * P, :], arena[:, m * D:(m + 1) * D]).then_inc(stored, 16)
                    else:
                        sp.dma_start(y_s.rearrange("b o d -> b (o d)"), arena[0:DEC, m * D:(m + 1) * D]).then_inc(stored, 16)
                sp.wait_ge(stored, c["stored"].next(80))


_INS = ['x_prompt', 'x_sample', 'c_prompt', 'c_sample', 'cache_k_diff', 'cache_v_diff', 'page_table', 'state_ret',
        'state_rwkv', 'state_shift', 'rel_bias', 'w_ada', 'b_ada', 'norm1', 'norm2', 'w_in', 'qk_norm_q', 'qk_norm_k',
        'lambda_q1', 'lambda_k1', 'lambda_q2', 'lambda_k2', 'subln_diff', 'mu_shift', 'w0', 'w_decay_up', 'a0',
        'w_a_up', 'w_g_up', 'v0', 'w_v_down', 'w_v_up', 'k_k', 'k_a', 'r_k', 'lnx_g', 'lnx_b', 'w_up_a', 'w_up_b',
        'w_up_c', 'w_out', 'w_ff1', 'w_ff2']
_OUTS = [(1, SEQ, D), (DEC, 1, D), (DEPTH, 1, SEQ, HB, 2 * DB), (DEPTH, 1, SEQ, HB, DVB), (DEPTH, DEC, 1, HB, 2 * DB),
         (DEPTH, DEC, 1, HB, DVB), (DEPTH, 1, HA, DA, DA), (DEPTH, DEC, HA, DA, DA), (DEPTH, 1, HC, DC, DC),
         (DEPTH, DEC, HC, DC, DC), (DEPTH, 1, 1, RW), (DEPTH, DEC, 1, RW)]


def kernel(**inputs):
    import numpy as _np
    import concourse.bacc as _bacc
    from concourse import mybir as _mybir
    from concourse.bass_utils import run_bass_kernel_spmd as _run

    nc = _bacc.Bacc("TRN2", target_bir_lowering=False, num_devices=1)
    arrays, args = {}, {}
    for name in _INS:
        v = _np.ascontiguousarray(inputs[name])
        arrays[f"in_{name}_dram"] = v
        args[name] = nc.dram_tensor(f"in_{name}_dram", v.shape, _mybir.dt.from_np(v.dtype), kind="ExternalInput").ap()
    table = shape_constants()
    arrays["shape_constants_dram"] = table
    consts = nc.dram_tensor("shape_constants_dram", table.shape, F32, kind="ExternalInput").ap()
    outs = [nc.dram_tensor(f"out_{i}_dram", shape, F32, kind="ExternalOutput").ap() for i, shape in enumerate(_OUTS)]
    build(nc, args, consts, outs)
    r = _run(nc, [arrays], core_ids=[0])
    return tuple(r.results[0][f"out_{i}_dram"] for i in range(len(_OUTS)))
```

```python
import math
from contextlib import ExitStack

import numpy as np

import concourse.bass as bass
from concourse import mybir

F32 = mybir.dt.float32
I32 = mybir.dt.int32
ALU = mybir.AluOpType
ACT = mybir.ActivationFunctionType
AX = mybir.AxisListType

P = 128
D = 1024
KD = D // P
SEQ = 512
MT = SEQ // P
DEC = 8
T = SEQ + DEC
TH = T // 2
DEPTH = 2
PAST, PAGE = 256, 128
NPG = PAST // PAGE
NB = 32
HA, DA = 4, 128
HB, DB, DVB = 4, 64, 128
HC, DC = 8, 64
HP = HC // 2
W = 512
CH = 64
RW = 3 * W + 64 + 64 + 160
RT = 15
RET0, DIFF0, RW0 = 0, 2048, 3584
GATE0 = RW0 + RW
DFF = 4096
KF = DFF // P
EPS = 1e-6
LNX_EPS = 64e-5
MASKED = -1e30
TOE = 640

_c = 0
COL = {}
for _n, _w in (("ident", P), ("ones", P), ("blk", P), ("inner", HA * P), ("cross", HA * P), ("keep", 2 * P),
               ("level", 6 * P), ("cosq", 320), ("sinq", 320), ("cosk", 320), ("sink", 320), ("tail", HA),
               ("chunk", HA), ("gamma", HA), ("scan", T), ("c0", HB * DEC), ("c1", HB * DEC), ("selb", DEC),
               ("pair", 2), ("laminit", 2 * DEPTH), ("vmix", DEPTH), ("toe", TOE), ("past", NPG * P)):
    COL[_n] = (_c, _w)
    _c += _w
NCONST = _c
NKEPT = COL["toe"][0]

PROW = {}
_r = 0
for _n, _w in (("b_ada", 48), ("norm1", 8), ("norm2", 8), ("mu", 15), ("w0", 4), ("a0", 4), ("v0", 4),
               ("k_k", 4), ("k_a", 4), ("r_k", 4)):
    PROW[_n] = (_r, _w)
    _r += _w
NPAR = _r

BROW = {}
_b = 0
for _n, _w in (("qn", 64), ("kn", 64), ("lq1", 64), ("lk1", 64), ("lq2", 64), ("lk2", 64), ("subln", 128),
               ("lnx_g", 512), ("lnx_b", 512)):
    BROW[_n] = (_b, _w)
    _b += _w
NROW = _b


def shape_constants():
    t = np.zeros((P, NCONST), np.float32)

    def put(name, a):
        o, w = COL[name]
        a = np.asarray(a, np.float32)
        a = a.reshape(a.shape[0], -1)
        assert a.shape[1] == w, (name, a.shape)
        t[:a.shape[0], o:o + w] = a

    i = np.arange(P)
    put("ident", np.eye(P))
    put("ones", np.ones((P, P)))
    put("blk", (i[:, None] // 64) == (i[None, :] // 64))
    log_g = np.log1p(-np.exp2(-5.0 - np.arange(HA, dtype=np.float32))).astype(np.float32)
    dist = i[None, :] - i[:, None]
    put("inner", np.stack([np.where(dist >= 0, np.exp(np.maximum(dist, 0) * g), 0.0) for g in log_g], 1))
    put("cross", np.broadcast_to(np.stack([np.exp((i + 1.0) * g) for g in log_g])[None], (P, HA, P)))
    put("tail", np.exp((P - 1.0 - i)[:, None] * log_g[None]))
    put("chunk", np.broadcast_to(np.exp(P * log_g)[None], (P, HA)))
    put("gamma", np.broadcast_to(np.exp(log_g)[None], (P, HA)))
    same = (i[:, None] // CH) == (i[None, :] // CH)
    before = same & (i[:, None] < i[None, :])
    upto = same & (i[:, None] <= i[None, :])
    put("keep", np.stack([before, upto], 1))
    lv = []
    for k in range(6):
        m = 1 << k
        lv.append((i[:, None] // (2 * m) == i[None, :] // (2 * m)) & (i[:, None] % (2 * m) >= m)
                  & (i[None, :] % (2 * m) < m))
    put("level", np.stack(lv, 1))
    half = DA // 2
    inv = (np.float32(10000.0) ** (-np.arange(half, dtype=np.float32) / np.float32(half))).astype(np.float32)
    pos = np.zeros((P, 5), np.float32)
    for m in range(MT):
        pos[:, m] = m * P + i
    pos[:, 4] = PAST
    ang = (pos[:, :, None] * inv[None, None, :]).astype(np.float32)
    cs, sn = np.cos(ang), np.sin(ang)
    sc = DA ** -0.5
    put("cosq", cs)
    put("sinq", sn)
    put("cosk", cs * sc)
    put("sink", sn * sc)
    scan = np.ones(T)
    scan[0:SEQ:CH] = 0
    scan[SEQ:] = 0
    put("scan", np.broadcast_to(scan[None], (P, T)))

    def bucket(n):
        n = np.maximum(n, 0)
        nf = np.maximum(n, 1).astype(np.float32)
        large = 16 + (np.log(nf / np.float32(16)).astype(np.float32) / np.float32(math.log(128 / 16))
                      * np.float32(16)).astype(np.int32)
        return np.where(n < 16, n, np.minimum(large, NB - 1))

    n = 511 - np.arange(TOE)
    toe = np.zeros((NB + 1, TOE), np.float32)
    toe[bucket(n), np.arange(TOE)] = (n >= 0)
    toe[NB] = np.where(n >= 0, 0.0, 1.0)
    put("toe", toe)
    n = PAST - np.arange(PAST)
    past = np.zeros((NB, PAST), np.float32)
    past[bucket(n), np.arange(PAST)] = 1
    put("past", past)
    r = np.arange(DEC * 8)
    bb, hh, cc = r // 8, (r // 2) % 4, r % 2
    col = np.arange(HB * DEC)
    hit = (bb[:, None] == col[None] % DEC) & (hh[:, None] == col[None] // DEC)
    put("c0", hit & (cc[:, None] == 0))
    put("c1", hit & (cc[:, None] == 1))
    put("selb", bb[:, None] == np.arange(DEC)[None])
    put("pair", (i[:, None] // 64) == np.arange(2)[None])
    li = [0.8 - 0.6 * math.exp(-0.3 * l) for l in range(DEPTH)]
    put("laminit", np.broadcast_to(np.array([[x, 1.0 - x] for x in li])[None], (P, DEPTH, 2)))
    put("vmix", np.broadcast_to((np.arange(DEPTH) > 0)[None], (P, DEPTH)))
    return t


class Count:

    def __init__(self, sem):
        self.sem, self.base, self.i, self.per, self.j = sem, 0, None, 0, 0

    def next(self, by=1):
        self.j += by
        if self.i is None:
            self.base, self.j = self.base + self.j, 0
            return self.base
        return self.i * self.per + (self.base + self.j)

    def skip(self, n):
        assert self.i is None
        self.base += n

    def enter(self, i, per):
        self.i, self.per = i, per

    def leave(self, n):
        assert self.j == self.per, (self.j, self.per)
        self.base, self.i, self.j = self.base + n * self.per, None, 0


class Chain(Count):

    def __init__(self, eng, sem):
        super().__init__(sem)
        self.eng = eng

    def __call__(self, ins):
        ins.then_inc(self.sem, 1)
        self.eng.wait_ge(self.sem, self.next())


def build(nc, a, consts, outs):
    (y_p, y_s, k_p, v_p, k_s, v_s, ret_p, ret_s, rwkv_p, rwkv_s, shift_p, shift_s) = outs
    skew = nc.dram_tensor("skew_dram", (HB, P, TOE), F32, kind="Internal").ap()
    V, S, G, PE = nc.vector, nc.scalar, nc.gpsimd, nc.tensor
    with ExitStack() as ctx:
        def sb(name, n, dt=F32, p=P):
            return ctx.enter_context(nc.sbuf_tensor(name, [p, n], dt))

        xT = sb("xT", KD * T)[:, :].rearrange("p (k t) -> p k t", k=KD)
        hT = sb("hT", KD * T)[:, :].rearrange("p (k t) -> p k t", k=KD)
        ring = [sb("ring0", 4096)[:, :], sb("ring1", 4096)[:, :], None, None]
        vfirst = sb("vfirst", HP * T)[:, :].rearrange("p (k t) -> p k t", k=HP)
        y_raw = sb("yT", 12 * T)[:, :]
        yT = y_raw.rearrange("p (k t) -> p k t", k=12)
        modT = sb("modT", 48 * 9)[:, :].rearrange("p (k s) -> p k s", k=48)
        coef = sb("coef", KD * 9)[:, :].rearrange("p (k s) -> p k s", k=KD)
        csT = sb("csT", KD * 9)[:, :].rearrange("p (k s) -> p k s", k=KD)
        par = sb("par", NPAR)[:, :]
        rows = sb("rows", NROW)[:, :]
        cst = sb("cst", NKEPT)[:, :]
        biasD = sb("biasD", NPG * HB)[:, :].rearrange("p (g h) -> p g h", g=NPG)
        bias0 = sb("bias0", HB)[:, :]
        tab = sb("tab", HB)[:, :]
        rstd = sb("rstd", T)[:, :]
        small = sb("small", 512)[:, :]
        pages = sb("pages", DEC * NPG, I32, 1)[:, :]
        AR = 20720
        arena = sb("arena", AR)[:, :]
        ring[2], ring[3] = arena[:, 6300:10396], arena[:, 10396:14492]
        pb = [ctx.enter_context(nc.psum_tensor(f"pb{i}", [P, 512], F32))[:, :] for i in range(8)]

        def at(base, off, *dims):
            n = 1
            for d in dims:
                n *= d
            ap = base[:, off:off + n]
            if len(dims) == 2:
                return ap.rearrange("p (a b) -> p a b", a=dims[0])
            if len(dims) == 3:
                return ap.rearrange("p (a b c) -> p a b c", a=dims[0], b=dims[1])
            if len(dims) == 4:
                return ap.rearrange("p (a b c d) -> p a b c d", a=dims[0], b=dims[1], c=dims[2])
            return ap

        def C(name, *dims):
            return at(cst, COL[name][0], *(dims or (COL[name][1],)))

        def PR(name):
            return par[:, PROW[name][0]:PROW[name][0] + PROW[name][1]]

        def BR(name):
            return rows[:, BROW[name][0]:BROW[name][0] + BROW[name][1]]

        ident, ones, blk = C("ident"), C("ones"), C("blk")
        eps = small[:, 0:1]
        eps_ln = small[:, 1:2]
        lam = small[:, 2:3]

        def sem(name):
            return ctx.enter_context(nc.semaphore(name))

        sems = {n: sem(n) for n in (
            "slot0_full", "slot1_full", "slot2_full", "slot3_full", "slot0_free", "slot1_free", "slot2_free", "slot3_free", "loaded", "loaded_act", "stored",
            "pe_for_dve", "dve_for_pe", "pe_for_act", "act_for_pe", "dve_for_act", "act_for_dve",
            "dve_done", "act_done", "dve_for_sp", "page0_full", "page1_full", "page_free",
            "scores_ready", "scores_read", "logits_ready", "exp_ready", "weights_ready", "turned", "turned_read",
            "values_ready", "values_read")}
        pe_for_dve, dve_for_pe = sems["pe_for_dve"], sems["dve_for_pe"]
        pe_for_act, act_for_pe = sems["pe_for_act"], sems["act_for_pe"]
        dve_for_act, act_for_dve = sems["dve_for_act"], sems["act_for_dve"]
        loaded, stored = sems["loaded"], sems["stored"]
        dve_for_sp = sems["dve_for_sp"]
        page_full, page_free = [sems["page0_full"], sems["page1_full"]], sems["page_free"]
        scores_ready, scores_read, logits_ready = sems["scores_ready"], sems["scores_read"], sems["logits_ready"]
        exp_ready, weights_ready = sems["exp_ready"], sems["weights_ready"]
        turned, turned_read = sems["turned"], sems["turned_read"]
        values_ready, values_read = sems["values_ready"], sems["values_read"]
        slot_full = [sems[f"slot{n}_full"] for n in range(4)]
        slot_free = [sems[f"slot{n}_free"] for n in range(4)]

        def counts():
            c = {
                "pe_full": [Count(s) for s in slot_full], "sp_free": [Count(s) for s in slot_free],
                "dve_from_pe": Count(pe_for_dve), "pe_from_dve": Count(dve_for_pe),
                "act_from_pe": Count(pe_for_act), "pe_from_act": Count(act_for_pe),
                "act_from_dve": Count(dve_for_act), "dve_from_act": Count(act_for_dve),
                "dve": Chain(V, sems["dve_done"]), "act": Chain(S, sems["act_done"]),
                "loaded": Count(loaded), "stored": Count(stored),
                "sp_from_dve": Count(dve_for_sp), 
            }
            return c

        def clear():
            with nc.Block() as block:
                @block.gpsimd
                def _(g):
                    for s in sems.values():
                        g.sem_clear(s)

        def mm(out, lhsT, rhs, start=True, stop=True):
            return PE.matmul(out, lhsT, rhs, start=start, stop=stop, skip_group_check=True)

        def tr(out, in_):
            return PE.transpose(out, in_, ident[0:in_.shape[0], 0:in_.shape[0]])

        def bc(ap, shape, *dims):
            for d in dims:
                ap = ap.unsqueeze(d)
            return ap.broadcast_to(shape)

        mult, add, sub, amax = ALU.mult, ALU.add, ALU.subtract, ALU.max

        c = counts()
        dist_rows = arena[:, 11000:11000 + NCONST - NKEPT]
        toe, past = dist_rows[:, 0:TOE], dist_rows[:, TOE:TOE + NPG * P]
        with nc.Block() as block:
            @block.vector
            def _(v):
                c["dve"](V.memset(arena[:, 4096:6144], 0.0))
        with nc.Block() as block:
            @block.sync
            def _(sp):
                sp.dma_start(cst, consts[:, 0:NKEPT]).then_inc(loaded, 16)
                sp.dma_start(dist_rows, consts[:, NKEPT:NCONST]).then_inc(loaded, 16)
                sp.dma_start(at(arena, 0, MT, D), a["x_prompt"].rearrange("o (m p) d -> p (o m) d", p=P)).then_inc(loaded, 16)
                sp.dma_start(arena[0:DEC, 4096:5120], a["x_sample"].rearrange("b o d -> b (o d)")).then_inc(loaded, 16)
                sp.dma_start(arena[0:1, 5120:6144], a["c_prompt"]).then_inc(loaded, 16)
                sp.dma_start(arena[1:9, 5120:6144], a["c_sample"]).then_inc(loaded, 16)
                sp.dma_start(tab[0:NB, :], a["rel_bias"]).then_inc(loaded, 16)
                sp.dma_start(bias0, a["rel_bias"][0].partition_broadcast(P)).then_inc(loaded, 16)
                sp.dma_start(pages, a["page_table"].rearrange("(o b) g -> o (b g)", o=1)).then_inc(loaded, 16)
                sp.wait_ge(loaded, 9 * 16)

            @block.vector
            def _(v):
                dv = c["dve"]
                dv(V.memset(arena[:, 6144:11000], 0.0))
                dv(V.memset(arena[:, 11000 + NCONST - NKEPT:AR], 0.0))
                dv(V.memset(tab[NB:NB + 1, :], MASKED))
                dv(V.memset(small, 0.0))
                dv(V.memset(eps, EPS))
                dv(V.memset(eps_ln, LNX_EPS))
                dv(V.memset(vfirst, 0.0))
                dv(V.memset(ring[1], 0.0))
                dv(V.memset(y_raw, 0.0))
        c["loaded"].skip(9 * 16)
        with nc.Block() as block:
            @block.scalar
            def _(s):
                c["act"](S.activation(arena[0:9, 6144:7168], arena[0:9, 5120:6144], ACT.Sigmoid))
                S.sem_inc(act_for_dve, 1)

            @block.tensor
            def _(pe):
                for k in range(KD):
                    if k >= 4:
                        pe.wait_ge(dve_for_pe, c["pe_from_dve"].next())
                    for m in range(MT):
                        tr(pb[k % 4][:, m * P:(m + 1) * P], arena[:, m * D + k * P:m * D + (k + 1) * P])
                    tr(pb[4 + k % 4][:, 0:DEC], arena[0:DEC, 4096 + k * P:4096 + (k + 1) * P]).then_inc(pe_for_dve, 1)
                pe.wait_ge(dve_for_pe, c["pe_from_dve"].next(5))
                for k in range(KD):
                    t = tr(pb[0][:, k * 9:k * 9 + 9], arena[0:9, 6144 + k * P:6144 + (k + 1) * P])
                t.then_inc(pe_for_dve, 1)
                pe.wait_ge(dve_for_pe, c["pe_from_dve"].next())
                for h in range(HB):
                    mm(pb[h], tab[0:NB + 1, h:h + 1].broadcast_to([NB + 1, P]), toe[0:NB + 1, 0:512])
                    mm(pb[4 + h][:, 0:128], tab[0:NB + 1, h:h + 1].broadcast_to([NB + 1, P]),
                       toe[0:NB + 1, 512:640])
                for g in range(NPG):
                    t = mm(pb[4][:, 256 + g * HB:256 + (g + 1) * HB], past[0:NB, g * P:(g + 1) * P], tab[0:NB, :])
                t.then_inc(pe_for_dve, 1)

            @block.vector
            def _(v):
                dv = c["dve"]
                for k in range(KD):
                    v.wait_ge(pe_for_dve, c["dve_from_pe"].next())
                    V.tensor_copy(xT[:, k, 0:SEQ], pb[k % 4])
                    dv(V.tensor_copy(xT[:, k, SEQ:T], pb[4 + k % 4][:, 0:DEC]))
                    V.sem_inc(dve_for_pe, 1)
                v.wait_ge(act_for_dve, c["dve_from_act"].next())
                dv(V.tensor_tensor(arena[0:9, 6144:7168], arena[0:9, 6144:7168], arena[0:9, 5120:6144], mult))
                V.sem_inc(dve_for_pe, 1)
                v.wait_ge(pe_for_dve, c["dve_from_pe"].next())
                dv(V.tensor_copy(csT.rearrange("p k s -> p (k s)"), pb[0][:, 0:72]))
                V.sem_inc(dve_for_pe, 1)
                v.wait_ge(pe_for_dve, c["dve_from_pe"].next())
                for h in range(HB):
                    V.tensor_copy(at(arena, 8192, HB, TOE)[:, h, 0:512], pb[h])
                    V.tensor_copy(at(arena, 8192, HB, TOE)[:, h, 512:640], pb[4 + h][:, 0:128])
                dv(V.tensor_copy(biasD.rearrange("p g h -> p (g h)"), pb[4][:, 256:256 + NPG * HB]))
                V.sem_inc(dve_for_sp, 1)

            @block.sync
            def _(sp):
                sp.wait_ge(dve_for_sp, c["sp_from_dve"].next())
                sp.dma_start(skew.rearrange("h p u -> p h u"), at(arena, 8192, HB, TOE)).then_inc(loaded, 16)
                sp.wait_ge(loaded, c["loaded"].next(16))
        clear()

        with nc.Fori(0, DEPTH) as l:
            c = counts()

            def L(name):
                ap = a[name][bass.ds(l, 1)]
                dims = "abcdef"[:len(ap.shape) - 1]
                return ap.rearrange("o " + " ".join(dims) + " -> (o " + dims[0] + ") " + " ".join(dims[1:]))

            def Lo(ap):
                ap = ap[bass.ds(l, 1)]
                dims = "abcdef"[:len(ap.shape) - 1]
                return ap.rearrange("o " + " ".join(dims) + " -> (o " + dims[0] + ") " + " ".join(dims[1:]))

            def load_w(sp, slot, src, k=8):
                sp.wait_ge(slot_free[slot], c["sp_free"][slot].next())
                n = src.shape[1]
                sp.dma_start(at(ring[slot], 0, k, 4096 // k)[:, :, 0:n],
                             src.rearrange("(k p) n -> p k n", p=P)).then_inc(slot_full[slot], 16)

            def wslot(slot, k=8):
                return at(ring[slot], 0, k, 4096 // k)

            def fm_tiles(pe, w, k0, src, n_tiles, cnt_free, done, nk=8, first=True, last=True, wk=0):
                for ct in range(n_tiles):
                    if first:
                        pe.wait_ge(cnt_free.sem, cnt_free.next())
                    mc = min(P, w.shape[2] - ct * P)
                    for k in range(nk):
                        for half in range(2):
                            t = mm(pb[4 * half + ct][0:mc, 0:TH], w[:, wk + k, ct * P:ct * P + mc],
                                   src[:, k0 + k, half * TH:(half + 1) * TH],
                                   start=first and k == 0, stop=last and k == nk - 1)
                    if last:
                        t.then_inc(done, 1)
                return t

            with nc.Block() as block:
                @block.sync
                def _(sp):
                    n = 0
                    for name in PROW:
                        r0, nr = PROW[name]
                        if name == "v0":
                            src = a["v0"].rearrange("o (r c) -> (o r) c", c=P)
                        elif name == "mu":
                            mu = L("mu_shift")
                            sp.dma_start(arena[r0 + 14:r0 + 15, 0:32], mu[14 * P:RW].rearrange("(o c) -> o c", o=1)).then_inc(loaded, 16)
                            src = mu[0:14 * P].rearrange("(r c) -> r c", c=P)
                            n += 1
                        elif name == "r_k":
                            src = L("r_k").rearrange("(r h) d -> r (h d)", h=2)
                        else:
                            src = L(name).rearrange("(r c) -> r c", c=P)
                        sp.dma_start(arena[r0:r0 + src.shape[0], 0:P], src).then_inc(loaded, 16)
                        n += 1
                    for name, key in (("qn", "qk_norm_q"), ("kn", "qk_norm_k"), ("lq1", "lambda_q1"), ("lk1", "lambda_k1"),
                                      ("lq2", "lambda_q2"), ("lk2", "lambda_k2"), ("subln", "subln_diff"),
                                      ("lnx_g", "lnx_g"), ("lnx_b", "lnx_b")):
                        sp.dma_start(BR(name), L(key).partition_broadcast(P)).then_inc(loaded, 16)
                        n += 1
                    sp.wait_ge(loaded, 16 * n)
                    c["loaded"].skip(16 * n)

                @block.tensor
                def _(pe):
                    for s in range(4):
                        pe.sem_inc(slot_free[s], 1)
            with nc.Block() as block:
                @block.tensor
                def _(pe):
                    tr(pb[0][:, 0:NPAR], arena[0:NPAR, 0:P]).then_inc(pe_for_dve, 1)

                @block.vector
                def _(v):
                    dv = c["dve"]
                    v.wait_ge(pe_for_dve, c["dve_from_pe"].next())
                    dv(V.tensor_copy(par, pb[0][:, 0:NPAR]))
                    dv(V.tensor_tensor(small[:, 16:80], BR("lq1"), BR("lk1"), mult))
                    dv(V.tensor_tensor(small[:, 80:144], BR("lq2"), BR("lk2"), mult))
                    dv(V.tensor_reduce(small[:, 4:6], at(small, 16, 2, 64), AX.X, add))
                    V.sem_inc(dve_for_act, 1)
                    v.wait_ge(act_for_dve, c["dve_from_act"].next())
                    dv(V.tensor_tensor(lam, small[:, 6:7], small[:, 7:8], sub))
                    li = C("laminit", DEPTH, 2)
                    dv(V.tensor_tensor(lam, lam, li[:, bass.ds(l, 1), 0:1].rearrange("p a b -> p (a b)"), add))
                    dv(V.tensor_scalar(BR("subln"), BR("subln"), li[:, bass.ds(l, 1), 1:2].rearrange("p a b -> p (a b)"), None, mult))

                @block.scalar
                def _(s):
                    s.wait_ge(dve_for_act, c["act_from_dve"].next())
                    c["act"](S.activation(small[:, 6:8], small[:, 4:6], ACT.Exp))
                    S.sem_inc(act_for_dve, 1)

            w_in = L("w_in")
            mrows = at(arena, 0, 4, 512)[0:9]

            def prefetch(sp, *blocks):
                for s, src in enumerate(blocks):
                    load_w(sp, s, src)

            with nc.Block() as block:
                @block.sync
                def _(sp):
                    wa = L("w_ada")
                    for s in range(4):
                        load_w(sp, s, wa[:, s * 512:(s + 1) * 512])
                    with sp.Fori(0, 2) as i:
                        for s in range(4):
                            c["sp_free"][s].enter(i, 1)
                            load_w(sp, s, wa[:, bass.ds(i * 2048 + (s + 4) * 512, 512)])
                    for s in range(4):
                        c["sp_free"][s].leave(2)
                    prefetch(sp, w_in[:, RET0:RET0 + 512], w_in[:, RET0 + 512:RET0 + 1024])

                @block.tensor
                def _(pe):
                    for i in range(3):
                        for s in range(5):
                            if s < 4:
                                pe.wait_ge(slot_full[s], c["pe_full"][s].next(16))
                                w = wslot(s)
                                for k in range(KD):
                                    t = mm(pb[s][0:9, :], csT[:, k, :], w[:, k, :], start=(k == 0), stop=(k == KD - 1))
                                t.then_inc(pe_for_dve, 1)
                            if s:
                                pe.wait_ge(dve_for_pe, c["pe_from_dve"].next())
                                for ct in range(4):
                                    t = tr(pb[3 + s][:, ct * 9:ct * 9 + 9], mrows[:, s - 1, ct * P:(ct + 1) * P])
                                t.then_inc(pe_for_dve, 1)

                @block.vector
                def _(v):
                    with v.Fori(0, 3) as i:
                        c["dve_from_pe"].enter(i, 8)
                        c["dve"].enter(i, 8)
                        for s in range(5):
                            if s < 4:
                                v.wait_ge(pe_for_dve, c["dve_from_pe"].next())
                                c["dve"](V.tensor_copy(mrows[:, s], pb[s][0:9, :]))
                                V.sem_inc(dve_for_pe, 1)
                                V.sem_inc(slot_free[s], 1)
                            if s:
                                v.wait_ge(pe_for_dve, c["dve_from_pe"].next())
                                c["dve"](V.tensor_tensor(
                                    modT[:, bass.ds(i * 16 + (s - 1) * 4, 4), :],
                                    pb[3 + s][:, 0:36].rearrange("p (c s) -> p c s", c=4),
                                    bc(PR("b_ada")[:, bass.ds(i * 16 + (s - 1) * 4, 4)], [P, 4, 9], 2), add))
                    c["dve_from_pe"].leave(3)
                    c["dve"].leave(3)

            def norm_stage(gain, shift0, scale0):
                with nc.Block() as block:
                    @block.vector
                    def _(v):
                        dv = c["dve"]
                        sq = at(arena, 0, KD, T)
                        dv(V.tensor_tensor(sq, xT, xT, mult))
                        V.sem_inc(dve_for_pe, 1)
                        dv(V.tensor_scalar(coef, modT[:, scale0:scale0 + KD, :], 1.0, None, add))
                        dv(V.tensor_tensor(coef, coef, bc(PR(gain), [P, KD, 9], 2), mult))
                        v.wait_ge(act_for_dve, c["dve_from_act"].next())
                        dv(V.reciprocal(rstd, rstd))
                        dv(V.tensor_tensor(hT, xT, bc(rstd, [P, KD, T], 1), mult))
                        for k in range(KD):
                            V.tensor_scalar(hT[:, k, 0:SEQ], hT[:, k, 0:SEQ], coef[:, k, 0:1],
                                            modT[:, shift0 + k, 0:1], mult, add)
                        dv(V.tensor_tensor(hT[:, :, SEQ:T], hT[:, :, SEQ:T], coef[:, :, 1:9], mult))
                        dv(V.tensor_tensor(hT[:, :, SEQ:T], hT[:, :, SEQ:T], modT[:, shift0:shift0 + KD, 1:9], add))

                    @block.tensor
                    def _(pe):
                        sq = at(arena, 0, KD, T)
                        pe.wait_ge(dve_for_pe, c["pe_from_dve"].next())
                        for k in range(KD):
                            for half in range(2):
                                t = mm(pb[half][:, 0:TH], ones, sq[:, k, half * TH:(half + 1) * TH],
                                       start=(k == 0), stop=(k == KD - 1))
                        t.then_inc(pe_for_act, 1)

                    @block.scalar
                    def _(s):
                        s.wait_ge(pe_for_act, c["act_from_pe"].next())
                        for half in range(2):
                            c["act"](S.activation(rstd[:, half * TH:(half + 1) * TH], pb[half][:, 0:TH], ACT.Sqrt,
                                                  bias=eps, scale=1.0 / D))
                        S.sem_inc(act_for_dve, 1)

            norm_stage("norm1", 0, 8)

            def token_major(col0, n_blocks):
                with nc.Block() as block:
                    @block.sync
                    def _(sp):
                        for b in range(2, n_blocks):
                            load_w(sp, b % 2, w_in[:, col0 + 512 * b:col0 + 512 * (b + 1)])

                    @block.tensor
                    def _(pe):
                        for b in range(n_blocks):
                            pe.wait_ge(slot_full[b % 2], c["pe_full"][b % 2].next(16))
                            w = wslot(b % 2)
                            for m in range(5):
                                pe.wait_ge(act_for_pe, c["pe_from_act"].next())
                                r = P if m < MT else DEC
                                for k in range(KD):
                                    t = mm(pb[m][0:r, :], hT[:, k, m * P:m * P + r], w[:, k, :],
                                           start=(k == 0), stop=(k == KD - 1))
                                t.then_inc(pe_for_act, 1)
                        c["pe_from_act"].skip(5)

                    @block.scalar
                    def _(s):
                        S.sem_inc(act_for_pe, 5)
                        for b in range(n_blocks):
                            for m in range(5):
                                r = P if m < MT else DEC
                                s.wait_ge(pe_for_act, c["act_from_pe"].next())
                                c["act"](S.activation(arena[0:r, (b * 5 + m) * 512:(b * 5 + m + 1) * 512],
                                                      pb[m][0:r, :], ACT.Copy))
                                S.sem_inc(act_for_pe, 1)
                            S.sem_inc(slot_free[b % 2], 1)

            def heads_to_columns(block_fns, srcs, dst, heads=4, m_tiles=5):
                def pe_part(pe):
                    for n, src in enumerate(srcs):
                        pe.wait_ge(dve_for_pe, c["pe_from_dve"].next())
                        for h in range(heads):
                            for m in range(MT):
                                tr(pb[h][:, m * P:(m + 1) * P], src[:, m, h * P:(h + 1) * P])
                            t = tr(pb[4 + h][:, 0:DEC], src[0:DEC, MT, h * P:(h + 1) * P])
                        t.then_inc(pe_for_dve, 1)

                def dve_part(v):
                    for n, src in enumerate(srcs):
                        V.sem_inc(dve_for_pe, 1)
                        v.wait_ge(pe_for_dve, c["dve_from_pe"].next())
                        for h in range(heads):
                            V.tensor_copy(dst[:, 4 * n + h, 0:SEQ], pb[h])
                            c["dve"](V.tensor_copy(dst[:, 4 * n + h, SEQ:T], pb[4 + h][:, 0:DEC]))
                return pe_part, dve_part

            token_major(RET0, 4)
            Z = lambda b: at(arena, b * 2560, 5, 512)
            rot = [at(arena, 10240, 5, 512), at(arena, 12800, 5, 512)]
            qkT = at(arena, 0, 8, T)
            with nc.Block() as block:
                pe_part, dve_part = heads_to_columns(None, rot, qkT)
                vmask = at(ring[0], 0, DEC, 512)
                dstate = at(y_raw, 4 * T, 2, 4, HA, P)
                qc = at(arena, 10240, HA, SEQ)
                sc = at(arena, 15360, HA, P)
                st = at(arena, 15872, HA, P)
                od = at(arena, 16384, HA, DEC)
                oa = at(arena, 16640, 5, 512)

                @block.vector
                def _(v):
                    dv = c["dve"]
                    tmp = at(arena, 15360, 5, HA, 64)
                    for n, (cn, sn) in enumerate((("cosq", "sinq"), ("cosk", "sink"))):
                        x = at(arena, n * 2560, 20, 2, 64).rearrange("p (m h) t d -> p m h t d", m=5)
                        o = at(arena, 10240 + n * 2560, 20, 2, 64).rearrange("p (m h) t d -> p m h t d", m=5)
                        cs = bc(C(cn, 5, 64), [P, 5, HA, 64], 2)
                        sn_ = bc(C(sn, 5, 64), [P, 5, HA, 64], 2)
                        x1, x2, o1, o2 = x[:, :, :, 0, :], x[:, :, :, 1, :], o[:, :, :, 0, :], o[:, :, :, 1, :]
                        dv(V.tensor_tensor(o1, x1, cs, mult))
                        dv(V.tensor_tensor(tmp, x2, sn_, mult))
                        dv(V.tensor_tensor(o1, o1, tmp, sub))
                        dv(V.tensor_tensor(o2, x1, sn_, mult))
                        dv(V.tensor_tensor(tmp, x2, cs, mult))
                        dv(V.tensor_tensor(o2, o2, tmp, add))
                    dve_part(v)
                    kt = at(arena, 12800, MT, HA, P)
                    dv(V.tensor_tensor(kt, kt, bc(C("tail"), [P, MT, HA, P], 1, 3), mult))
                    q4 = at(arena, 0, HA, T)[:, :, 0:SEQ].rearrange("p h (n i) -> p h n i", n=MT)
                    dv(V.tensor_tensor(qc.rearrange("p h (n i) -> p h n i", n=MT), q4,
                                       bc(C("cross", HA, P), [P, HA, MT, P], 2), mult))
                    V.sem_inc(dve_for_pe, 1)
                    for n in range(MT):
                        v.wait_ge(pe_for_dve, c["dve_from_pe"].next())
                        dv(V.tensor_tensor(sc, at(pb[0], 0, HA, P), C("inner", HA, P), mult))
                        V.sem_inc(dve_for_pe, 1)
                        v.wait_ge(pe_for_dve, c["dve_from_pe"].next())
                        dv(V.tensor_copy(oa[:, n, :], pb[1]))
                        if n == 0:
                            dv(V.tensor_copy(st, at(pb[2], 0, HA, P)))
                        else:
                            dv(V.tensor_tensor(st, st, bc(C("chunk"), [P, HA, P], 2), mult))
                            dv(V.tensor_tensor(st, st, at(pb[2], 0, HA, P), add))
                        V.sem_inc(dve_for_pe, 1)
                    V.sem_inc(dve_for_sp, 1)
                    dv(V.tensor_tensor(vmask[0:DEC], bc(Z(2)[0:DEC, MT, :], [DEC, DEC, 512], 1),
                                       bc(ident[0:DEC, 0:DEC], [DEC, DEC, 512], 2), mult))
                    V.sem_inc(dve_for_pe, 1)
                    v.wait_ge(loaded, c["loaded"].base + 16 * DEC)
                    for hf in range(2):
                        v.wait_ge(pe_for_dve, c["dve_from_pe"].next())
                        for h in range(HA):
                            dv(V.scalar_tensor_tensor(dstate[:, hf, :, h, :], dstate[:, hf, :, h, :],
                                                      C("gamma")[:, h:h + 1], at(pb[4 * hf + h], 0, 4, P), mult, add))
                    V.sem_inc(dve_for_pe, 1)
                    V.sem_inc(dve_for_sp, 1)
                    v.wait_ge(pe_for_dve, c["dve_from_pe"].next())
                    dv(V.tensor_copy(od, at(pb[0], 0, HA, DEC)))
                    V.sem_inc(dve_for_pe, 1)
                    v.wait_ge(pe_for_dve, c["dve_from_pe"].next())
                    dv(V.tensor_copy(oa[0:DEC, MT, :], pb[1][0:DEC, :]))

                @block.tensor
                def _(pe):
                    pe_part(pe)
                    pe.wait_ge(dve_for_pe, c["pe_from_dve"].next())
                    for n in range(MT):
                        tok = slice(n * P, (n + 1) * P)
                        for h in range(HA):
                            t = mm(pb[0][:, h * P:(h + 1) * P], qkT[:, 4 + h, tok], qkT[:, h, tok])
                        t.then_inc(pe_for_dve, 1)
                        pe.wait_ge(dve_for_pe, c["pe_from_dve"].next())
                        for h in range(HA):
                            hs = slice(h * P, (h + 1) * P)
                            mm(pb[1][:, hs], sc[:, h, :], Z(2)[:, n, hs], stop=(n == 0))
                            if n:
                                mm(pb[1][:, hs], qc[:, h, tok], st[:, h, :], start=False)
                            t = mm(pb[2][:, hs], rot[1][:, n, hs], Z(2)[:, n, hs])
                        t.then_inc(pe_for_dve, 1)
                        pe.wait_ge(dve_for_pe, c["pe_from_dve"].next())
                    pe.wait_ge(dve_for_pe, c["pe_from_dve"].next())
                    for hf in range(2):
                        for h in range(HA):
                            hs = slice(h * P, (h + 1) * P)
                            t = mm(pb[4 * hf + h], rot[1][0:DEC, MT, hs], vmask[0:DEC, 4 * hf:4 * hf + 4, hs])
                        t.then_inc(pe_for_dve, 1)
                    pe.wait_ge(dve_for_pe, c["pe_from_dve"].next())
                    for b in range(DEC):
                        for h in range(HA):
                            t = mm(pb[0][:, h * DEC + b:h * DEC + b + 1], dstate[:, b // 4, b % 4, h, :],
                                   qkT[:, h, SEQ + b:SEQ + b + 1])
                    t.then_inc(pe_for_dve, 1)
                    pe.wait_ge(dve_for_pe, c["pe_from_dve"].next())
                    for h in range(HA):
                        t = tr(pb[1][0:DEC, h * P:(h + 1) * P], od[:, h, :])
                    t.then_inc(pe_for_dve, 1)

                @block.sync
                def _(sp):
                    sr = L("state_ret").rearrange("b h d e -> d b h e")
                    so = Lo(ret_s).rearrange("b h d e -> d b h e")
                    for b in range(DEC):
                        sp.dma_start(dstate[:, b // 4, b % 4], sr[:, b]).then_inc(loaded, 16)
                    sp.wait_ge(dve_for_sp, c["sp_from_dve"].next())
                    sp.dma_start(Lo(ret_p).rearrange("o h d e -> d (o h) e"), st).then_inc(stored, 16)
                    sp.wait_ge(dve_for_sp, c["sp_from_dve"].next())
                    for b in range(DEC):
                        sp.dma_start(so[:, b], dstate[:, b // 4, b % 4]).then_inc(stored, 16)
                    sp.wait_ge(stored, c["stored"].next(16 + 16 * DEC))
            c["loaded"].skip(16 * DEC)

            def head_rms(v, dv, o, sq, ms, groups, width):
                dv(V.tensor_tensor(sq, o, o, mult))
                dv(V.tensor_reduce(ms, sq.rearrange("p m (g d) -> p (m g) d", d=width), AX.X, add))
                V.sem_inc(dve_for_act, 1)
                v.wait_ge(act_for_dve, c["dve_from_act"].next())
                dv(V.reciprocal(ms, ms))
                og = o.rearrange("p m (g d) -> p (m g) d", d=width)
                dv(V.tensor_tensor(og, og, bc(ms, [P, groups, width], 2), mult))

            def act_root(s, ms, width):
                s.wait_ge(dve_for_act, c["act_from_dve"].next())
                c["act"](S.activation(ms, ms, ACT.Sqrt, bias=eps, scale=1.0 / width))
                S.sem_inc(act_for_dve, 1)

            with nc.Block() as block:
                oa = at(arena, 16640, 5, 512)
                sg = at(arena, 10240, 5, 512)
                sq = at(arena, 12800, 5, 512)
                ms = small[:, 160:180]
                pe_part, dve_part = heads_to_columns(None, [oa], yT)

                @block.sync
                def _(sp):
                    prefetch(sp, w_in[:, DIFF0:DIFF0 + 512], w_in[:, DIFF0 + 512:DIFF0 + 1024])

                @block.scalar
                def _(s):
                    c["act"](S.activation(sg, Z(3), ACT.Sigmoid))
                    act_root(s, ms, DA)

                @block.vector
                def _(v):
                    dv = c["dve"]
                    head_rms(v, dv, oa, sq, ms, 20, DA)
                    dv(V.tensor_tensor(sg, sg, Z(3), mult))
                    dv(V.tensor_tensor(oa, oa, sg, mult))
                    dve_part(v)

                @block.tensor
                def _(pe):
                    pe_part(pe)

            token_major(DIFF0, 3)
            zq, zk, zv = Z(0), Z(1), Z(2)
            qkT2 = at(arena, 10240, 8, T)
            biasT = at(arena, 14912, HB, SEQ)
            with nc.Block() as block:
                sq = at(arena, 7680, 5, 512)
                ms = [small[:, 160:200], small[:, 200:240]]
                pe_part, dve_part = heads_to_columns(None, [zq, zk], qkT2)

                @block.vector
                def _(v):
                    dv = c["dve"]
                    dv(V.tensor_scalar(BR("qn"), BR("qn"), DB ** -0.5, None, mult))
                    for n, (z, g) in enumerate(((zq, "qn"), (zk, "kn"))):
                        head_rms(v, dv, z, sq, ms[n], 40, DB)
                        zg = z.rearrange("p m (g d) -> p (m g) d", d=DB)
                        dv(V.tensor_tensor(zg, zg, bc(BR(g), [P, 40, DB], 1), mult))
                    V.sem_inc(dve_for_sp, 1)
                    dve_part(v)

                @block.scalar
                def _(s):
                    for n in range(2):
                        act_root(s, ms[n], DB)

                @block.tensor
                def _(pe):
                    pe_part(pe)

                @block.sync
                def _(sp):
                    sp.dma_start(biasT, bass.AP(tensor=skew.tensor, offset=P - 1,
                                                ap=[[TOE - 1, P], [P * TOE, HB], [1, SEQ]])).then_inc(loaded, 16)
                    sp.wait_ge(loaded, c["loaded"].next(16))
                    sp.wait_ge(dve_for_sp, c["sp_from_dve"].next())
                    for z, op, os in ((zk, k_p, k_s), (zv, v_p, v_s)):
                        sp.dma_start(Lo(op).rearrange("o (m p) h d -> p (o m) (h d)", p=P), z[:, 0:MT, :]).then_inc(stored, 16)
                        sp.dma_start(Lo(os).rearrange("b o h d -> b (o h d)"), z[0:DEC, MT, :]).then_inc(stored, 16)
                    sp.wait_ge(stored, c["stored"].next(64))

            ob = at(arena, 0, 5, 512)
            with nc.Block() as block:
                s_ = at(arena, 16960, 2, 2, SEQ)
                p_ = at(arena, 7680, 2, 2, SEQ)
                aw = [at(arena, 9728, SEQ), at(arena, 19008, SEQ)]
                aT = [at(arena, 14400, MT, P), at(arena, 19520, MT, P)]
                units = [(h, qb) for h in range(HB) for qb in range(MT)]
                NU = len(units)

                def st8(n):
                    return small[:, 160 + n % 2 * 8:168 + n % 2 * 8]

                @block.vector
                def _(v):
                    dv = c["dve"]
                    for n in range(NU + 1):
                        if n < NU:
                            h, qb = units[n]
                            kw = (qb + 1) * P
                            sn, t8 = s_[:, n % 2], st8(n)
                            v.wait_ge(scores_ready, n + 1)
                            if n >= 2:
                                v.wait_ge(exp_ready, n - 1)
                            for cc in range(2):
                                V.tensor_tensor(sn[:, cc, 0:kw], pb[2 * (n % 2) + cc][:, 0:kw], biasT[:, h, SEQ - kw:SEQ],
                                                add).then_inc(scores_read, 1)
                            v.wait_ge(scores_read, 2 * (n + 1))
                            dv(V.tensor_reduce(t8[:, 0:2], sn[:, :, 0:kw], AX.X, amax))
                            V.tensor_scalar(t8[:, 2:4], t8[:, 0:2], -1.0, None, mult).then_inc(logits_ready, 1)
                        if n:
                            h, qb = units[n - 1]
                            kw = (qb + 1) * P
                            pn, t8 = p_[:, (n - 1) % 2], st8(n - 1)
                            v.wait_ge(exp_ready, n)
                            dv(V.reciprocal(t8[:, 6:8], t8[:, 4:6]))
                            dv(V.tensor_tensor(t8[:, 7:8], t8[:, 7:8], lam, mult))
                            dv(V.tensor_scalar(pn[:, 1, 0:kw], pn[:, 1, 0:kw], t8[:, 7:8], None, mult))
                            if n >= 3:
                                v.wait_ge(turned, n - 2)
                            V.scalar_tensor_tensor(aw[(n - 1) % 2][:, 0:kw], pn[:, 0, 0:kw], t8[:, 6:7], pn[:, 1, 0:kw],
                                                   mult, sub).then_inc(weights_ready, 1)
                            v.wait_ge(weights_ready, n)

                @block.scalar
                def _(s):
                    for n in range(NU + 2):
                        if n < NU:
                            kw = (units[n][1] + 1) * P
                            s.wait_ge(logits_ready, n + 1)
                            if n >= 2:
                                s.wait_ge(weights_ready, n - 1)
                            for cc in range(2):
                                t = S.activation(p_[:, n % 2, cc, 0:kw], s_[:, n % 2, cc, 0:kw], ACT.Exp,
                                                 bias=st8(n)[:, 2 + cc:3 + cc], accum_out=st8(n)[:, 4 + cc:5 + cc])
                            t.then_inc(exp_ready, 1)
                        if 1 <= n <= NU:
                            qb = units[n - 1][1]
                            s.wait_ge(turned, n)
                            if n >= 3:
                                s.wait_ge(values_ready, n - 2)
                            S.activation(aT[(n - 1) % 2][:, 0:qb + 1, :], at(pb[4 + (n - 1) % 2], 0, MT, P)[:, 0:qb + 1, :],
                                         ACT.Copy).then_inc(turned_read, 1)
                        if n >= 2:
                            h, qb = units[n - 2]
                            s.wait_ge(values_ready, n - 1)
                            S.activation(ob[:, qb, h * P:(h + 1) * P], pb[6 + n % 2][:, 0:P], ACT.Copy)\
                             .then_inc(values_read, 1)

                @block.tensor
                def _(pe):
                    for n in range(NU + 2):
                        if n < NU:
                            h, qb = units[n]
                            kw = (qb + 1) * P
                            if n >= 2:
                                pe.wait_ge(scores_read, 2 * (n - 1))
                            for cc in range(2):
                                r = slice(cc * DB, (cc + 1) * DB)
                                t = mm(pb[2 * (n % 2) + cc][:, 0:kw], qkT2[r, h, qb * P:(qb + 1) * P], qkT2[r, 4 + h, 0:kw])
                            t.then_inc(scores_ready, 1)
                        if 1 <= n <= NU:
                            qb = units[n - 1][1]
                            pe.wait_ge(weights_ready, n)
                            if n >= 3:
                                pe.wait_ge(turned_read, n - 2)
                            for kb in range(qb + 1):
                                t = tr(pb[4 + (n - 1) % 2][:, kb * P:(kb + 1) * P], aw[(n - 1) % 2][:, kb * P:(kb + 1) * P])
                            t.then_inc(turned, 1)
                        if n >= 2:
                            h, qb = units[n - 2]
                            pe.wait_ge(turned_read, n - 1)
                            if n >= 4:
                                pe.wait_ge(values_read, n - 3)
                            for kb in range(qb + 1):
                                t = mm(pb[6 + n % 2][:, 0:P], aT[n % 2][:, kb, :], zv[:, kb, h * P:(h + 1) * P],
                                       start=(kb == 0), stop=(kb == qb))
                            t.then_inc(values_ready, 1)

            with nc.Block() as block:
                pg = [at(arena, 16384, NPG, 512), at(arena, 17408, NPG, 512)]
                prod = at(arena, 18432, NPG, 512)
                scr = at(arena, 19456, NPG, DEC, 8)
                sown = at(arena, 19584, DEC, 8)
                srow = at(arena, 19648, PAST + 1)
                comb = at(arena, 19920, HB * DEC)
                comb2 = at(arena, 19952, HB * DEC)
                ap_ = at(arena, 19984, NPG, HB * DEC)
                aown = at(arena, 20048, HB * DEC)
                odT = at(arena, 20080, HB * DEC)
                zqd = at(arena, 20112, 512)
                st4 = small[:, 160:164]
                own = arena[0:DEC, 20624:20632]

                @block.sync
                def _(sp):
                    n = 0
                    for src in (a["cache_k_diff"], a["cache_v_diff"]):
                        for b in range(DEC):
                            if n >= 2:
                                sp.wait_ge(page_free, n - 1)
                            for g in range(NPG):
                                pid = sp.value_load(pages[0:1, b * NPG + g:b * NPG + g + 1], min_val=0,
                                                    max_val=a["cache_k_diff"].shape[1] - 1)
                                sp.dma_start(pg[b % 2][:, g, :], src[bass.ds(l, 1), bass.ds(pid, 1)]
                                             .rearrange("o g p h d -> p (o g h d)")).then_inc(page_full[b % 2], 16)
                            n += 1

                @block.vector
                def _(v):
                    dv = c["dve"]
                    dv(V.tensor_copy(zqd[0:DEC, :], zq[0:DEC, MT, :]))
                    V.sem_inc(dve_for_pe, 1)
                    for b in range(DEC):
                        v.wait_ge(pe_for_dve, c["dve_from_pe"].next())
                        v.wait_ge(page_full[b % 2], 32 * (b // 2 + 1))
                        dv(V.tensor_tensor(prod, pg[b % 2], bc(pb[b % 2], [P, NPG, 512], 1), mult))
                        dv(V.tensor_reduce(scr[:, :, b, :], prod.rearrange("p g (x d) -> p g x d", d=DB), AX.X, add))
                        V.sem_inc(page_free, 1)
                        V.sem_inc(dve_for_pe, 1)
                    for g in range(NPG):
                        sg_ = scr[:, g].rearrange("p b (h c) -> p b h c", c=2)
                        dv(V.tensor_tensor(sg_, sg_, bc(biasD[:, g, :], [P, DEC, HB, 2], 1, 3), add))
                    dv(V.tensor_tensor(prod[0:DEC, 0, :], zqd[0:DEC, :], zk[0:DEC, MT, :], mult))
                    dv(V.tensor_reduce(own, prod[0:DEC, 0, :].rearrange("p (x d) -> p x d", d=DB), AX.X, add))
                    ow = own.rearrange("p (h c) -> p h c", c=2)
                    dv(V.tensor_tensor(ow, ow, bc(bias0[0:DEC], [DEC, HB, 2], 2), add))
                    dv(V.tensor_tensor(sown[0:DEC], bc(own, [DEC, DEC, 8], 1), bc(ident[0:DEC, 0:DEC], [DEC, DEC, 8], 2), mult))
                    V.sem_inc(dve_for_pe, 1)
                    v.wait_ge(pe_for_dve, c["dve_from_pe"].next())
                    dv(V.tensor_copy(srow[0:64], pb[0][0:64, 0:PAST + 1]))
                    dv(V.tensor_reduce(st4[0:64, 0:1], srow[0:64], AX.X, amax))
                    dv(V.tensor_scalar(st4[0:64, 1:2], st4[0:64, 0:1], -1.0, None, mult))
                    V.sem_inc(dve_for_act, 1)
                    v.wait_ge(act_for_dve, c["dve_from_act"].next())
                    dv(V.reciprocal(st4[0:64, 3:4], st4[0:64, 2:3]))
                    dv(V.tensor_scalar(srow[0:64], srow[0:64], st4[0:64, 3:4], None, mult))
                    dv(V.tensor_scalar(comb[0:64], C("c1")[0:64], lam[0:64], None, mult))
                    dv(V.tensor_tensor(comb[0:64], C("c0")[0:64], comb[0:64], sub))
                    dv(V.tensor_scalar(comb2[0:64], comb[0:64], srow[0:64, PAST:PAST + 1], None, mult))
                    V.sem_inc(dve_for_pe, 1)
                    v.wait_ge(pe_for_dve, c["dve_from_pe"].next())
                    dv(V.tensor_copy(ap_.rearrange("p g c -> p (g c)"), pb[1][:, 0:64]))
                    dv(V.tensor_copy(aown[0:DEC], pb[1][0:DEC, 64:96]))
                    V.sem_inc(dve_for_pe, 1)
                    for b in range(DEC):
                        v.wait_ge(pe_for_dve, c["dve_from_pe"].next())
                        V.sem_inc(page_free, 1)
                    dv(V.tensor_copy(odT, pb[2][:, 0:32]))
                    V.sem_inc(dve_for_pe, 1)
                    v.wait_ge(pe_for_dve, c["dve_from_pe"].next())
                    dv(V.tensor_copy(ob[0:DEC, MT, :], pb[3][0:DEC, :]))

                @block.scalar
                def _(s):
                    s.wait_ge(dve_for_act, c["act_from_dve"].next())
                    c["act"](S.activation(srow[0:64], srow[0:64], ACT.Exp, bias=st4[0:64, 1:2],
                                          accum_out=st4[0:64, 2:3]))
                    S.sem_inc(act_for_dve, 1)

                @block.tensor
                def _(pe):
                    pe.wait_ge(dve_for_pe, c["pe_from_dve"].next())
                    for b in range(DEC):
                        if b >= 2:
                            pe.wait_ge(dve_for_pe, c["pe_from_dve"].next())
                        mm(pb[b % 2], ident[0:DEC, b:b + 1].broadcast_to([DEC, P]), zqd[0:DEC, :]).then_inc(pe_for_dve, 1)
                    pe.wait_ge(dve_for_pe, c["pe_from_dve"].next(3))
                    for g in range(NPG):
                        tr(pb[0][0:64, g * P:(g + 1) * P], scr[:, g].rearrange("p b x -> p (b x)"))
                    mm(pb[0][0:64, PAST:PAST + 1], sown[0:DEC].rearrange("p b x -> p (b x)"),
                       ones[0:DEC, 0:1]).then_inc(pe_for_dve, 1)
                    pe.wait_ge(dve_for_pe, c["pe_from_dve"].next())
                    for g in range(NPG):
                        mm(pb[1][:, g * 32:(g + 1) * 32], srow[0:64, g * P:(g + 1) * P], comb[0:64])
                    mm(pb[1][0:DEC, 64:96], C("selb")[0:64], comb2[0:64]).then_inc(pe_for_dve, 1)
                    pe.wait_ge(dve_for_pe, c["pe_from_dve"].next())
                    for h in range(HB):
                        mm(pb[2][:, h * DEC:(h + 1) * DEC], zv[0:DEC, MT, h * P:(h + 1) * P],
                           aown[0:DEC, h * DEC:(h + 1) * DEC], start=(h == 0), stop=False)
                    for b in range(DEC):
                        pe.wait_ge(page_full[b % 2], 32 * (DEC // 2 + b // 2 + 1))
                        for h in range(HB):
                            for g in range(NPG):
                                t = mm(pb[2][:, h * DEC + b:h * DEC + b + 1], pg[b % 2][:, g, h * P:(h + 1) * P],
                                       ap_[:, g, h * DEC + b:h * DEC + b + 1], start=False, stop=(b == DEC - 1))
                        t.then_inc(pe_for_dve, 1)
                    pe.wait_ge(dve_for_pe, c["pe_from_dve"].next())
                    for h in range(HB):
                        t = tr(pb[3][0:DEC, h * P:(h + 1) * P], odT[:, h * DEC:(h + 1) * DEC])
                    t.then_inc(pe_for_dve, 1)

            with nc.Block() as block:
                sq = at(arena, 7680, 5, 512)
                ms = small[:, 160:180]
                pe_part, dve_part = heads_to_columns(None, [ob], yT[:, 4:8, :])

                @block.sync
                def _(sp):
                    prefetch(sp, w_in[:, RW0:RW0 + 512], w_in[:, RW0 + 512:RW0 + 1024])

                @block.scalar
                def _(s):
                    act_root(s, ms, DVB)

                @block.vector
                def _(v):
                    dv = c["dve"]
                    head_rms(v, dv, ob, sq, ms, 20, DVB)
                    og = ob.rearrange("p m (g d) -> p (m g) d", d=DVB)
                    dv(V.tensor_tensor(og, og, bc(BR("subln"), [P, 20, DVB], 1), mult))
                    dve_part(v)

                @block.tensor
                def _(pe):
                    pe_part(pe)

            z = at(arena, 0, RT, T)
            zs = at(arena, 7800, RT, T)
            slab = [at(arena, n * 2080, HP, T) for n in range(3)]
            z0, z1, z2 = slab
            y3 = yT[:, 8:12, :]
            r_, k_, v_ = zs[:, 0:4, :], zs[:, 4:8, :], zs[:, 8:12, :]
            wdad, gd = zs[:, 12, :], zs[:, 13:15, :]
            w_up2 = ring[1][:, 0:512]
            w_g1, w_g2 = ring[1][:, 512:1024], ring[1][0:32, 1024:1536]
            w_vu = ring[1][0:32, 1536:2048]
            w_vd = at(ring[1], 2048, HP, 32)
            with nc.Block() as block:
                @block.sync
                def _(sp):
                    for b in range(2, 4):
                        c0 = RW0 + 512 * b
                        load_w(sp, b % 2, w_in[:, c0:min(c0 + 512, GATE0)])

                @block.tensor
                def _(pe):
                    for b in range(4):
                        pe.wait_ge(slot_full[b % 2], c["pe_full"][b % 2].next(16))
                        n = 4 if b < 3 else 3
                        w = wslot(b % 2) if b < 3 else wslot(1)[:, :, 0:RW - 3 * W]
                        fm_tiles(pe, w, 0, hT, n, c["pe_from_act"], pe_for_act)
                    c["pe_from_act"].skip(4)

                @block.scalar
                def _(s):
                    S.sem_inc(act_for_pe, 4)
                    for b in range(4):
                        for ct in range(4 if b < 3 else 3):
                            mc = 32 if b == 3 and ct == 2 else P
                            s.wait_ge(pe_for_act, c["act_from_pe"].next())
                            for half in range(2):
                                c["act"](S.activation(z[0:mc, 4 * b + ct, half * TH:(half + 1) * TH],
                                                      pb[4 * half + ct][0:mc, 0:TH], ACT.Copy))
                            S.sem_inc(act_for_pe, 1)
                        S.sem_inc(slot_free[b % 2], 1)

            with nc.Block() as block:
                prev_rows = arena[0:DEC, 15600:15600 + RT * P]
                prevT = at(arena, 17520, RT, DEC)
                last_rows = arena[0:9, 17664:17664 + RT * P]

                @block.sync
                def _(sp):
                    sp.dma_start(prev_rows[:, 0:RW], L("state_shift").rearrange("b o c -> b (o c)")).then_inc(loaded, 16)
                    sp.dma_start(w_up2[0:64, :], L("w_decay_up")).then_inc(loaded, 16)
                    sp.dma_start(w_up2[64:128, :], L("w_a_up")).then_inc(loaded, 16)
                    wg = L("w_g_up")
                    sp.dma_start(w_g1, wg[0:P, :]).then_inc(loaded, 16)
                    sp.dma_start(w_g2, wg[P:160, :]).then_inc(loaded, 16)
                    sp.dma_start(w_vu, a["w_v_up"][0]).then_inc(loaded, 16)
                    sp.dma_start(w_vd, a["w_v_down"][0].rearrange("(k p) n -> p k n", p=P)).then_inc(loaded, 16)
                    sp.wait_ge(loaded, c["loaded"].base + 112)
                    sp.wait_ge(dve_for_sp, c["sp_from_dve"].next())
                    sp.dma_start(Lo(shift_p).rearrange("b o c -> b (o c)"), last_rows[0:1, 0:RW]).then_inc(stored, 16)
                    sp.dma_start(Lo(shift_s).rearrange("b o c -> b (o c)"), last_rows[1:9, 0:RW]).then_inc(stored, 16)
                    sp.wait_ge(stored, c["stored"].next(32))

                @block.tensor
                def _(pe):
                    pe.wait_ge(loaded, c["loaded"].base + 112)
                    for t in range(RT):
                        mc = P if t < 14 else 32
                        tr(pb[0][0:mc, t * DEC:(t + 1) * DEC], prev_rows[:, t * P:t * P + mc])
                    for t in range(RT):
                        mc = P if t < 14 else 32
                        i = tr(pb[1 + t // 4][0:9, (t % 4) * P:(t % 4) * P + mc], z[0:mc, t, SEQ - 1:T])
                    i.then_inc(pe_for_dve, 1)

                @block.vector
                def _(v):
                    dv = c["dve"]
                    v.wait_ge(pe_for_dve, c["dve_from_pe"].next())
                    for g in range(4):
                        w_ = 512 if g < 3 else RW - 1536
                        dv(V.tensor_copy(last_rows[:, g * 512:g * 512 + w_], pb[1 + g][0:9, 0:w_]))
                    V.sem_inc(dve_for_sp, 1)
                    dv(V.tensor_copy(prevT[:, 0:14], at(pb[0], 0, 14, DEC)))
                    dv(V.tensor_copy(prevT[0:32, 14], pb[0][0:32, 14 * DEC:15 * DEC]))
                    for lo, hi, mc in ((0, 14, P), (14, 15, 32)):
                        dv(V.tensor_tensor(zs[0:mc, lo:hi, 1:SEQ], z[0:mc, lo:hi, 0:SEQ - 1], z[0:mc, lo:hi, 1:SEQ], sub))
                        dv(V.tensor_scalar(zs[0:mc, lo:hi, 0:1], z[0:mc, lo:hi, 0:1], -1.0, None, mult))
                        dv(V.tensor_tensor(zs[0:mc, lo:hi, SEQ:T], prevT[0:mc, lo:hi], z[0:mc, lo:hi, SEQ:T], sub))
                    for t in range(RT):
                        mc = P if t < 14 else 32
                        dv(V.scalar_tensor_tensor(zs[0:mc, t, :], zs[0:mc, t, :], PR("mu")[0:mc, t:t + 1], z[0:mc, t, :], mult, add))
            c["loaded"].skip(112)

            dvec = at(arena, 6760, 5, HP, DEC)
            tokv = at(arena, 18160, 5, 512)
            bonus = at(small, 200, 5, HC)
            dend = at(small, 256, HP, 8)
            yd = at(small, 288, HP, DEC)
            vdn = at(arena, 6240, T)
            with nc.Block() as block:
                def up(pe, lhs, rows_, rhs):
                    for ct in range(HP):
                        for half in range(2):
                            t = mm(pb[4 * half + ct][:, 0:TH], lhs[rows_, ct * P:(ct + 1) * P],
                                   rhs[rows_, half * TH:(half + 1) * TH])
                    return t

                @block.tensor
                def _(pe):
                    pe.wait_ge(act_for_pe, c["pe_from_act"].next())
                    up(pe, w_up2, slice(0, 64), wdad).then_inc(pe_for_act, 1)
                    pe.wait_ge(act_for_pe, c["pe_from_act"].next())
                    up(pe, w_up2, slice(64, 128), wdad).then_inc(pe_for_act, 1)
                    pe.wait_ge(act_for_pe, c["pe_from_act"].next())
                    for k in range(HP):
                        for half in range(2):
                            t = mm(pb[half][0:32, 0:TH], w_vd[:, k, :], v_[:, k, half * TH:(half + 1) * TH],
                                   start=(k == 0), stop=(k == HP - 1))
                    t.then_inc(pe_for_act, 1)
                    pe.wait_ge(act_for_pe, c["pe_from_act"].next())
                    up(pe, w_vu, slice(0, 32), vdn).then_inc(pe_for_act, 1)
                    pe.wait_ge(dve_for_pe, c["pe_from_dve"].next())
                    for ct in range(HP):
                        for half in range(2):
                            t = mm(pb[4 * half + ct][:, 0:TH], blk, y3[:, ct, half * TH:(half + 1) * TH])
                    t.then_inc(pe_for_act, 1)
                    pe.wait_ge(dve_for_pe, c["pe_from_dve"].next())
                    for m in range(5):
                        r = P if m < MT else DEC
                        for hp in range(HP):
                            t = mm(pb[5][0:r, m * 8 + hp * 2:m * 8 + hp * 2 + 2], y3[:, hp, m * P:m * P + r], C("pair"))
                    t.then_inc(pe_for_dve, 1)
                    pe.wait_ge(dve_for_pe, c["pe_from_dve"].next())
                    for n in range(5):
                        for hp in range(HP):
                            t = tr(pb[n][0:DEC, hp * P:(hp + 1) * P], dvec[:, n, hp, :])
                    t.then_inc(pe_for_dve, 1)

                @block.scalar
                def _(s):
                    ac = c["act"]
                    ac(S.activation(wdad[0:64], wdad[0:64], ACT.Tanh))
                    S.sem_inc(act_for_pe, 1)
                    ac(S.activation(gd[:, 0], gd[:, 0], ACT.Sigmoid))
                    ac(S.activation(gd[0:32, 1], gd[0:32, 1], ACT.Sigmoid))

                    def bias_sigmoid(dst, name):
                        s.wait_ge(pe_for_act, c["act_from_pe"].next())
                        for ct in range(HP):
                            b_ = PR(name)[:, ct:ct + 1]
                            for half in range(2):
                                ac(S.activation(dst[:, ct, half * TH:(half + 1) * TH], pb[4 * half + ct][:, 0:TH],
                                                ACT.Sigmoid, bias=b_))

                    bias_sigmoid(z0, "w0")
                    S.sem_inc(act_for_pe, 1)
                    bias_sigmoid(z1, "a0")
                    S.sem_inc(act_for_pe, 1)
                    s.wait_ge(pe_for_act, c["act_from_pe"].next())
                    for half in range(2):
                        ac(S.activation(vdn[0:32, half * TH:(half + 1) * TH], pb[half][0:32, 0:TH], ACT.Copy))
                    S.sem_inc(act_for_pe, 1)
                    bias_sigmoid(z2, "v0")
                    S.sem_inc(act_for_dve, 1)
                    s.wait_ge(pe_for_act, c["act_from_pe"].next())
                    for ct in range(HP):
                        for half in range(2):
                            ac(S.activation(y3[:, ct, half * TH:(half + 1) * TH], pb[4 * half + ct][:, 0:TH], ACT.Sqrt))
                    S.sem_inc(act_for_dve, 1)
                    s.wait_ge(dve_for_act, c["act_from_dve"].next())
                    ac(S.activation(dvec[:, 0], z0[:, :, SEQ:T], ACT.Exp))
                    S.sem_inc(act_for_dve, 1)
                    s.wait_ge(dve_for_act, c["act_from_dve"].next())
                    ac(S.activation(z0, z0, ACT.Exp))
                    S.sem_inc(act_for_dve, 1)
                    s.wait_ge(dve_for_act, c["act_from_dve"].next())
                    ac(S.activation(z0, y3, ACT.Exp, scale=-1.0))
                    ac(S.activation(y3, y3, ACT.Exp))
                    S.sem_inc(act_for_dve, 1)

                @block.vector
                def _(v):
                    dv = c["dve"]
                    vm = C("vmix", DEPTH)[:, bass.ds(l, 1)]
                    v.wait_ge(act_for_dve, c["dve_from_act"].next())
                    dv(V.tensor_scalar(z0, z0, -math.exp(-0.5), None, mult))
                    dv(V.tensor_scalar(z2, z2, vm, None, mult))
                    dv(V.tensor_tensor(y3, vfirst, v_, sub))
                    dv(V.scalar_tensor_tensor(vfirst, y3, vm, v_, mult, add))
                    dv(V.tensor_tensor(y3, y3, z2, mult))
                    dv(V.tensor_tensor(v_, v_, y3, add))
                    for ct in range(HP):
                        dv(V.tensor_scalar(z2[:, ct], k_[:, ct], PR("k_k")[:, ct:ct + 1], None, mult))
                    dv(V.tensor_tensor(y3, z2, z2, mult))
                    V.sem_inc(dve_for_pe, 1)
                    v.wait_ge(act_for_dve, c["dve_from_act"].next())
                    dv(V.tensor_scalar(y3, y3, 1e-12, None, amax))
                    dv(V.reciprocal(y3, y3))
                    dv(V.tensor_tensor(z2, z2, y3, mult))
                    for ct in range(HP):
                        ka = PR("k_a")[:, ct:ct + 1]
                        dv(V.tensor_scalar(y3[:, ct], z1[:, ct], ka, ka, mult, sub))
                    dv(V.scalar_tensor_tensor(k_, y3, 1.0, k_, add, mult))
                    dv(V.tensor_tensor(z1, z1, z2, mult))
                    for ct in range(HP):
                        dv(V.scalar_tensor_tensor(y3[:, ct], r_[:, ct], PR("r_k")[:, ct:ct + 1], k_[:, ct], mult, mult))
                    V.sem_inc(dve_for_pe, 1)
                    v.wait_ge(pe_for_dve, c["dve_from_pe"].next())
                    dv(V.tensor_copy(bonus[:, 0:MT], at(pb[5], 0, MT, HC)))
                    dv(V.tensor_copy(bonus[0:DEC, MT], pb[5][0:DEC, MT * 8:MT * 8 + 8]))
                    V.sem_inc(dve_for_act, 1)
                    dv(V.tensor_copy(dvec[:, 1], k_[:, :, SEQ:T]))
                    dv(V.tensor_scalar(dvec[:, 2], z2[:, :, SEQ:T], -1.0, None, mult))
                    dv(V.tensor_copy(dvec[:, 3], z1[:, :, SEQ:T]))
                    dv(V.tensor_copy(dvec[:, 4], r_[:, :, SEQ:T]))
                    v.wait_ge(act_for_dve, c["dve_from_act"].next())
                    V.sem_inc(dve_for_pe, 1)
                    for ct in range(HP):
                        dv(V.tensor_tensor_scan(y3[:, ct], C("scan"), z0[:, ct], 0.0, mult, add))
                    dv(V.tensor_tensor(z0, y3, z0, sub))
                    V.sem_inc(dve_for_act, 1)
                    v.wait_ge(act_for_dve, c["dve_from_act"].next())
                    dv(V.scalar_tensor_tensor(z2, z2, -1.0, z0, mult, mult))
                    V.sem_inc(dve_for_act, 1)
                    v.wait_ge(act_for_dve, c["dve_from_act"].next())
                    dv(V.tensor_tensor(z1, z1, z0, mult))
                    dv(V.tensor_tensor(k_, k_, z0, mult))
                    dv(V.tensor_tensor(r_, r_, y3, mult))
                    dv(V.tensor_copy(dend, y3[:, :, CH - 1:SEQ:CH]))
                    v.wait_ge(pe_for_dve, c["dve_from_pe"].next())
                    for n in range(5):
                        dv(V.tensor_copy(tokv[0:DEC, n], pb[n][0:DEC, :]))

            ytok = at(arena, 18160, 5, 512)
            with nc.Block() as block:
                ds_ = at(arena, 15600, DEC, HP, DC)
                t1 = at(arena, 17648, 2, HP, DC)
                u = at(small, 320, 2, HP)

                @block.sync
                def _(sp):
                    sr = L("state_rwkv").rearrange("b (q g) i j -> g i b q j", g=2)
                    so = Lo(rwkv_s).rearrange("b (q g) i j -> g i b q j", g=2)
                    for g in range(2):
                        for b in range(DEC):
                            sp.dma_start(ds_[g * 64:(g + 1) * 64, b], sr[g, :, b]).then_inc(loaded, 16)
                    sp.wait_ge(dve_for_sp, c["sp_from_dve"].next())
                    for g in range(2):
                        for b in range(DEC):
                            sp.dma_start(so[g, :, b], ds_[g * 64:(g + 1) * 64, b]).then_inc(stored, 16)
                    sp.wait_ge(stored, c["stored"].next(256))

                @block.tensor
                def _(pe):
                    for q in range(4):
                        if q:
                            pe.wait_ge(dve_for_pe, c["pe_from_dve"].next())
                        for n in range(5):
                            x = tokv[0:DEC, n, :].rearrange("b (q g j) -> b g q j", g=2, j=DC)
                            for b2 in range(2):
                                for g in range(2):
                                    b = 2 * q + b2
                                    t = mm(pb[n][g * 64:(g + 1) * 64, b2 * 256:(b2 + 1) * 256],
                                           ident[0:DEC, b:b + 1].broadcast_to([DEC, 64]), x[:, g])
                        t.then_inc(pe_for_dve, 1)
                    pe.wait_ge(dve_for_pe, c["pe_from_dve"].next())
                    for hp in range(HP):
                        t = tr(pb[5][0:DEC, hp * P:(hp + 1) * P], yd[:, hp, :])
                    t.then_inc(pe_for_dve, 1)

                @block.vector
                def _(v):
                    dv = c["dve"]
                    v.wait_ge(loaded, c["loaded"].base + 256)
                    for q in range(4):
                        s2 = ds_[:, 2 * q:2 * q + 2]
                        sf, tf = s2.rearrange("p b q j -> p (b q) j"), t1.rearrange("p b q j -> p (b q) j")
                        w3, k3, a3, b3, r3 = (at(pb[n], 0, 8, DC) for n in range(5))
                        uf = u.rearrange("p b q -> p (b q)")
                        v.wait_ge(pe_for_dve, c["dve_from_pe"].next())
                        dv(V.tensor_tensor(tf, sf, a3, mult))
                        dv(V.tensor_reduce(uf, tf, AX.X, add))
                        dv(V.tensor_tensor(sf, sf, w3, mult))
                        dv(V.tensor_tensor(tf, b3, bc(uf, [P, 8, DC], 2), mult))
                        dv(V.tensor_tensor(sf, sf, tf, add))
                        vv = v_[:, :, SEQ + 2 * q:SEQ + 2 * q + 2].rearrange("p q b -> p b q")
                        dv(V.tensor_tensor(t1, at(pb[1], 0, 2, HP, DC), bc(vv, [P, 2, HP, DC], 3), mult))
                        dv(V.tensor_tensor(sf, sf, tf, add))
                        dv(V.tensor_tensor(tf, sf, r3, mult))
                        dv(V.tensor_reduce(yd[:, :, 2 * q:2 * q + 2].rearrange("p q b -> p b q"), t1, AX.X, add))
                        V.sem_inc(dve_for_pe, 1)
                    V.sem_inc(dve_for_sp, 1)
                    v.wait_ge(pe_for_dve, c["dve_from_pe"].next())
                    dv(V.tensor_copy(ytok[0:DEC, MT], pb[5][0:DEC, :]))
            c["loaded"].skip(256)

            vtok = at(arena, 15600, 5, 512)
            btok = at(arena, 0, MT, 512)
            ktok = at(arena, 11960, MT, 512)
            with nc.Block() as block:
                @block.tensor
                def _(pe):
                    for n, src in enumerate((v_, z1, k_)):
                        if n:
                            pe.wait_ge(dve_for_pe, c["pe_from_dve"].next())
                        for m in range(MT):
                            for hp in range(HP):
                                t = tr(pb[m][:, hp * P:(hp + 1) * P], src[:, hp, m * P:(m + 1) * P])
                        if n == 0:
                            for hp in range(HP):
                                t = tr(pb[4][0:DEC, hp * P:(hp + 1) * P], src[:, hp, SEQ:T])
                        t.then_inc(pe_for_dve, 1)

                @block.vector
                def _(v):
                    dv = c["dve"]
                    for n, dst in enumerate((vtok, btok, ktok)):
                        v.wait_ge(pe_for_dve, c["dve_from_pe"].next())
                        for m in range(MT):
                            dv(V.tensor_copy(dst[:, m], pb[m]))
                        if n == 0:
                            dv(V.tensor_copy(dst[0:DEC, MT], pb[4][0:DEC, :]))
                        V.sem_inc(dve_for_pe, 1)
            c["pe_from_dve"].skip(1)

            m_ba, m_br, m_ka, m_kr = (at(ring[0], n * 1024, 2, HP, P) for n in range(4))
            xt = at(arena, 6240, 2, HP, P)
            xm = at(y_raw, 8 * T, 2, HP, P)
            m1 = at(y_raw, 8 * T + 1024, 2, HP, P)
            rhs1 = ring[1][:, 3200:3712]
            uu = arena[:, 7264:7776]
            stb = at(arena, 14040, HP, P)
            with nc.Block() as block:
                @block.vector
                def _(v):
                    c["dve"](V.memset(stb, 0.0))
            keep = C("keep", 2, P)
            level = C("level", 6, P)
            with nc.Block() as block:
                @block.tensor
                def _(pe):
                    turn = c["pe_from_dve"]
                    for m in range(MT):
                        tok = slice(m * P, (m + 1) * P)
                        if m:
                            pe.wait_ge(dve_for_pe, turn.next())
                        if m:
                            pe.wait_ge(act_for_pe, c["pe_from_act"].next())
                        for n, (left, right) in enumerate(((z1, z2), (z1, r_), (k_, z2), (k_, r_))):
                            for g in range(2):
                                gs = slice(g * 64, (g + 1) * 64)
                                for hp in range(HP):
                                    t = mm(pb[2 * n + g][:, hp * P:(hp + 1) * P], left[gs, hp, tok], right[gs, hp, tok])
                        t.then_inc(pe_for_dve, 1)
                        for lv in range(6):
                            for g in range(2):
                                pe.wait_ge(dve_for_pe, turn.next())
                                for hp in range(HP):
                                    t = mm(pb[g][:, hp * P:(hp + 1) * P], m_ba[:, g, hp, :],
                                           ident if lv == 0 else xm[:, g, hp, :])
                                t.then_inc(pe_for_dve, 1)
                            for g in range(2):
                                pe.wait_ge(dve_for_pe, turn.next())
                                for hp in range(HP):
                                    hs = slice(hp * P, (hp + 1) * P)
                                    t = mm(pb[4 + g][:, hs], m1[:, g, hp, :], ident if lv == 0 else xt[:, g, hp, :])
                                    if 0 < lv < 5:
                                        t = mm(pb[2 + g][:, hs], xt[:, g, hp, :], m1[:, g, hp, :])
                                t.then_inc(pe_for_dve, 1)
                        for cc in range(2):
                            r = slice(cc * 64, (cc + 1) * 64)
                            tk = slice(m * P + cc * 64, m * P + (cc + 1) * 64)
                            hsl = [slice(h * 64, (h + 1) * 64) for h in range(HC)]
                            pe.wait_ge(dve_for_pe, turn.next())
                            for hp in range(HP):
                                mm(pb[0][r, hp * P:(hp + 1) * P], z2[:, hp, tk], stb[:, hp, :], start=(hp == 0), stop=False)
                            for h in range(HC):
                                t = mm(pb[0][r, hsl[h]], m_ka[r, h % 2, h // 2, r], vtok[r, m, hsl[h]], start=False)
                            t.then_inc(pe_for_dve, 1)
                            pe.wait_ge(dve_for_pe, turn.next())
                            for h in range(HC):
                                t = mm(pb[1][r, hsl[h]], xt[r, h % 2, h // 2, r], rhs1[r, hsl[h]])
                            t.then_inc(pe_for_dve, 1)
                            pe.wait_ge(dve_for_pe, turn.next())
                            for hp in range(HP):
                                hs = slice(hp * P, (hp + 1) * P)
                                mm(pb[3][:, hs], btok[r, m, hs], uu[r, hs], stop=False)
                                t = mm(pb[3][:, hs], ktok[r, m, hs], vtok[r, m, hs], start=False)
                            if cc:
                                pe.wait_ge(act_for_pe, c["pe_from_act"].next())
                            for hp in range(HP):
                                t = mm(pb[2][r, hp * P:(hp + 1) * P], r_[:, hp, tk], stb[:, hp, :], start=(hp == 0), stop=False)
                            t.then_inc(pe_for_dve, 1)
                            for h in range(HC):
                                mm(pb[2][r, hsl[h]], m_br[r, h % 2, h // 2, r], uu[r, hsl[h]], start=False, stop=False)
                                t = mm(pb[2][r, hsl[h]], m_kr[r, h % 2, h // 2, r], vtok[r, m, hsl[h]], start=False)
                            t.then_inc(pe_for_act, 1)
                    pe.wait_ge(dve_for_pe, turn.next())
                    for hp in range(HP):
                        t = tr(pb[0][:, hp * P:(hp + 1) * P], stb[:, hp, :])
                    t.then_inc(pe_for_dve, 1)
                    c["pe_from_act"].skip(1)

                @block.vector
                def _(v):
                    dv = c["dve"]
                    done = c["dve_from_pe"]
                    for m in range(MT):
                        v.wait_ge(pe_for_dve, done.next())
                        for n, (dst, kp) in enumerate(((m_ba, 0), (m_br, 1), (m_ka, 0), (m_kr, 1))):
                            for g in range(2):
                                dv(V.tensor_tensor(dst[:, g], at(pb[2 * n + g], 0, HP, P), bc(keep[:, kp], [P, HP, P], 1), mult))
                        V.sem_inc(dve_for_pe, 2)
                        for lv in range(6):
                            for g in range(2):
                                v.wait_ge(pe_for_dve, done.next())
                                dv(V.tensor_tensor(m1[:, g], at(pb[g], 0, HP, P), bc(level[:, lv], [P, HP, P], 1), mult))
                                V.sem_inc(dve_for_pe, 1)
                            for g in range(2):
                                v.wait_ge(pe_for_dve, done.next())
                                if lv == 0:
                                    V.tensor_tensor(xm[:, g], m1[:, g], bc(ident, [P, HP, P], 1), add)
                                elif lv < 5:
                                    V.tensor_tensor(xm[:, g], xm[:, g], at(pb[2 + g], 0, HP, P), add)
                                dv(V.tensor_tensor(xt[:, g], bc(ident, [P, HP, P], 1) if lv == 0 else xt[:, g],
                                                   at(pb[4 + g], 0, HP, P), add))
                                if lv < 5:
                                    V.sem_inc(dve_for_pe, 1)
                        for cc in range(2):
                            r = slice(cc * 64, (cc + 1) * 64)
                            V.sem_inc(dve_for_pe, 1)
                            v.wait_ge(pe_for_dve, done.next())
                            dv(V.tensor_copy(rhs1[r], pb[0][r]))
                            V.sem_inc(dve_for_pe, 1)
                            v.wait_ge(pe_for_dve, done.next())
                            dv(V.tensor_copy(uu[r], pb[1][r]))
                            V.sem_inc(dve_for_pe, 1)
                            v.wait_ge(pe_for_dve, done.next())
                            upd = at(m1.rearrange("p g q t -> p (g q t)"), 0, HP, P)
                            dv(V.tensor_tensor(upd, at(pb[3], 0, HP, P), bc(blk, [P, HP, P], 1), mult))
                            dv(V.tensor_tensor(stb, stb, upd, add))
                            dv(V.tensor_tensor(stb, stb, bc(dend[:, :, 2 * m + cc], [P, HP, P], 2), mult))
                        V.sem_inc(dve_for_pe, 1)
                    v.wait_ge(pe_for_dve, done.next())
                    dv(V.tensor_copy(uu, pb[0]))
                    V.sem_inc(dve_for_sp, 1)

                @block.scalar
                def _(s):
                    for n in range(2 * MT):
                        r = slice(n % 2 * 64, (n % 2 + 1) * 64)
                        s.wait_ge(pe_for_act, c["act_from_pe"].next())
                        c["act"](S.activation(ytok[r, n // 2], pb[2][r], ACT.Copy))
                        S.sem_inc(act_for_pe, 1)

                @block.sync
                def _(sp):
                    sp.wait_ge(dve_for_sp, c["sp_from_dve"].next())
                    o = Lo(rwkv_p).rearrange("o (q g) i j -> g i (o q) j", g=2)
                    for g in range(2):
                        sp.dma_start(o[g], at(arena, 7264, HP, P)[g * 64:(g + 1) * 64, :, g * 64:(g + 1) * 64]).then_inc(stored, 16)
                    sp.wait_ge(stored, c["stored"].next(32))

            with nc.Block() as block:
                sq = at(arena, 0, 5, 512)
                ms = small[:, 160:200]
                mu_ = small[:, 330:370]
                pe_part, dve_part = heads_to_columns(None, [ytok], yT[:, 8:12, :])

                @block.sync
                def _(sp):
                    load_w(sp, 0, w_in[:, GATE0:GATE0 + 512])
                    load_w(sp, 2, L("w_up_a")[:, 0:512], k=4)

                @block.scalar
                def _(s):
                    s.wait_ge(dve_for_act, c["act_from_dve"].next())
                    c["act"](S.activation(ms, ms, ACT.Sqrt, bias=eps_ln, scale=1.0 / DC))
                    S.sem_inc(act_for_dve, 1)

                @block.tensor
                def _(pe):
                    for m in range(5):
                        r = P if m < MT else DEC
                        mm(pb[m][0:r], gd[:, 0, m * P:m * P + r], w_g1, stop=False)
                        t = mm(pb[m][0:r], gd[0:32, 1, m * P:m * P + r], w_g2, start=False)
                    t.then_inc(pe_for_dve, 1)
                    pe_part(pe)

                @block.vector
                def _(v):
                    dv = c["dve"]
                    yg = ytok.rearrange("p m (g d) -> p (m g) d", d=DC)
                    vg = vtok.rearrange("p m (g d) -> p (m g) d", d=DC)
                    sg_ = sq.rearrange("p m (g d) -> p (m g) d", d=DC)
                    dv(V.tensor_reduce(mu_, yg, AX.X, add))
                    dv(V.tensor_scalar(mu_, mu_, 1.0 / DC, None, mult))
                    dv(V.tensor_tensor(yg, yg, bc(mu_, [P, 40, DC], 2), sub))
                    dv(V.tensor_tensor(sq, ytok, ytok, mult))
                    dv(V.tensor_reduce(ms, sg_, AX.X, add))
                    V.sem_inc(dve_for_act, 1)
                    v.wait_ge(act_for_dve, c["dve_from_act"].next())
                    dv(V.reciprocal(ms, ms))
                    dv(V.tensor_tensor(yg, yg, bc(ms, [P, 40, DC], 2), mult))
                    dv(V.tensor_tensor(ytok, ytok, bc(BR("lnx_g"), [P, 5, 512], 1), mult))
                    dv(V.tensor_tensor(ytok, ytok, bc(BR("lnx_b"), [P, 5, 512], 1), add))
                    dv(V.tensor_tensor(sg_, vg, bc(bonus.rearrange("p m h -> p (m h)"), [P, 40, DC], 2), mult))
                    dv(V.tensor_tensor(ytok, ytok, sq, add))
                    v.wait_ge(pe_for_dve, c["dve_from_pe"].next())
                    for m in range(5):
                        r = P if m < MT else DEC
                        dv(V.tensor_tensor(ytok[0:r, m], ytok[0:r, m], pb[m][0:r], mult))
                    dve_part(v)

            merged = at(arena, 0, KD, T)
            with nc.Block() as block:
                sgb = at(arena, 4160, 2, T)
                tmp = at(arena, 5200, 2, T)

                @block.sync
                def _(sp):
                    names = ("w_up_a", "w_up_b", "w_up_c")
                    for q in range(1, 6):
                        og, n = q // 3, q % 3
                        g0 = GATE0 + n * D + og * 512
                        load_w(sp, q % 2, w_in[:, g0:g0 + 512])
                        load_w(sp, 2 + q % 2, L(names[n])[:, og * 512:(og + 1) * 512], k=4)
                    prefetch(sp, L("w_out")[:, 0:512], L("w_out")[:, 512:1024])

                @block.tensor
                def _(pe):
                    for q in range(6):
                        n, s = q % 3, q % 2
                        pe.wait_ge(slot_full[s], c["pe_full"][s].next(16))
                        pe.wait_ge(slot_full[2 + s], c["pe_full"][2 + s].next(16))
                        wg, wu = wslot(s), wslot(2 + s, 4)
                        for ct in range(4):
                            b = ct % 2
                            cs = slice(ct * P, (ct + 1) * P)
                            pe.wait_ge(dve_for_pe, c["pe_from_dve"].next())
                            for k in range(KD):
                                for half in range(2):
                                    mm(pb[b + 4 * half][:, 0:TH], wg[:, k, cs], hT[:, k, half * TH:(half + 1) * TH],
                                       start=(k == 0), stop=(k == KD - 1))
                            for k in range(4):
                                for half in range(2):
                                    t = mm(pb[2 + b + 4 * half][:, 0:TH], wu[:, k, cs],
                                           yT[:, 4 * n + k, half * TH:(half + 1) * TH], start=(k == 0), stop=(k == 3))
                            t.then_inc(pe_for_act, 1)
                    c["pe_from_dve"].skip(2)

                @block.scalar
                def _(s):
                    with s.Fori(0, 12) as i:
                        c["act_from_pe"].enter(i, 2)
                        c["act"].enter(i, 4)
                        for b in range(2):
                            s.wait_ge(pe_for_act, c["act_from_pe"].next())
                            for half in range(2):
                                c["act"](S.activation(sgb[:, b, half * TH:(half + 1) * TH], pb[b + 4 * half][:, 0:TH],
                                                      ACT.Sigmoid))
                            S.sem_inc(act_for_dve, 1)
                    c["act_from_pe"].leave(12)
                    c["act"].leave(12)

                @block.vector
                def _(v):
                    dv = c["dve"]
                    V.sem_inc(dve_for_pe, 2)
                    for q in range(6):
                        og, n = q // 3, q % 3
                        for ct in range(4):
                            b = ct % 2
                            mg = merged[:, og * 4 + ct, :]
                            dst = mg if n == 0 else tmp[:, b]
                            v.wait_ge(act_for_dve, c["dve_from_act"].next())
                            for half in range(2):
                                hs = slice(half * TH, (half + 1) * TH)
                                dv(V.tensor_tensor(dst[:, hs], sgb[:, b, hs], pb[2 + b + 4 * half][:, 0:TH], mult))
                            V.sem_inc(dve_for_pe, 1)
                            if ct == 3:
                                V.sem_inc(slot_free[q % 2], 1)
                                V.sem_inc(slot_free[2 + q % 2], 1)
                            if n:
                                dv(V.tensor_tensor(mg, mg, tmp[:, b], add))

            def residual(v, dv, kt, bank, gate0, tmp8):
                g = modT[:, gate0 + kt, 0:1]
                dv(V.scalar_tensor_tensor(xT[:, kt, 0:TH], pb[bank][:, 0:TH], g, xT[:, kt, 0:TH], mult, add))
                dv(V.scalar_tensor_tensor(xT[:, kt, TH:SEQ], pb[4 + bank][:, 0:SEQ - TH], g, xT[:, kt, TH:SEQ], mult, add))
                dv(V.tensor_tensor(tmp8, pb[4 + bank][:, SEQ - TH:TH], modT[:, gate0 + kt, 1:9], mult))
                V.sem_inc(dve_for_pe, 1)
                dv(V.tensor_tensor(xT[:, kt, SEQ:T], xT[:, kt, SEQ:T], tmp8, add))

            tmp8 = small[:, 400:408]
            with nc.Block() as block:
                @block.sync
                def _(sp):
                    w1 = L("w_ff1")
                    prefetch(sp, w1[:, 0:512], w1[:, 512:1024])

                @block.tensor
                def _(pe):
                    for b in range(2):
                        pe.wait_ge(slot_full[b], c["pe_full"][b].next(16))
                        fm_tiles(pe, wslot(b), 0, merged, 4, c["pe_from_dve"], pe_for_dve)
                    c["pe_from_dve"].skip(4)

                @block.vector
                def _(v):
                    V.sem_inc(dve_for_pe, 4)
                    for b in range(2):
                        for ct in range(4):
                            v.wait_ge(pe_for_dve, c["dve_from_pe"].next())
                            residual(v, c["dve"], 4 * b + ct, ct, 16, tmp8)
                        V.sem_inc(slot_free[b], 1)

            norm_stage("norm2", 24, 32)

            ff = at(arena, 0, KF, T)
            with nc.Block() as block:
                @block.sync
                def _(sp):
                    w1 = L("w_ff1")
                    with sp.Fori(0, 3) as i:
                        for s in range(2):
                            c["sp_free"][s].enter(i, 1)
                            load_w(sp, s, w1[:, bass.ds(i * 1024 + (s + 2) * 512, 512)])
                    for s in range(2):
                        c["sp_free"][s].leave(3)
                    w2 = L("w_ff2")
                    prefetch(sp, w2[0:1024, 0:512], w2[1024:2048, 0:512])

                @block.tensor
                def _(pe):
                    with pe.Fori(0, 4) as i:
                        c["pe_from_dve"].enter(i, 8)
                        for s in range(2):
                            c["pe_full"][s].enter(i, 16)
                            pe.wait_ge(slot_full[s], c["pe_full"][s].next(16))
                            fm_tiles(pe, wslot(s), 0, hT, 4, c["pe_from_dve"], pe_for_act)
                    c["pe_from_dve"].leave(4)
                    c["pe_from_dve"].skip(4)
                    for s in range(2):
                        c["pe_full"][s].leave(4)

                @block.scalar
                def _(s):
                    with s.Fori(0, 4) as i:
                        c["act_from_pe"].enter(i, 8)
                        c["act"].enter(i, 16)
                        for sl in range(2):
                            for ct in range(4):
                                f = ff[:, bass.ds(i * 8 + sl * 4 + ct, 1), :].rearrange("p o t -> p (o t)")
                                s.wait_ge(pe_for_act, c["act_from_pe"].next())
                                for half in range(2):
                                    c["act"](S.activation(f[:, half * TH:(half + 1) * TH], pb[4 * half + ct][:, 0:TH], ACT.Relu))
                                S.sem_inc(act_for_dve, 1)
                    c["act_from_pe"].leave(4)
                    c["act"].leave(4)

                @block.vector
                def _(v):
                    dv = c["dve"]
                    V.sem_inc(dve_for_pe, 4)
                    with v.Fori(0, 4) as i:
                        c["dve_from_act"].enter(i, 8)
                        dv.enter(i, 8)
                        for sl in range(2):
                            for ct in range(4):
                                f = ff[:, bass.ds(i * 8 + sl * 4 + ct, 1), :].rearrange("p o t -> p (o t)")
                                v.wait_ge(act_for_dve, c["dve_from_act"].next())
                                V.sem_inc(dve_for_pe, 1)
                                dv(V.tensor_tensor(f, f, f, mult))
                            V.sem_inc(slot_free[sl], 1)
                    c["dve_from_act"].leave(4)
                    dv.leave(4)

            with nc.Block() as block:
                @block.sync
                def _(sp):
                    w2 = L("w_ff2")
                    for og in range(2):
                        for kg in range(0 if og else 2, 4):
                            load_w(sp, kg % 2, w2[kg * 1024:(kg + 1) * 1024, og * 512:(og + 1) * 512])

                @block.tensor
                def _(pe):
                    for og in range(2):
                        for kg in range(4):
                            pe.wait_ge(slot_full[kg % 2], c["pe_full"][kg % 2].next(16))
                            t = fm_tiles(pe, wslot(kg % 2), kg * 8, ff, 4, c["pe_from_dve"], pe_for_dve,
                                         first=(kg == 0), last=(kg == 3))
                            if kg < 3:
                                t.then_inc(slot_free[kg % 2], 1)
                    c["pe_from_dve"].skip(4)

                @block.vector
                def _(v):
                    V.sem_inc(dve_for_pe, 4)
                    for og in range(2):
                        for ct in range(4):
                            v.wait_ge(pe_for_dve, c["dve_from_pe"].next())
                            residual(v, c["dve"], 4 * og + ct, ct, 40, tmp8)
                        V.sem_inc(slot_free[1], 1)
            clear()

        c = counts()
        with nc.Block() as block:
            @block.tensor
            def _(pe):
                for m in range(5):
                    if m >= 3:
                        pe.wait_ge(dve_for_pe, c["pe_from_dve"].next())
                    r = P if m < MT else DEC
                    for k in range(KD):
                        t = tr(pb[2 * (m % 3) + k // 4][0:r, (k % 4) * P:(k % 4 + 1) * P], xT[:, k, m * P:m * P + r])
                    t.then_inc(pe_for_dve, 1)

            @block.vector
            def _(v):
                for m in range(5):
                    r = P if m < MT else DEC
                    v.wait_ge(pe_for_dve, c["dve_from_pe"].next())
                    for j in range(2):
                        c["dve"](V.tensor_copy(arena[0:r, m * D + j * 512:m * D + (j + 1) * 512], pb[2 * (m % 3) + j][0:r]))
                    V.sem_inc(dve_for_pe, 1)
                    V.sem_inc(dve_for_sp, 1)

            @block.sync
            def _(sp):
                for m in range(5):
                    sp.wait_ge(dve_for_sp, c["sp_from_dve"].next())
                    if m < MT:
                        sp.dma_start(y_p[0, m * P:(m + 1) * P, :], arena[:, m * D:(m + 1) * D]).then_inc(stored, 16)
                    else:
                        sp.dma_start(y_s.rearrange("b o d -> b (o d)"), arena[0:DEC, m * D:(m + 1) * D]).then_inc(stored, 16)
                sp.wait_ge(stored, c["stored"].next(80))


_INS = ['x_prompt', 'x_sample', 'c_prompt', 'c_sample', 'cache_k_diff', 'cache_v_diff', 'page_table', 'state_ret',
        'state_rwkv', 'state_shift', 'rel_bias', 'w_ada', 'b_ada', 'norm1', 'norm2', 'w_in', 'qk_norm_q', 'qk_norm_k',
        'lambda_q1', 'lambda_k1', 'lambda_q2', 'lambda_k2', 'subln_diff', 'mu_shift', 'w0', 'w_decay_up', 'a0',
        'w_a_up', 'w_g_up', 'v0', 'w_v_down', 'w_v_up', 'k_k', 'k_a', 'r_k', 'lnx_g', 'lnx_b', 'w_up_a', 'w_up_b',
        'w_up_c', 'w_out', 'w_ff1', 'w_ff2']
_OUTS = [(1, SEQ, D), (DEC, 1, D), (DEPTH, 1, SEQ, HB, 2 * DB), (DEPTH, 1, SEQ, HB, DVB), (DEPTH, DEC, 1, HB, 2 * DB),
         (DEPTH, DEC, 1, HB, DVB), (DEPTH, 1, HA, DA, DA), (DEPTH, DEC, HA, DA, DA), (DEPTH, 1, HC, DC, DC),
         (DEPTH, DEC, HC, DC, DC), (DEPTH, 1, 1, RW), (DEPTH, DEC, 1, RW)]


def kernel(**inputs):
    import numpy as _np
    import concourse.bacc as _bacc
    from concourse import mybir as _mybir
    from concourse.bass_utils import run_bass_kernel_spmd as _run

    nc = _bacc.Bacc("TRN2", target_bir_lowering=False, num_devices=1)
    arrays, args = {}, {}
    for name in _INS:
        v = _np.ascontiguousarray(inputs[name])
        arrays[f"in_{name}_dram"] = v
        args[name] = nc.dram_tensor(f"in_{name}_dram", v.shape, _mybir.dt.from_np(v.dtype), kind="ExternalInput").ap()
    table = shape_constants()
    arrays["shape_constants_dram"] = table
    consts = nc.dram_tensor("shape_constants_dram", table.shape, F32, kind="ExternalInput").ap()
    outs = [nc.dram_tensor(f"out_{i}_dram", shape, F32, kind="ExternalOutput").ap() for i, shape in enumerate(_OUTS)]
    build(nc, args, consts, outs)
    r = _run(nc, [arrays], core_ids=[0])
    return tuple(r.results[0][f"out_{i}_dram"] for i in range(len(_OUTS)))
```

```python
import math
from contextlib import ExitStack

import numpy as np

import concourse.bass as bass
from concourse import mybir

F32 = mybir.dt.float32
F32R = mybir.dt.float32r
I32 = mybir.dt.int32
ALU = mybir.AluOpType
ACT = mybir.ActivationFunctionType
AX = mybir.AxisListType

P = 128
D = 1024
KD = D // P
SEQ = 512
MT = SEQ // P
DEC = 8
T = SEQ + DEC
TH = T // 2
DEPTH = 2
PAST, PAGE = 256, 128
NPG = PAST // PAGE
NB = 32
HA, DA = 4, 128
HB, DB, DVB = 4, 64, 128
HC, DC = 8, 64
HP = HC // 2
W = 512
CH = 64
RW = 3 * W + 64 + 64 + 160
RT = 15
RET0, DIFF0, RW0 = 0, 2048, 3584
GATE0 = RW0 + RW
DFF = 4096
KF = DFF // P
EPS = 1e-6
LNX_EPS = 64e-5
MASKED = -1e30
TOE = 640

_c = 0
COL = {}
for _n, _w in (("ident", P), ("ones", P), ("blk", P), ("inner", HA * P), ("cross", HA * P), ("keep", 2 * P),
               ("level", 6 * P), ("cosq", 320), ("sinq", 320), ("cosk", 320), ("sink", 320), ("tail", HA),
               ("chunk", HA), ("gamma", HA), ("scan", T), ("c0", HB * DEC), ("c1", HB * DEC), ("selb", DEC),
               ("pair", 2), ("laminit", 2 * DEPTH), ("vmix", DEPTH), ("toe", TOE), ("past", NPG * P)):
    COL[_n] = (_c, _w)
    _c += _w
NCONST = _c
NKEPT = COL["toe"][0]

PROW = {}
_r = 0
for _n, _w in (("b_ada", 48), ("norm1", 8), ("norm2", 8), ("mu", 15), ("w0", 4), ("a0", 4), ("v0", 4),
               ("k_k", 4), ("k_a", 4), ("r_k", 4)):
    PROW[_n] = (_r, _w)
    _r += _w
NPAR = _r

BROW = {}
_b = 0
for _n, _w in (("qn", 64), ("kn", 64), ("subln", 128),
               ("lnx_g", 512), ("lnx_b", 512)):
    BROW[_n] = (_b, _w)
    _b += _w
NROW = _b


def shape_constants():
    t = np.zeros((P, NCONST), np.float32)

    def put(name, a):
        o, w = COL[name]
        a = np.asarray(a, np.float32)
        a = a.reshape(a.shape[0], -1)
        assert a.shape[1] == w, (name, a.shape)
        t[:a.shape[0], o:o + w] = a

    i = np.arange(P)
    put("ident", np.eye(P))
    put("ones", np.ones((P, P)))
    put("blk", (i[:, None] // 64) == (i[None, :] // 64))
    log_g = np.log1p(-np.exp2(-5.0 - np.arange(HA, dtype=np.float32))).astype(np.float32)
    dist = i[None, :] - i[:, None]
    put("inner", np.stack([np.where(dist >= 0, np.exp(np.maximum(dist, 0) * g), 0.0) for g in log_g], 1))
    put("cross", np.broadcast_to(np.stack([np.exp((i + 1.0) * g) for g in log_g])[None], (P, HA, P)))
    put("tail", np.exp((P - 1.0 - i)[:, None] * log_g[None]))
    put("chunk", np.broadcast_to(np.exp(P * log_g)[None], (P, HA)))
    put("gamma", np.broadcast_to(np.exp(log_g)[None], (P, HA)))
    same = (i[:, None] // CH) == (i[None, :] // CH)
    before = same & (i[:, None] < i[None, :])
    upto = same & (i[:, None] <= i[None, :])
    put("keep", np.stack([before, upto], 1))
    lv = []
    for k in range(6):
        m = 1 << k
        lv.append((i[:, None] // (2 * m) == i[None, :] // (2 * m)) & (i[:, None] % (2 * m) >= m)
                  & (i[None, :] % (2 * m) < m))
    put("level", np.stack(lv, 1))
    half = DA // 2
    inv = (np.float32(10000.0) ** (-np.arange(half, dtype=np.float32) / np.float32(half))).astype(np.float32)
    pos = np.zeros((P, 5), np.float32)
    for m in range(MT):
        pos[:, m] = m * P + i
    pos[:, 4] = PAST
    ang = (pos[:, :, None] * inv[None, None, :]).astype(np.float32)
    cs, sn = np.cos(ang), np.sin(ang)
    sc = DA ** -0.5
    put("cosq", cs)
    put("sinq", sn)
    put("cosk", cs * sc)
    put("sink", sn * sc)
    scan = np.ones(T)
    scan[0:SEQ:CH] = 0
    scan[SEQ:] = 0
    put("scan", np.broadcast_to(scan[None], (P, T)))

    def bucket(n):
        n = np.maximum(n, 0)
        nf = np.maximum(n, 1).astype(np.float32)
        large = 16 + (np.log(nf / np.float32(16)).astype(np.float32) / np.float32(math.log(128 / 16))
                      * np.float32(16)).astype(np.int32)
        return np.where(n < 16, n, np.minimum(large, NB - 1))

    n = 511 - np.arange(TOE)
    toe = np.zeros((NB + 1, TOE), np.float32)
    toe[bucket(n), np.arange(TOE)] = (n >= 0)
    toe[NB] = np.where(n >= 0, 0.0, 1.0)
    put("toe", toe)
    n = PAST - np.arange(PAST)
    past = np.zeros((NB, PAST), np.float32)
    past[bucket(n), np.arange(PAST)] = 1
    put("past", past)
    r = np.arange(DEC * 8)
    bb, hh, cc = r // 8, (r // 2) % 4, r % 2
    col = np.arange(HB * DEC)
    hit = (bb[:, None] == col[None] % DEC) & (hh[:, None] == col[None] // DEC)
    put("c0", hit & (cc[:, None] == 0))
    put("c1", hit & (cc[:, None] == 1))
    put("selb", bb[:, None] == np.arange(DEC)[None])
    put("pair", (i[:, None] // 64) == np.arange(2)[None])
    li = [0.8 - 0.6 * math.exp(-0.3 * l) for l in range(DEPTH)]
    put("laminit", np.broadcast_to(np.array([[x, 1.0 - x] for x in li])[None], (P, DEPTH, 2)))
    put("vmix", np.broadcast_to((np.arange(DEPTH) > 0)[None], (P, DEPTH)))
    return t


class Count:

    def __init__(self, sem):
        self.sem, self.base, self.i, self.per, self.j = sem, 0, None, 0, 0

    def next(self, by=1):
        self.j += by
        if self.i is None:
            self.base, self.j = self.base + self.j, 0
            return self.base
        return self.i * self.per + (self.base + self.j)

    def skip(self, n):
        assert self.i is None
        self.base += n

    def enter(self, i, per):
        self.i, self.per = i, per

    def leave(self, n):
        assert self.j == self.per, (self.j, self.per)
        self.base, self.i, self.j = self.base + n * self.per, None, 0


class Chain(Count):

    def __init__(self, eng, sem):
        super().__init__(sem)
        self.eng = eng

    def __call__(self, ins):
        ins.then_inc(self.sem, 1)
        self.eng.wait_ge(self.sem, self.next())


def build(nc, a, consts, outs):
    (y_p, y_s, k_p, v_p, k_s, v_s, ret_p, ret_s, rwkv_p, rwkv_s, shift_p, shift_s) = outs
    skew = nc.dram_tensor("skew_dram", (HB, P, TOE), F32, kind="Internal").ap()
    x_spill = nc.dram_tensor("x_spill_dram", (P, KD * T), F32, kind="Internal").ap()
    v_spill = nc.dram_tensor("v_spill_dram", (P, HP * T), F32, kind="Internal").ap()
    V, S, G, PE = nc.vector, nc.scalar, nc.gpsimd, nc.tensor
    with ExitStack() as ctx:
        def sb(name, n, dt=F32, p=P):
            return ctx.enter_context(nc.sbuf_tensor(name, [p, n], dt))

        def aligned(at_byte):
            return -(-at_byte // 32) * 32

        x_at = aligned(nc.sbuf_base)
        xT = sb("xT", KD * T)[:, :].rearrange("p (k t) -> p k t", k=KD)
        x_raw = xT.rearrange("p k t -> p (k t)")
        h_raw = [sb(f"h_{n}", KD * T + P - DEC, F32R)[:, :] for n in ("high", "low")]
        hT = [h[:, 0:KD * T].rearrange("p (k t) -> p k t", k=KD) for h in h_raw]
        ring_at = aligned(nc.sbuf_base)
        ring = [sb("ring0", 4096)[:, :], sb("ring1", 4096)[:, :], None, None]
        y_at = aligned(nc.sbuf_base)
        y_raw = sb("yT", 12 * T)[:, :]
        yT = y_raw.rearrange("p (k t) -> p k t", k=12)
        modT = sb("modT", 48 * 9)[:, :].rearrange("p (k s) -> p k s", k=48)
        coef = sb("coef", KD * 9)[:, :].rearrange("p (k s) -> p k s", k=KD)
        csT = sb("csT", KD * 9)[:, :].rearrange("p (k s) -> p k s", k=KD)
        par = sb("par", NPAR)[:, :]
        rows = sb("rows", NROW)[:, :]
        cst = sb("cst", NKEPT)[:, :]
        biasD = sb("biasD", NPG * HB)[:, :].rearrange("p (g h) -> p g h", g=NPG)
        bias0 = sb("bias0", HB)[:, :]
        tab = sb("tab", HB)[:, :]
        rstd = sb("rstd", T)[:, :]
        small = sb("small", 512)[:, :]
        pages = sb("pages", DEC * NPG, I32, 1)[:, :]
        AR = 18688
        arena_at = aligned(nc.sbuf_base)
        arena = sb("arena", AR)[:, :]

        def halves(name, where, offset, n):
            return nc.alloc_sbuf_tensor_at(name, [P, n], F32R, offset=where + 4 * offset)[:, :]

        w_split = [[halves("w_high0", arena_at, 10240, 2048), halves("w_low0", arena_at, 12288, 2048)],
                   [halves("w_high1", arena_at, 14336, 2048), halves("w_low1", arena_at, 16384, 2048)]]
        f_split = [[halves("f_high0", y_at, 0, 2048), halves("f_low0", y_at, 2048, 2048)],
                   [halves("f_high1", y_at, 4096, 2048), halves("f_low1", arena_at, 16640, 2048)]]
        y_split = [halves("y_high", x_at, 0, HP * T), halves("y_low", x_at, HP * T, HP * T)]
        tok_split = [halves("tok_high", x_at, 0, 2560), halves("tok_low", ring_at, 4096 + 1536, 2560)]
        tok_place = halves("tok_place", ring_at, 2560, DEC * P).rearrange("p (b n) -> p b n", b=DEC)
        m_split = [halves("m_high", arena_at, 4160, KD * T), halves("m_low", y_at, 0, KD * T)]
        ring[2], ring[3] = arena[:, 6300:10396], arena[:, 10396:14492]
        pb = [ctx.enter_context(nc.psum_tensor(f"pb{i}", [P, 512], F32))[:, :] for i in range(8)]

        def at(base, off, *dims):
            n = 1
            for d in dims:
                n *= d
            ap = base[:, off:off + n]
            if len(dims) == 2:
                return ap.rearrange("p (a b) -> p a b", a=dims[0])
            if len(dims) == 3:
                return ap.rearrange("p (a b c) -> p a b c", a=dims[0], b=dims[1])
            if len(dims) == 4:
                return ap.rearrange("p (a b c d) -> p a b c d", a=dims[0], b=dims[1], c=dims[2])
            return ap

        def C(name, *dims):
            return at(cst, COL[name][0], *(dims or (COL[name][1],)))

        def PR(name):
            return par[:, PROW[name][0]:PROW[name][0] + PROW[name][1]]

        def BR(name):
            return rows[:, BROW[name][0]:BROW[name][0] + BROW[name][1]]

        ident, ones, blk = C("ident"), C("ones"), C("blk")
        eps = small[:, 0:1]
        eps_ln = small[:, 1:2]
        lam = small[:, 2:3]

        def sem(name):
            return ctx.enter_context(nc.semaphore(name))

        sems = {n: sem(n) for n in (
            "split_high", "split_ready", "split_free", "y_split", "slot0_full", "slot1_full", "slot2_full", "slot3_full", "slot0_free", "slot1_free", "slot2_free", "slot3_free", "loaded", "states_loaded", "stored",
            "pe_for_dve", "dve_for_pe", "pe_for_act", "act_for_pe", "dve_for_act", "act_for_dve",
            "dve_done", "act_done", "dve_for_sp", "page0_full", "page1_full", "page_free",
            "scores_ready", "scores_read", "logits_ready", "exp_ready", "weights_ready", "turned", "turned_read",
            "values_ready", "values_read", "ada_ready", "ada_copied", "ada_turned", "ada_read", "chunk_scores", "chunk_weighted", "decode_added")}
        chunk_scores, chunk_weighted, decode_added = sems["chunk_scores"], sems["chunk_weighted"], sems["decode_added"]
        pe_for_dve, dve_for_pe = sems["pe_for_dve"], sems["dve_for_pe"]
        pe_for_act, act_for_pe = sems["pe_for_act"], sems["act_for_pe"]
        dve_for_act, act_for_dve = sems["dve_for_act"], sems["act_for_dve"]
        split_high, split_ready, split_free = sems["split_high"], sems["split_ready"], sems["split_free"]
        y_split_ready = sems["y_split"]
        loaded, stored = sems["loaded"], sems["stored"]
        states_loaded = sems["states_loaded"]
        dve_for_sp = sems["dve_for_sp"]
        page_full, page_free = [sems["page0_full"], sems["page1_full"]], sems["page_free"]
        scores_ready, scores_read, logits_ready = sems["scores_ready"], sems["scores_read"], sems["logits_ready"]
        exp_ready, weights_ready = sems["exp_ready"], sems["weights_ready"]
        turned, turned_read = sems["turned"], sems["turned_read"]
        values_ready, values_read = sems["values_ready"], sems["values_read"]
        ada_ready, ada_copied = sems["ada_ready"], sems["ada_copied"]
        ada_turned, ada_read = sems["ada_turned"], sems["ada_read"]
        slot_full = [sems[f"slot{n}_full"] for n in range(4)]
        slot_free = [sems[f"slot{n}_free"] for n in range(4)]

        def counts():
            c = {
                "split_high": Count(split_high), "split_ready": Count(split_ready), "split_free": Count(split_free),
                "pe_full": [Count(s) for s in slot_full], "sp_free": [Count(s) for s in slot_free],
                "dve_from_pe": Count(pe_for_dve), "pe_from_dve": Count(dve_for_pe),
                "act_from_pe": Count(pe_for_act), "pe_from_act": Count(act_for_pe),
                "act_from_dve": Count(dve_for_act), "dve_from_act": Count(act_for_dve),
                "dve": Chain(V, sems["dve_done"]), "act": Chain(S, sems["act_done"]),
                "loaded": Count(loaded), "stored": Count(stored),
                "sp_from_dve": Count(dve_for_sp), 
            }
            return c

        def clear():
            with nc.Block() as block:
                @block.gpsimd
                def _(g):
                    for s in sems.values():
                        g.sem_clear(s)

        def mm(out, lhsT, rhs, start=True, stop=True):
            return PE.matmul(out, lhsT, rhs, start=start, stop=stop, skip_group_check=True)

        def tr(out, in_):
            return PE.transpose(out, in_, ident[0:in_.shape[0], 0:in_.shape[0]])

        def bc(ap, shape, *dims):
            for d in dims:
                ap = ap.unsqueeze(d)
            return ap.broadcast_to(shape)

        mult, add, sub, amax = ALU.mult, ALU.add, ALU.subtract, ALU.max

        c = counts()
        dist_rows = arena[:, 11000:11000 + NCONST - NKEPT]
        toe, past = dist_rows[:, 0:TOE], dist_rows[:, TOE:TOE + NPG * P]
        with nc.Block() as block:
            @block.vector
            def _(v):
                c["dve"](V.memset(arena[:, 4096:6144], 0.0))
        with nc.Block() as block:
            @block.sync
            def _(sp):
                sp.dma_start(cst, consts[:, 0:NKEPT]).then_inc(loaded, 16)
                sp.dma_start(dist_rows, consts[:, NKEPT:NCONST]).then_inc(loaded, 16)
                sp.dma_start(at(arena, 0, MT, D), a["x_prompt"].rearrange("o (m p) d -> p (o m) d", p=P)).then_inc(loaded, 16)
                sp.dma_start(arena[0:DEC, 4096:5120], a["x_sample"].rearrange("b o d -> b (o d)")).then_inc(loaded, 16)
                sp.dma_start(arena[0:1, 5120:6144], a["c_prompt"]).then_inc(loaded, 16)
                sp.dma_start(arena[1:9, 5120:6144], a["c_sample"]).then_inc(loaded, 16)
                sp.dma_start(tab[0:NB, :], a["rel_bias"]).then_inc(loaded, 16)
                sp.dma_start(bias0, a["rel_bias"][0].partition_broadcast(P)).then_inc(loaded, 16)
                sp.dma_start(pages, a["page_table"].rearrange("(o b) g -> o (b g)", o=1)).then_inc(loaded, 16)
                sp.wait_ge(loaded, 9 * 16)

            @block.vector
            def _(v):
                dv = c["dve"]
                dv(V.memset(arena[:, 6144:11000], 0.0))
                dv(V.memset(arena[:, 11000 + NCONST - NKEPT:AR], 0.0))
                dv(V.memset(tab[NB:NB + 1, :], MASKED))
                dv(V.memset(small, 0.0))
                dv(V.memset(eps, EPS))
                dv(V.memset(eps_ln, LNX_EPS))
                for h in h_raw:
                    dv(V.memset(h.bitcast(F32)[:, KD * T:], 0.0))
                dv(V.memset(ring[1], 0.0))
                dv(V.memset(y_raw, 0.0))
        c["loaded"].skip(9 * 16)
        with nc.Block() as block:
            @block.scalar
            def _(s):
                c["act"](S.activation(arena[0:9, 6144:7168], arena[0:9, 5120:6144], ACT.Sigmoid))
                S.sem_inc(act_for_dve, 1)

            @block.tensor
            def _(pe):
                for k in range(KD):
                    if k >= 4:
                        pe.wait_ge(dve_for_pe, c["pe_from_dve"].next())
                    for m in range(MT):
                        tr(pb[k % 4][:, m * P:(m + 1) * P], arena[:, m * D + k * P:m * D + (k + 1) * P])
                    tr(pb[4 + k % 4][:, 0:DEC], arena[0:DEC, 4096 + k * P:4096 + (k + 1) * P]).then_inc(pe_for_dve, 1)
                pe.wait_ge(dve_for_pe, c["pe_from_dve"].next(5))
                for k in range(KD):
                    t = tr(pb[0][:, k * 9:k * 9 + 9], arena[0:9, 6144 + k * P:6144 + (k + 1) * P])
                t.then_inc(pe_for_dve, 1)
                pe.wait_ge(dve_for_pe, c["pe_from_dve"].next())
                for h in range(HB):
                    mm(pb[h], tab[0:NB + 1, h:h + 1].broadcast_to([NB + 1, P]), toe[0:NB + 1, 0:512])
                    mm(pb[4 + h][:, 0:128], tab[0:NB + 1, h:h + 1].broadcast_to([NB + 1, P]),
                       toe[0:NB + 1, 512:640])
                for g in range(NPG):
                    t = mm(pb[4][:, 256 + g * HB:256 + (g + 1) * HB], past[0:NB, g * P:(g + 1) * P], tab[0:NB, :])
                t.then_inc(pe_for_dve, 1)

            @block.vector
            def _(v):
                dv = c["dve"]
                for k in range(KD):
                    v.wait_ge(pe_for_dve, c["dve_from_pe"].next())
                    V.tensor_copy(xT[:, k, 0:SEQ], pb[k % 4])
                    dv(V.tensor_copy(xT[:, k, SEQ:T], pb[4 + k % 4][:, 0:DEC]))
                    V.sem_inc(dve_for_pe, 1)
                v.wait_ge(act_for_dve, c["dve_from_act"].next())
                dv(V.tensor_tensor(arena[0:9, 6144:7168], arena[0:9, 6144:7168], arena[0:9, 5120:6144], mult))
                V.sem_inc(dve_for_pe, 1)
                v.wait_ge(pe_for_dve, c["dve_from_pe"].next())
                dv(V.tensor_copy(csT.rearrange("p k s -> p (k s)"), pb[0][:, 0:72]))
                V.sem_inc(dve_for_pe, 1)
                v.wait_ge(pe_for_dve, c["dve_from_pe"].next())
                for h in range(HB):
                    V.tensor_copy(at(arena, 8192, HB, TOE)[:, h, 0:512], pb[h])
                    V.tensor_copy(at(arena, 8192, HB, TOE)[:, h, 512:640], pb[4 + h][:, 0:128])
                dv(V.tensor_copy(biasD.rearrange("p g h -> p (g h)"), pb[4][:, 256:256 + NPG * HB]))
                V.sem_inc(dve_for_sp, 1)

            @block.sync
            def _(sp):
                sp.wait_ge(dve_for_sp, c["sp_from_dve"].next())
                sp.dma_start(skew.rearrange("h p u -> p h u"), at(arena, 8192, HB, TOE)).then_inc(loaded, 16)
                sp.dma_start(v_spill, arena[:, 14000:14000 + HP * T]).then_inc(loaded, 16)
                sp.wait_ge(loaded, c["loaded"].next(32))
        clear()

        with nc.Fori(0, DEPTH) as l:
            c = counts()

            def L(name):
                ap = a[name][bass.ds(l, 1)]
                dims = "abcdef"[:len(ap.shape) - 1]
                return ap.rearrange("o " + " ".join(dims) + " -> (o " + dims[0] + ") " + " ".join(dims[1:]))

            def Lo(ap):
                ap = ap[bass.ds(l, 1)]
                dims = "abcdef"[:len(ap.shape) - 1]
                return ap.rearrange("o " + " ".join(dims) + " -> (o " + dims[0] + ") " + " ".join(dims[1:]))

            def load_w(sp, slot, src, k=8):
                sp.wait_ge(slot_free[slot], c["sp_free"][slot].next())
                n = src.shape[1]
                sp.dma_start(at(ring[slot], 0, k, 4096 // k)[:, :, 0:n],
                             src.rearrange("(k p) n -> p k n", p=P)).then_inc(slot_full[slot], 16)

            def load_w4(sp, slot, src):
                sp.wait_ge(slot_free[slot], c["sp_free"][slot].next())
                sp.dma_start(at(ring[slot], 0, 4, 512), src.rearrange("(k p) n -> p k n", p=P)).then_inc(slot_full[slot], 16)

            def wslot(slot, k=8):
                return at(ring[slot], 0, k, 4096 // k)

            def split_hi(s, ws, n, slot, u=0, first=True, acts=None):
                if first:
                    s.wait_ge(slot_full[slot], c["pe_full"][slot].next(16))
                t = S.activation(ws[n % 2][0], ring[slot][:, u * 2048:(u + 1) * 2048], ACT.Copy)
                if acts is not None:
                    t = S.activation(acts[0], acts[2], ACT.Copy)
                t.then_inc(split_high, 1)

            def split_lo(v, ws, n, slot, u=0, last=True, acts=None):
                v.wait_ge(split_high, c["split_high"].next())
                t = V.tensor_tensor(ws[n % 2][1], ring[slot][:, u * 2048:(u + 1) * 2048], ws[n % 2][0].bitcast(F32), sub)
                if acts is not None:
                    t = V.tensor_tensor(acts[1], acts[2], acts[0].bitcast(F32), sub)
                c["dve"](t)
                V.sem_inc(split_ready, 1)
                if last:
                    V.sem_inc(slot_free[slot], 1)

            def fm_unit(pe, ws, n, hi, lo, k0, free, done, n_tiles=4, first=True, last=True, nk=4):
                pe.wait_ge(split_ready, c["split_ready"].next())
                wh, wl = (ws[n % 2][x].rearrange("p (k n) -> p k n", k=nk) for x in range(2))
                for ct in range(n_tiles):
                    if first and free is not None:
                        pe.wait_ge(free.sem, free.next())
                    cs = slice(ct * P, (ct + 1) * P)
                    for k in range(nk):
                        for x, (w, act) in enumerate(((wh, hi), (wh, lo), (wl, hi))):
                            for half in range(2):
                                t = mm(pb[4 * half + ct][:, 0:TH], w[:, k, cs], act[:, k0 + k, half * TH:(half + 1) * TH],
                                       start=first and k == 0 and x == 0, stop=last and k == nk - 1 and x == 2)
                    if last:
                        t.then_inc(done, 1)
                if not last:
                    t.then_inc(split_free, 1)

            lambdas = at(arena, 256, 4, 64)
            with nc.Block() as block:
                @block.sync
                def _(sp):
                    n = 0
                    for name in PROW:
                        r0, nr = PROW[name]
                        if name == "v0":
                            src = a["v0"].rearrange("o (r c) -> (o r) c", c=P)
                        elif name == "mu":
                            mu = L("mu_shift")
                            sp.dma_start(arena[r0 + 14:r0 + 15, 0:32], mu[14 * P:RW].rearrange("(o c) -> o c", o=1)).then_inc(loaded, 16)
                            src = mu[0:14 * P].rearrange("(r c) -> r c", c=P)
                            n += 1
                        elif name == "r_k":
                            src = L("r_k").rearrange("(r h) d -> r (h d)", h=2)
                        else:
                            src = L(name).rearrange("(r c) -> r c", c=P)
                        sp.dma_start(arena[r0:r0 + src.shape[0], 0:P], src).then_inc(loaded, 16)
                        n += 1
                    for name, key in (("qn", "qk_norm_q"), ("kn", "qk_norm_k"), ("subln", "subln_diff"), ("lnx_g", "lnx_g"), ("lnx_b", "lnx_b")):
                        sp.dma_start(BR(name), L(key).partition_broadcast(P)).then_inc(loaded, 16)
                        n += 1
                    for i, key in enumerate(("lambda_q1", "lambda_q2", "lambda_k1", "lambda_k2")):
                        sp.dma_start(lambdas[:, i], L(key).partition_broadcast(P)).then_inc(loaded, 16)
                        n += 1
                    for s in range(4):
                        load_w(sp, s, L("w_ada")[:, s * 512:(s + 1) * 512])
                    sp.wait_ge(loaded, 16 * n)
                    c["loaded"].skip(16 * n)

                @block.tensor
                def _(pe):
                    for s in range(4):
                        pe.sem_inc(slot_free[s], 1)
            with nc.Block() as block:
                @block.tensor
                def _(pe):
                    tr(pb[0][:, 0:NPAR], arena[0:NPAR, 0:P]).then_inc(pe_for_dve, 1)

                @block.vector
                def _(v):
                    dv = c["dve"]
                    v.wait_ge(pe_for_dve, c["dve_from_pe"].next())
                    dv(V.tensor_copy(par, pb[0][:, 0:NPAR]))
                    dv(V.tensor_tensor(at(small, 16, 2, 64), lambdas[:, 0:2], lambdas[:, 2:4], mult))
                    dv(V.tensor_reduce(small[:, 4:6], at(small, 16, 2, 64), AX.X, add))
                    V.sem_inc(dve_for_act, 1)
                    v.wait_ge(act_for_dve, c["dve_from_act"].next())
                    dv(V.tensor_tensor(lam, small[:, 6:7], small[:, 7:8], sub))
                    li = C("laminit", DEPTH, 2)
                    dv(V.tensor_tensor(lam, lam, li[:, bass.ds(l, 1), 0:1].rearrange("p a b -> p (a b)"), add))
                    dv(V.tensor_scalar(BR("subln"), BR("subln"), li[:, bass.ds(l, 1), 1:2].rearrange("p a b -> p (a b)"), None, mult))

                @block.scalar
                def _(s):
                    s.wait_ge(dve_for_act, c["act_from_dve"].next())
                    c["act"](S.activation(small[:, 6:8], small[:, 4:6], ACT.Exp))
                    S.sem_inc(act_for_dve, 1)

            w_in = L("w_in")
            mrows = at(arena, 0, 4, 512)[0:9]

            def prefetch(sp, *blocks):
                for s, src in enumerate(blocks):
                    load_w(sp, s, src)

            with nc.Block() as block:
                @block.sync
                def _(sp):
                    prefetch(sp, w_in[:, RET0:RET0 + 512], w_in[:, RET0 + 512:RET0 + 1024])

                @block.tensor
                def _(pe):
                    for s in range(5):
                        if s < 4:
                            pe.wait_ge(slot_full[s], c["pe_full"][s].next(16))
                            w = wslot(s)
                            for k in range(KD):
                                t = mm(pb[s][0:9, :], csT[:, k, :], w[:, k, :], start=(k == 0), stop=(k == KD - 1))
                            t.then_inc(pe_for_dve, 1)
                        if s:
                            pe.wait_ge(dve_for_pe, c["pe_from_dve"].next())
                            for ct in range(4):
                                t = tr(pb[3 + s][:, ct * 9:ct * 9 + 9], mrows[:, s - 1, ct * P:(ct + 1) * P])
                            t.then_inc(pe_for_dve, 1)

                @block.vector
                def _(v):
                    for s in range(5):
                        if s < 4:
                            v.wait_ge(pe_for_dve, c["dve_from_pe"].next())
                            c["dve"](V.tensor_copy(mrows[:, s], pb[s][0:9, :]))
                            V.sem_inc(dve_for_pe, 1)
                            V.sem_inc(slot_free[s], 1)
                        if s:
                            v.wait_ge(pe_for_dve, c["dve_from_pe"].next())
                            c["dve"](V.tensor_tensor(
                                modT[:, (s - 1) * 4:s * 4, :], pb[3 + s][:, 0:36].rearrange("p (c s) -> p c s", c=4),
                                bc(PR("b_ada")[:, (s - 1) * 4:s * 4], [P, 4, 9], 2), add))

            def norm_stage(gain, shift0, scale0, spill, ws):
                with nc.Block() as block:
                    ht = at(arena, 4160, KD, T)
                    sq = at(arena, 0, KD, T)

                    @block.vector
                    def _(v):
                        dv = c["dve"]
                        for k in range(0, KD, 2):
                            dv(V.tensor_tensor(sq[:, k], xT[:, k], xT[:, k], mult))
                            v.wait_ge(act_for_dve, c["dve_from_act"].next())
                            V.tensor_tensor(sq[:, k], sq[:, k], sq[:, k + 1], add).then_inc(dve_for_pe, 1)
                        dv(V.tensor_scalar(coef, modT[:, scale0:scale0 + KD, :], 1.0, None, add))
                        dv(V.tensor_tensor(coef, coef, bc(PR(gain), [P, KD, 9], 2), mult))
                        split_lo(v, ws, 0, 0, 0, last=False)
                        v.wait_ge(act_for_dve, c["dve_from_act"].next())
                        dv(V.reciprocal(rstd, rstd))
                        dv(V.tensor_tensor(ht[:, :, SEQ:T], xT[:, :, SEQ:T], bc(rstd[:, SEQ:T], [P, KD, DEC], 1), mult))
                        dv(V.tensor_tensor(ht[:, :, SEQ:T], ht[:, :, SEQ:T], coef[:, :, 1:9], mult))
                        dv(V.tensor_tensor(ht[:, :, SEQ:T], ht[:, :, SEQ:T], modT[:, shift0:shift0 + KD, 1:9], add))
                        for k in range(KD + 2):
                            if k < KD:
                                dv(V.tensor_tensor(ht[:, k, 0:SEQ], xT[:, k, 0:SEQ], rstd[:, 0:SEQ], mult))
                                V.tensor_scalar(ht[:, k, 0:SEQ], ht[:, k, 0:SEQ], coef[:, k, 0:1],
                                                modT[:, shift0 + k, 0:1], mult, add).then_inc(dve_for_act, 1)
                            if k >= 2:
                                v.wait_ge(act_for_dve, c["dve_from_act"].next())
                                t = V.tensor_tensor(hT[1][:, k - 2], ht[:, k - 2], hT[0][:, k - 2].bitcast(F32), sub)
                        dv(t)

                    @block.tensor
                    def _(pe):
                        for k in range(0, KD, 2):
                            pe.wait_ge(dve_for_pe, c["pe_from_dve"].next())
                            for half in range(2):
                                t = mm(pb[half][:, 0:TH], ones, sq[:, k, half * TH:(half + 1) * TH],
                                       start=(k == 0), stop=(k == KD - 2))
                        t.then_inc(pe_for_act, 1)

                    @block.scalar
                    def _(s):
                        for k in range(1, KD, 2):
                            S.activation(sq[:, k], xT[:, k], ACT.Square).then_inc(act_for_dve, 1)
                        split_hi(s, ws, 0, 0, 0)
                        s.wait_ge(pe_for_act, c["act_from_pe"].next())
                        for half in range(2):
                            c["act"](S.activation(rstd[:, half * TH:(half + 1) * TH], pb[half][:, 0:TH], ACT.Sqrt,
                                                  bias=eps, scale=1.0 / D))
                        S.sem_inc(act_for_dve, 1)
                        for k in range(KD):
                            s.wait_ge(dve_for_act, c["act_from_dve"].next())
                            S.activation(hT[0][:, k], ht[:, k], ACT.Copy).then_inc(act_for_dve, 1)

                    if spill:
                        @block.sync
                        def _(sp):
                            sp.dma_start(x_spill, x_raw).then_inc(stored, 16)
                            sp.wait_ge(stored, c["stored"].next(16))

            norm_stage("norm1", 0, 8, True, w_split)

            def token_major(col0, n_blocks, n_split):
                with nc.Block() as block:
                    @block.sync
                    def _(sp):
                        for b in range(2, n_blocks):
                            load_w(sp, b % 2, w_in[:, col0 + 512 * b:col0 + 512 * (b + 1)])

                    @block.tensor
                    def _(pe):
                        for n in range(2 * n_blocks):
                            u = n % 2
                            pe.wait_ge(split_ready, c["split_ready"].next())
                            wh, wl = (w_split[u][x].rearrange("p (k n) -> p k n", k=4) for x in range(2))
                            for m in range(5):
                                if u == 0:
                                    pe.wait_ge(act_for_pe, c["pe_from_act"].next())
                                for k in range(4):
                                    tk = slice((4 * u + k) * T + m * P, (4 * u + k) * T + (m + 1) * P)
                                    for x, (h, w) in enumerate(((0, wh), (1, wh), (0, wl))):
                                        t = mm(pb[m], h_raw[h][:, tk], w[:, k, :], start=(u == 0 and k == 0 and x == 0),
                                               stop=(u == 1 and k == 3 and x == 2))
                                if u:
                                    t.then_inc(pe_for_act, 1)
                            if u == 0:
                                t.then_inc(split_free, 1)
                        c["pe_from_act"].skip(5)

                    @block.scalar
                    def _(s):
                        S.sem_inc(act_for_pe, 5)
                        if n_split == 0:
                            split_hi(s, w_split, 0, 0, 0)
                        split_hi(s, w_split, 1, 0, 1, first=False)
                        for b in range(n_blocks):
                            s.wait_ge(split_free, c["split_free"].next())
                            if b + 1 < n_blocks:
                                split_hi(s, w_split, 2 * b + 2, (b + 1) % 2, 0)
                            for m in range(5):
                                r = P if m < MT else DEC
                                s.wait_ge(pe_for_act, c["act_from_pe"].next())
                                c["act"](S.activation(arena[0:r, (b * 5 + m) * 512:(b * 5 + m + 1) * 512],
                                                      pb[m][0:r, :], ACT.Copy))
                                S.sem_inc(act_for_pe, 1)
                            if b + 1 < n_blocks:
                                split_hi(s, w_split, 2 * b + 3, (b + 1) % 2, 1, first=False)

                    @block.vector
                    def _(v):
                        for n in range(n_split, 2 * n_blocks):
                            split_lo(v, w_split, n, n // 2 % 2, n % 2, last=(n % 2 == 1))

            def heads_to_columns(block_fns, srcs, dst, heads=4, m_tiles=5):
                def pe_part(pe):
                    pe.wait_ge(dve_for_pe, c["pe_from_dve"].next())
                    for n, src in enumerate(srcs):
                        for h in range(heads):
                            if n:
                                pe.wait_ge(dve_for_pe, c["pe_from_dve"].next())
                            for m in range(MT):
                                tr(pb[h][:, m * P:(m + 1) * P], src[:, m, h * P:(h + 1) * P])
                            t = tr(pb[4 + h][:, 0:DEC], src[0:DEC, MT, h * P:(h + 1) * P])
                            t.then_inc(pe_for_dve, 1)

                def dve_part(v):
                    V.sem_inc(dve_for_pe, 1)
                    for n in range(len(srcs)):
                        for h in range(heads):
                            v.wait_ge(pe_for_dve, c["dve_from_pe"].next())
                            V.tensor_copy(dst[:, 4 * n + h, 0:SEQ], pb[h])
                            c["dve"](V.tensor_copy(dst[:, 4 * n + h, SEQ:T], pb[4 + h][:, 0:DEC]))
                            if n < len(srcs) - 1:
                                V.sem_inc(dve_for_pe, 1)
                return pe_part, dve_part

            token_major(RET0, 4, 1)
            Z = lambda b: at(arena, b * 2560, 5, 512)
            rot = [at(arena, 10240, 5, 512), at(arena, 12800, 5, 512)]
            qkT = at(arena, 0, 8, T)
            with nc.Block() as block:
                pe_part, dve_part = heads_to_columns(None, rot, qkT)
                vmask = at(ring[0], 0, DEC, 512)
                dstate = at(y_raw, 4 * T, 2, 4, HA, P)
                qc = at(arena, 10240, HA, SEQ)
                sc = [at(arena, 15360, HA, P), at(arena, 16896, HA, P)]
                st = at(arena, 15872, HA, P)
                od = at(arena, 16384, HA, DEC)
                oa = at(x_raw, 0, 5, 512)

                @block.vector
                def _(v):
                    dv = c["dve"]
                    tmp = at(arena, 15360, 5, HA, 64)
                    for n, (cn, sn) in enumerate((("cosq", "sinq"), ("cosk", "sink"))):
                        x = at(arena, n * 2560, 20, 2, 64).rearrange("p (m h) t d -> p m h t d", m=5)
                        o = at(arena, 10240 + n * 2560, 20, 2, 64).rearrange("p (m h) t d -> p m h t d", m=5)
                        cs = bc(C(cn, 5, 64), [P, 5, HA, 64], 2)
                        sn_ = bc(C(sn, 5, 64), [P, 5, HA, 64], 2)
                        x1, x2, o1, o2 = x[:, :, :, 0, :], x[:, :, :, 1, :], o[:, :, :, 0, :], o[:, :, :, 1, :]
                        dv(V.tensor_tensor(o1, x1, cs, mult))
                        dv(V.tensor_tensor(tmp, x2, sn_, mult))
                        dv(V.tensor_tensor(o1, o1, tmp, sub))
                        dv(V.tensor_tensor(o2, x1, sn_, mult))
                        dv(V.tensor_tensor(tmp, x2, cs, mult))
                        dv(V.tensor_tensor(o2, o2, tmp, add))
                    dve_part(v)
                    kt = at(arena, 12800, MT, HA, P)
                    dv(V.tensor_tensor(kt, kt, bc(C("tail"), [P, MT, HA, P], 1, 3), mult))
                    q4 = at(arena, 0, HA, T)[:, :, 0:SEQ].rearrange("p h (n i) -> p h n i", n=MT)
                    dv(V.tensor_tensor(qc.rearrange("p h (n i) -> p h n i", n=MT), q4,
                                       bc(C("cross", HA, P), [P, HA, MT, P], 2), mult))
                    dv(V.tensor_tensor(vmask[0:DEC], bc(Z(2)[0:DEC, MT, :], [DEC, DEC, 512], 1),
                                       bc(ident[0:DEC, 0:DEC], [DEC, DEC, 512], 2), mult))
                    V.sem_inc(dve_for_pe, 1)
                    for n in range(MT):
                        v.wait_ge(chunk_scores, n + 1)
                        V.tensor_tensor(sc[n % 2], at(pb[3 * (n % 2)], 0, HA, P), C("inner", HA, P), mult)\
                         .then_inc(chunk_weighted, 1)
                        v.wait_ge(pe_for_dve, c["dve_from_pe"].next())
                        V.tensor_copy(oa[:, n, :], pb[1])
                        if n == 0:
                            dv(V.tensor_copy(st, at(pb[2], 0, HA, P)))
                        else:
                            dv(V.tensor_tensor(st, st, bc(C("chunk"), [P, HA, P], 2), mult))
                            dv(V.tensor_tensor(st, st, at(pb[2], 0, HA, P), add))
                        V.sem_inc(dve_for_pe, 1)
                        if n == 0:
                            v.wait_ge(loaded, c["loaded"].base + 16 * DEC)
                        v.wait_ge(pe_for_dve, c["dve_from_pe"].next())
                        for h in range(2 * (n % 2), 2 * (n % 2) + 2):
                            V.scalar_tensor_tensor(dstate[:, n // 2, :, h, :], dstate[:, n // 2, :, h, :],
                                                   C("gamma")[:, h:h + 1], at(pb[4 + h], 0, 4, P), mult, add)\
                             .then_inc(decode_added, 1)
                    v.wait_ge(decode_added, 2 * MT)
                    V.sem_inc(dve_for_sp, 1)
                    v.wait_ge(pe_for_dve, c["dve_from_pe"].next())
                    dv(V.tensor_copy(od, at(pb[0], 0, HA, DEC)))
                    V.sem_inc(dve_for_pe, 1)
                    v.wait_ge(pe_for_dve, c["dve_from_pe"].next())
                    dv(V.tensor_copy(oa[0:DEC, MT, :], pb[1][0:DEC, :]))

                @block.tensor
                def _(pe):
                    pe_part(pe)
                    pe.wait_ge(dve_for_pe, c["pe_from_dve"].next())
                    for n in range(-1, MT):
                        if n + 1 < MT:
                            tok = slice((n + 1) * P, (n + 2) * P)
                            if n >= 1:
                                pe.wait_ge(chunk_weighted, n)
                            for h in range(HA):
                                t = mm(pb[3 * ((n + 1) % 2)][:, h * P:(h + 1) * P], qkT[:, 4 + h, tok], qkT[:, h, tok])
                            t.then_inc(chunk_scores, 1)
                        if n < 0:
                            continue
                        tok = slice(n * P, (n + 1) * P)
                        pe.wait_ge(chunk_weighted, n + 1)
                        if n:
                            pe.wait_ge(dve_for_pe, c["pe_from_dve"].next())
                        for h in range(HA):
                            hs = slice(h * P, (h + 1) * P)
                            mm(pb[1][:, hs], sc[n % 2][:, h, :], Z(2)[:, n, hs], stop=(n == 0))
                            if n:
                                mm(pb[1][:, hs], qc[:, h, tok], st[:, h, :], start=False)
                            t = mm(pb[2][:, hs], rot[1][:, n, hs], Z(2)[:, n, hs])
                        t.then_inc(pe_for_dve, 1)
                        if n >= 2:
                            pe.wait_ge(decode_added, 2 * (n - 1))
                        for h in range(2 * (n % 2), 2 * (n % 2) + 2):
                            hs = slice(h * P, (h + 1) * P)
                            t = mm(pb[4 + h], rot[1][0:DEC, MT, hs], vmask[0:DEC, 4 * (n // 2):4 * (n // 2) + 4, hs])
                        t.then_inc(pe_for_dve, 1)
                    pe.wait_ge(decode_added, 2 * MT)
                    c["pe_from_dve"].skip(1)
                    for b in range(DEC):
                        for h in range(HA):
                            t = mm(pb[0][:, h * DEC + b:h * DEC + b + 1], dstate[:, b // 4, b % 4, h, :],
                                   qkT[:, h, SEQ + b:SEQ + b + 1])
                    t.then_inc(pe_for_dve, 1)
                    pe.wait_ge(dve_for_pe, c["pe_from_dve"].next())
                    for h in range(HA):
                        t = tr(pb[1][0:DEC, h * P:(h + 1) * P], od[:, h, :])
                    t.then_inc(pe_for_dve, 1)

                @block.sync
                def _(sp):
                    sr = L("state_ret").rearrange("b h d e -> d b h e")
                    so = Lo(ret_s).rearrange("b h d e -> d b h e")
                    for b in range(DEC):
                        sp.dma_start(dstate[:, b // 4, b % 4], sr[:, b]).then_inc(loaded, 16)
                    sp.wait_ge(dve_for_sp, c["sp_from_dve"].next())
                    sp.dma_start(Lo(ret_p).rearrange("o h d e -> d (o h) e"), st).then_inc(stored, 16)
                    for b in range(DEC):
                        sp.dma_start(so[:, b], dstate[:, b // 4, b % 4]).then_inc(stored, 16)
            c["loaded"].skip(16 * DEC)

            def head_rms(v, dv, o, sq, ms, groups, width):
                dv(V.tensor_tensor(sq, o, o, mult))
                dv(V.tensor_reduce(ms, sq.rearrange("p m (g d) -> p (m g) d", d=width), AX.X, add))
                V.sem_inc(dve_for_act, 1)
                v.wait_ge(act_for_dve, c["dve_from_act"].next())
                dv(V.reciprocal(ms, ms))
                og = o.rearrange("p m (g d) -> p (m g) d", d=width)
                dv(V.tensor_tensor(og, og, bc(ms, [P, groups, width], 2), mult))

            def act_root(s, ms, width):
                s.wait_ge(dve_for_act, c["act_from_dve"].next())
                c["act"](S.activation(ms, ms, ACT.Sqrt, bias=eps, scale=1.0 / width))
                S.sem_inc(act_for_dve, 1)

            with nc.Block() as block:
                oa = at(x_raw, 0, 5, 512)
                sg = at(arena, 10240, 5, 512)
                sq = at(arena, 12800, 5, 512)
                ms = small[:, 160:180]
                pe_part, dve_part = heads_to_columns(None, [oa], yT)

                @block.sync
                def _(sp):
                    prefetch(sp, w_in[:, DIFF0:DIFF0 + 512], w_in[:, DIFF0 + 512:DIFF0 + 1024])
                    sp.wait_ge(stored, c["stored"].next(16 + 16 * DEC))

                @block.scalar
                def _(s):
                    c["act"](S.activation(sg, Z(3), ACT.Sigmoid))
                    act_root(s, ms, DA)

                @block.vector
                def _(v):
                    dv = c["dve"]
                    head_rms(v, dv, oa, sq, ms, 20, DA)
                    dv(V.tensor_tensor(sg, sg, Z(3), mult))
                    dv(V.tensor_tensor(oa, oa, sg, mult))
                    dve_part(v)

                @block.tensor
                def _(pe):
                    pe_part(pe)

            token_major(DIFF0, 3, 0)
            zq, zk, zv = Z(0), Z(1), Z(2)
            qkT2 = at(arena, 10240, 8, T)
            biasT = at(arena, 14912, HB, SEQ)
            with nc.Block() as block:
                sq = at(arena, 7680, 5, 512)
                ms = [small[:, 160:200], small[:, 200:240]]
                pe_part, dve_part = heads_to_columns(None, [zq, zk], qkT2)

                @block.vector
                def _(v):
                    dv = c["dve"]
                    dv(V.tensor_scalar(BR("qn"), BR("qn"), DB ** -0.5, None, mult))
                    for n, (z, g) in enumerate(((zq, "qn"), (zk, "kn"))):
                        head_rms(v, dv, z, sq, ms[n], 40, DB)
                        zg = z.rearrange("p m (g d) -> p (m g) d", d=DB)
                        dv(V.tensor_tensor(zg, zg, bc(BR(g), [P, 40, DB], 1), mult))
                    V.sem_inc(dve_for_sp, 1)
                    dve_part(v)

                @block.scalar
                def _(s):
                    for n in range(2):
                        act_root(s, ms[n], DB)

                @block.tensor
                def _(pe):
                    pe_part(pe)

                @block.sync
                def _(sp):
                    sp.dma_start(biasT, bass.AP(tensor=skew.tensor, offset=P - 1,
                                                ap=[[TOE - 1, P], [P * TOE, HB], [1, SEQ]])).then_inc(loaded, 16)
                    sp.wait_ge(loaded, c["loaded"].next(16))
                    sp.wait_ge(dve_for_sp, c["sp_from_dve"].next())
                    for z, op, os in ((zk, k_p, k_s), (zv, v_p, v_s)):
                        sp.dma_start(Lo(op).rearrange("o (m p) h d -> p (o m) (h d)", p=P), z[:, 0:MT, :]).then_inc(stored, 16)
                        sp.dma_start(Lo(os).rearrange("b o h d -> b (o h d)"), z[0:DEC, MT, :]).then_inc(stored, 16)
                    sp.wait_ge(stored, c["stored"].next(64))

            ob = at(arena, 0, 5, 512)
            w_ada_rest = L("w_ada")[:, 4 * 512:12 * 512]
            with nc.Block() as block:
                s_ = at(x_raw, 0, 2, 2, SEQ)
                p_ = at(arena, 7680, 2, 2, SEQ)
                aw = [at(arena, 9728, SEQ), at(x_raw, 2048, SEQ)]
                aT = [at(arena, 14400, MT, P), at(x_raw, 2560, MT, P)]
                units = [(h, qb) for h in range(HB) for qb in range(MT)]
                NU = len(units)

                def st8(n):
                    return small[:, 160 + n % 2 * 8:168 + n % 2 * 8]

                @block.sync
                def _(sp):
                    for q in range(2):
                        load_w(sp, q, w_ada_rest[:, q * 512:(q + 1) * 512])

                @block.vector
                def _(v):
                    dv = c["dve"]
                    for n in range(NU + 1):
                        if n < NU:
                            h, qb = units[n]
                            kw = (qb + 1) * P
                            sn, t8 = s_[:, n % 2], st8(n)
                            v.wait_ge(scores_ready, n + 1)
                            if n >= 2:
                                v.wait_ge(exp_ready, n - 1)
                            for cc in range(2):
                                V.tensor_tensor(sn[:, cc, 0:kw], pb[2 * (n % 2) + cc][:, 0:kw], biasT[:, h, SEQ - kw:SEQ],
                                                add).then_inc(scores_read, 1)
                            v.wait_ge(scores_read, 2 * (n + 1))
                            dv(V.tensor_reduce(t8[:, 0:2], sn[:, :, 0:kw], AX.X, amax))
                            V.tensor_scalar(t8[:, 2:4], t8[:, 0:2], -1.0, None, mult).then_inc(logits_ready, 1)
                        if n:
                            h, qb = units[n - 1]
                            kw = (qb + 1) * P
                            pn, t8 = p_[:, (n - 1) % 2], st8(n - 1)
                            v.wait_ge(exp_ready, n)
                            dv(V.reciprocal(t8[:, 6:8], t8[:, 4:6]))
                            dv(V.tensor_tensor(t8[:, 7:8], t8[:, 7:8], lam, mult))
                            dv(V.tensor_scalar(pn[:, 1, 0:kw], pn[:, 1, 0:kw], t8[:, 7:8], None, mult))
                            if n >= 3:
                                v.wait_ge(turned, n - 2)
                            V.scalar_tensor_tensor(aw[(n - 1) % 2][:, 0:kw], pn[:, 0, 0:kw], t8[:, 6:7], pn[:, 1, 0:kw],
                                                   mult, sub).then_inc(weights_ready, 1)
                            v.wait_ge(weights_ready, n)

                @block.scalar
                def _(s):
                    for n in range(NU + 2):
                        if n < NU:
                            kw = (units[n][1] + 1) * P
                            s.wait_ge(logits_ready, n + 1)
                            if n >= 2:
                                s.wait_ge(weights_ready, n - 1)
                            for cc in range(2):
                                t = S.activation(p_[:, n % 2, cc, 0:kw], s_[:, n % 2, cc, 0:kw], ACT.Exp,
                                                 bias=st8(n)[:, 2 + cc:3 + cc], accum_out=st8(n)[:, 4 + cc:5 + cc])
                            t.then_inc(exp_ready, 1)
                        if 1 <= n <= NU:
                            qb = units[n - 1][1]
                            s.wait_ge(turned, n)
                            if n >= 3:
                                s.wait_ge(values_ready, n - 2)
                            S.activation(aT[(n - 1) % 2][:, 0:qb + 1, :], at(pb[4 + (n - 1) % 2], 0, MT, P)[:, 0:qb + 1, :],
                                         ACT.Copy).then_inc(turned_read, 1)
                        if n >= 2:
                            h, qb = units[n - 2]
                            s.wait_ge(values_ready, n - 1)
                            S.activation(ob[:, qb, h * P:(h + 1) * P], pb[6 + n % 2][:, 0:P], ACT.Copy)\
                             .then_inc(values_read, 1)

                @block.tensor
                def _(pe):
                    for n in range(-1, NU + 2):
                        if n + 1 < NU:
                            h, qb = units[n + 1]
                            kw = (qb + 1) * P
                            if n >= 1:
                                pe.wait_ge(scores_read, 2 * n)
                            for cc in range(2):
                                r = slice(cc * DB, (cc + 1) * DB)
                                t = mm(pb[2 * ((n + 1) % 2) + cc][:, 0:kw], qkT2[r, h, qb * P:(qb + 1) * P], qkT2[r, 4 + h, 0:kw])
                            t.then_inc(scores_ready, 1)
                        if 1 <= n <= NU:
                            qb = units[n - 1][1]
                            pe.wait_ge(weights_ready, n)
                            if n >= 3:
                                pe.wait_ge(turned_read, n - 2)
                            for kb in range(qb + 1):
                                t = tr(pb[4 + (n - 1) % 2][:, kb * P:(kb + 1) * P], aw[(n - 1) % 2][:, kb * P:(kb + 1) * P])
                            t.then_inc(turned, 1)
                        if n >= 2:
                            h, qb = units[n - 2]
                            pe.wait_ge(turned_read, n - 1)
                            if n >= 4:
                                pe.wait_ge(values_read, n - 3)
                            for kb in range(qb + 1):
                                t = mm(pb[6 + n % 2][:, 0:P], aT[n % 2][:, kb, :], zv[:, kb, h * P:(h + 1) * P],
                                       start=(kb == 0), stop=(kb == qb))
                            t.then_inc(values_ready, 1)

            with nc.Block() as block:
                pg = [at(arena, 16384, NPG, 512), at(arena, 17408, NPG, 512)]
                prod = at(x_raw, 0, NPG, 512)
                scr = at(x_raw, 1024, NPG, DEC, 8)
                sown = at(x_raw, 1152, DEC, 8)
                srow = at(x_raw, 1216, PAST + 1)
                comb = at(x_raw, 1488, HB * DEC)
                comb2 = at(x_raw, 1520, HB * DEC)
                ap_ = at(x_raw, 1552, NPG, HB * DEC)
                aown = at(x_raw, 1616, HB * DEC)
                odT = at(x_raw, 1648, HB * DEC)
                zqd = at(x_raw, 1680, 512)
                st4 = small[:, 160:164]
                own = x_raw[0:DEC, 2192:2200]

                @block.sync
                def _(sp):
                    n = 0
                    for src in (a["cache_k_diff"], a["cache_v_diff"]):
                        for b in range(DEC):
                            if n >= 2:
                                sp.wait_ge(page_free, n - 1)
                            for g in range(NPG):
                                pid = sp.value_load(pages[0:1, b * NPG + g:b * NPG + g + 1], min_val=0,
                                                    max_val=a["cache_k_diff"].shape[1] - 1)
                                sp.dma_start(pg[b % 2][:, g, :], src[bass.ds(l, 1), bass.ds(pid, 1)]
                                             .rearrange("o g p h d -> p (o g h d)")).then_inc(page_full[b % 2], 16)
                            if n % 2 and 3 <= n <= 13:
                                q = (n + 1) // 2
                                load_w(sp, q % 2, w_ada_rest[:, q * 512:(q + 1) * 512])
                            n += 1

                @block.vector
                def _(v):
                    dv = c["dve"]
                    dv(V.tensor_copy(zqd[0:DEC, :], zq[0:DEC, MT, :]))
                    V.sem_inc(dve_for_pe, 1)
                    for b in range(DEC):
                        v.wait_ge(pe_for_dve, c["dve_from_pe"].next())
                        v.wait_ge(page_full[b % 2], 32 * (b // 2 + 1))
                        dv(V.tensor_tensor(prod, pg[b % 2], bc(pb[b % 2], [P, NPG, 512], 1), mult))
                        dv(V.tensor_reduce(scr[:, :, b, :], prod.rearrange("p g (x d) -> p g x d", d=DB), AX.X, add))
                        V.sem_inc(page_free, 1)
                        V.sem_inc(dve_for_pe, 1)
                    for g in range(NPG):
                        sg_ = scr[:, g].rearrange("p b (h c) -> p b h c", c=2)
                        dv(V.tensor_tensor(sg_, sg_, bc(biasD[:, g, :], [P, DEC, HB, 2], 1, 3), add))
                    dv(V.tensor_tensor(prod[0:DEC, 0, :], zqd[0:DEC, :], zk[0:DEC, MT, :], mult))
                    dv(V.tensor_reduce(own, prod[0:DEC, 0, :].rearrange("p (x d) -> p x d", d=DB), AX.X, add))
                    ow = own.rearrange("p (h c) -> p h c", c=2)
                    dv(V.tensor_tensor(ow, ow, bc(bias0[0:DEC], [DEC, HB, 2], 2), add))
                    dv(V.tensor_tensor(sown[0:DEC], bc(own, [DEC, DEC, 8], 1), bc(ident[0:DEC, 0:DEC], [DEC, DEC, 8], 2), mult))
                    V.sem_inc(dve_for_pe, 1)
                    v.wait_ge(pe_for_dve, c["dve_from_pe"].next())
                    dv(V.tensor_copy(srow[0:64], pb[0][0:64, 0:PAST + 1]))
                    dv(V.tensor_reduce(st4[0:64, 0:1], srow[0:64], AX.X, amax))
                    dv(V.tensor_scalar(st4[0:64, 1:2], st4[0:64, 0:1], -1.0, None, mult))
                    V.sem_inc(dve_for_act, 1)
                    v.wait_ge(act_for_dve, c["dve_from_act"].next())
                    dv(V.reciprocal(st4[0:64, 3:4], st4[0:64, 2:3]))
                    dv(V.tensor_scalar(srow[0:64], srow[0:64], st4[0:64, 3:4], None, mult))
                    dv(V.tensor_scalar(comb[0:64], C("c1")[0:64], lam[0:64], None, mult))
                    dv(V.tensor_tensor(comb[0:64], C("c0")[0:64], comb[0:64], sub))
                    dv(V.tensor_scalar(comb2[0:64], comb[0:64], srow[0:64, PAST:PAST + 1], None, mult))
                    V.sem_inc(dve_for_pe, 1)
                    v.wait_ge(pe_for_dve, c["dve_from_pe"].next())
                    dv(V.tensor_copy(ap_.rearrange("p g c -> p (g c)"), pb[1][:, 0:64]))
                    dv(V.tensor_copy(aown[0:DEC], pb[1][0:DEC, 64:96]))
                    V.sem_inc(dve_for_pe, 1)
                    for b in range(DEC):
                        v.wait_ge(pe_for_dve, c["dve_from_pe"].next())
                        V.sem_inc(page_free, 1)
                    dv(V.tensor_copy(odT, pb[2][:, 0:32]))
                    V.sem_inc(dve_for_pe, 1)
                    v.wait_ge(pe_for_dve, c["dve_from_pe"].next())
                    dv(V.tensor_copy(ob[0:DEC, MT, :], pb[3][0:DEC, :]))

                arows = at(x_raw, 2560, 2, 512)[0:9]

                @block.scalar
                def _(s):
                    def ada_copy(q):
                        s.wait_ge(ada_ready, q + 1)
                        if q >= 2:
                            s.wait_ge(ada_turned, q - 1)
                        S.activation(arows[:, q % 2], pb[4 + q % 2][0:9, :], ACT.Copy).then_inc(ada_copied, 1)
                        S.sem_inc(slot_free[q % 2], 1)

                    def ada_store(q):
                        s.wait_ge(ada_turned, q + 1)
                        S.activation(modT[:, 16 + 4 * q:20 + 4 * q, :], at(pb[6 + q % 2], 0, 4, 9), ACT.Copy)\
                         .then_inc(ada_read, 1)

                    ada_copy(0)
                    for q in range(1, 4):
                        ada_copy(q)
                        ada_store(q - 1)
                    s.wait_ge(dve_for_act, c["act_from_dve"].next())
                    c["act"](S.activation(srow[0:64], srow[0:64], ACT.Exp, bias=st4[0:64, 1:2],
                                          accum_out=st4[0:64, 2:3]))
                    S.sem_inc(act_for_dve, 1)
                    for q in range(4, 8):
                        ada_copy(q)
                        ada_store(q - 1)
                    ada_store(7)
                    s.wait_ge(ada_read, 8)

                @block.tensor
                def _(pe):
                    def ada_half(q, half):
                        if half == 0:
                            pe.wait_ge(slot_full[q % 2], c["pe_full"][q % 2].next(16))
                            if q >= 2:
                                pe.wait_ge(ada_copied, q - 1)
                        w = wslot(q % 2)
                        for k in range(4 * half, 4 * half + 4):
                            t = mm(pb[4 + q % 2][0:9, :], csT[:, k, :], w[:, k, :], start=(k == 0), stop=(k == KD - 1))
                        if half:
                            t.then_inc(ada_ready, 1)

                    def ada_turn(q):
                        pe.wait_ge(ada_copied, q + 1)
                        if q >= 2:
                            pe.wait_ge(ada_read, q - 1)
                        for ct in range(4):
                            t = tr(pb[6 + q % 2][:, ct * 9:ct * 9 + 9], arows[:, q % 2, ct * P:(ct + 1) * P])
                        t.then_inc(ada_turned, 1)

                    pe.wait_ge(dve_for_pe, c["pe_from_dve"].next())
                    for b in range(DEC):
                        if b >= 2:
                            pe.wait_ge(dve_for_pe, c["pe_from_dve"].next())
                        mm(pb[b % 2], ident[0:DEC, b:b + 1].broadcast_to([DEC, P]), zqd[0:DEC, :]).then_inc(pe_for_dve, 1)
                        ada_half(b // 2, b % 2)
                        if b % 2 and b > 1:
                            ada_turn(b // 2 - 1)
                    ada_half(4, 0)
                    pe.wait_ge(dve_for_pe, c["pe_from_dve"].next(3))
                    for g in range(NPG):
                        tr(pb[0][0:64, g * P:(g + 1) * P], scr[:, g].rearrange("p b x -> p (b x)"))
                    mm(pb[0][0:64, PAST:PAST + 1], sown[0:DEC].rearrange("p b x -> p (b x)"),
                       ones[0:DEC, 0:1]).then_inc(pe_for_dve, 1)
                    ada_half(4, 1)
                    ada_turn(3)
                    pe.wait_ge(dve_for_pe, c["pe_from_dve"].next())
                    for g in range(NPG):
                        mm(pb[1][:, g * 32:(g + 1) * 32], srow[0:64, g * P:(g + 1) * P], comb[0:64])
                    mm(pb[1][0:DEC, 64:96], C("selb")[0:64], comb2[0:64]).then_inc(pe_for_dve, 1)
                    pe.wait_ge(dve_for_pe, c["pe_from_dve"].next())
                    for h in range(HB):
                        mm(pb[2][:, h * DEC:(h + 1) * DEC], zv[0:DEC, MT, h * P:(h + 1) * P],
                           aown[0:DEC, h * DEC:(h + 1) * DEC], start=(h == 0), stop=False)
                    for b in range(DEC):
                        pe.wait_ge(page_full[b % 2], 32 * (DEC // 2 + b // 2 + 1))
                        for h in range(HB):
                            for g in range(NPG):
                                t = mm(pb[2][:, h * DEC + b:h * DEC + b + 1], pg[b % 2][:, g, h * P:(h + 1) * P],
                                       ap_[:, g, h * DEC + b:h * DEC + b + 1], start=False, stop=(b == DEC - 1))
                        t.then_inc(pe_for_dve, 1)
                        if b < 6:
                            ada_half(5 + b // 2, b % 2)
                            if b % 2:
                                ada_turn(4 + b // 2)
                    ada_turn(7)
                    pe.wait_ge(dve_for_pe, c["pe_from_dve"].next())
                    for h in range(HB):
                        t = tr(pb[3][0:DEC, h * P:(h + 1) * P], odT[:, h * DEC:(h + 1) * DEC])
                    t.then_inc(pe_for_dve, 1)

            with nc.Block() as block:
                sq = at(arena, 7680, 5, 512)
                ms = small[:, 160:180]
                pe_part, dve_part = heads_to_columns(None, [ob], yT[:, 4:8, :])

                @block.sync
                def _(sp):
                    prefetch(sp, w_in[:, RW0:RW0 + 512], w_in[:, RW0 + 512:RW0 + 1024])

                @block.scalar
                def _(s):
                    act_root(s, ms, DVB)

                @block.vector
                def _(v):
                    dv = c["dve"]
                    V.tensor_tensor(modT[:, 16:48], modT[:, 16:48], bc(PR("b_ada")[:, 16:48], [P, 32, 9], 2), add)
                    head_rms(v, dv, ob, sq, ms, 20, DVB)
                    og = ob.rearrange("p m (g d) -> p (m g) d", d=DVB)
                    dv(V.tensor_tensor(og, og, bc(BR("subln"), [P, 20, DVB], 1), mult))
                    dve_part(v)

                @block.tensor
                def _(pe):
                    pe_part(pe)

            z = at(arena, 0, RT, T)
            zs = at(arena, 7800, RT, T)
            slab = [at(arena, n * 2080, HP, T) for n in range(3)]
            z0, z1, z2 = slab
            y3 = yT[:, 8:12, :]
            r_, k_, v_ = zs[:, 0:4, :], zs[:, 4:8, :], zs[:, 8:12, :]
            wdad, gd = zs[:, 12, :], zs[:, 13:15, :]
            w_up2 = ring[1][:, 0:512]
            w_g1, w_g2 = ring[1][:, 512:1024], ring[1][0:32, 1024:1536]
            w_vu = ring[1][0:32, 1536:2048]
            w_vd = at(ring[1], 2048, HP, 32)
            with nc.Block() as block:
                @block.sync
                def _(sp):
                    for b in range(2, 4):
                        c0 = RW0 + 512 * b
                        load_w(sp, b % 2, w_in[:, c0:min(c0 + 512, GATE0)])

                @block.tensor
                def _(pe):
                    for n in range(8):
                        fm_unit(pe, w_split, n, hT[0], hT[1], n % 2 * 4, c["pe_from_act"], pe_for_act,
                                n_tiles=4 if n < 6 else 3, first=(n % 2 == 0), last=(n % 2 == 1))
                    c["pe_from_act"].skip(4)

                @block.scalar
                def _(s):
                    S.sem_inc(act_for_pe, 4)
                    split_hi(s, w_split, 0, 0, 0)
                    split_hi(s, w_split, 1, 0, 1, first=False)
                    for b in range(4):
                        s.wait_ge(split_free, c["split_free"].next())
                        if b < 3:
                            split_hi(s, w_split, 2 * b + 2, (b + 1) % 2, 0)
                        for ct in range(4 if b < 3 else 3):
                            mc = 32 if b == 3 and ct == 2 else P
                            s.wait_ge(pe_for_act, c["act_from_pe"].next())
                            for half in range(2):
                                c["act"](S.activation(z[0:mc, 4 * b + ct, half * TH:(half + 1) * TH],
                                                      pb[4 * half + ct][0:mc, 0:TH], ACT.Copy))
                            S.sem_inc(act_for_pe, 1)
                        if b < 3:
                            split_hi(s, w_split, 2 * b + 3, (b + 1) % 2, 1, first=False)

                @block.vector
                def _(v):
                    for n in range(8):
                        split_lo(v, w_split, n, n // 2 % 2, n % 2, last=(n % 2 == 1))

            prev_rows = arena[0:DEC, 15600:15600 + RT * P]
            prevT = at(arena, 17520, RT, DEC)
            last_rows = ring[0][0:9, 2048:2048 + RT * P]
            dvec = at(arena, 6760, 5, HP, DEC)
            tokv = [x.rearrange("p (n c) -> p n c", n=5) for x in tok_split]
            bonus = at(small, 200, 5, HC)
            dend = at(small, 256, HP, 8)
            yd = at(small, 288, HP, DEC)
            vdn = at(arena, 6240, T)
            vkeep = at(arena, 15600, HP, T)
            kk = at(x_raw, 0, HP, T)
            work = at(x_raw, HP * T, HP, T)
            ds_ = at(ring[0], 0, DEC, HP, DC)
            with nc.Block() as block:
                @block.sync
                def _(sp):
                    sp.dma_start(prev_rows[:, 0:RW], L("state_shift").rearrange("b o c -> b (o c)")).then_inc(loaded, 16)
                    sp.dma_start(w_up2[0:64, :], L("w_decay_up")).then_inc(loaded, 16)
                    sp.dma_start(w_up2[64:128, :], L("w_a_up")).then_inc(loaded, 16)
                    wg = L("w_g_up")
                    sp.dma_start(w_g1, wg[0:P, :]).then_inc(loaded, 16)
                    sp.dma_start(w_g2, wg[P:160, :]).then_inc(loaded, 16)
                    sp.dma_start(w_vu, a["w_v_up"][0]).then_inc(loaded, 16)
                    sp.dma_start(w_vd, a["w_v_down"][0].rearrange("(k p) n -> p k n", p=P)).then_inc(loaded, 16)
                    sp.dma_start(y3.rearrange("p k t -> p (k t)"), v_spill).then_inc(loaded, 16)
                    sr = L("state_rwkv").rearrange("b (q g) i j -> g i b q j", g=2)
                    for g in range(2):
                        for b in range(DEC):
                            sp.dma_start(ds_[g * 64:(g + 1) * 64, b], sr[g, :, b]).then_inc(states_loaded, 16)
                    sp.wait_ge(dve_for_sp, c["sp_from_dve"].next())
                    sp.dma_start(Lo(shift_p).rearrange("b o c -> b (o c)"), last_rows[0:1, 0:RW]).then_inc(stored, 16)
                    sp.dma_start(Lo(shift_s).rearrange("b o c -> b (o c)"), last_rows[1:9, 0:RW]).then_inc(stored, 16)
                    sp.wait_ge(dve_for_sp, c["sp_from_dve"].next())
                    sp.dma_start(v_spill, arena[:, 15600:15600 + HP * T]).then_inc(stored, 16)
                    sp.wait_ge(stored, c["stored"].next(48))

                @block.tensor
                def _(pe):
                    credit = c["pe_from_act"]
                    pe.wait_ge(loaded, c["loaded"].base + 128)
                    for t in range(RT):
                        mc = P if t < 14 else 32
                        tr(pb[0][0:mc, t * DEC:(t + 1) * DEC], prev_rows[:, t * P:t * P + mc])
                    for t in range(RT):
                        mc = P if t < 14 else 32
                        i = tr(pb[1 + t // 4][0:9, (t % 4) * P:(t % 4) * P + mc], z[0:mc, t, SEQ - 1:T])
                    i.then_inc(pe_for_dve, 1)

                    def up_tile(lhs, rows_, rhs, ct):
                        for half in range(2):
                            t = mm(pb[4 * half + ct][:, 0:TH], lhs[rows_, ct * P:(ct + 1) * P],
                                   rhs[rows_, half * TH:(half + 1) * TH])
                        t.then_inc(pe_for_act, 1)

                    pe.wait_ge(act_for_pe, credit.next())
                    for ct in range(HP):
                        up_tile(w_up2, slice(0, 64), wdad, ct)
                    for ct in range(HP):
                        pe.wait_ge(act_for_pe, credit.next())
                        up_tile(w_up2, slice(64, 128), wdad, ct)
                    pe.wait_ge(dve_for_pe, c["pe_from_dve"].next())
                    for ct in range(HP):
                        pe.wait_ge(act_for_pe, credit.next())
                        for half in range(2):
                            t = mm(pb[4 * half + ct][:, 0:TH], blk, work[:, ct, half * TH:(half + 1) * TH])
                        t.then_inc(pe_for_act, 1)
                    pe.wait_ge(dve_for_pe, c["pe_from_dve"].next())
                    pe.wait_ge(act_for_pe, credit.next())
                    for k in range(HP):
                        for half in range(2):
                            t = mm(pb[4 * half][0:32, 0:TH], w_vd[:, k, :], v_[:, k, half * TH:(half + 1) * TH],
                                   start=(k == 0), stop=(k == HP - 1))
                    t.then_inc(pe_for_act, 1)
                    pe.wait_ge(act_for_pe, credit.next(4))
                    for ct in range(HP):
                        up_tile(w_vu, slice(0, 32), vdn, ct)
                    pe.wait_ge(dve_for_pe, c["pe_from_dve"].next())
                    pe.wait_ge(act_for_pe, credit.next(4))
                    for m in range(5):
                        r = P if m < MT else DEC
                        for hp in range(HP):
                            t = mm(pb[5][0:r, m * 8 + hp * 2:m * 8 + hp * 2 + 2], y3[:, hp, m * P:m * P + r], C("pair"))
                    t.then_inc(pe_for_dve, 1)
                    pe.wait_ge(dve_for_pe, c["pe_from_dve"].next())
                    for n in range(5):
                        for hp in range(HP):
                            t = tr(pb[n][0:DEC, hp * P:(hp + 1) * P], dvec[:, n, hp, :])
                    t.then_inc(pe_for_dve, 1)

                @block.scalar
                def _(s):
                    ac = c["act"]

                    def tiles(dst, fn, name=None):
                        for ct in range(HP):
                            s.wait_ge(pe_for_act, c["act_from_pe"].next())
                            for half in range(2):
                                hs = slice(half * TH, (half + 1) * TH)
                                if name:
                                    ac(S.activation(dst[:, ct, hs], pb[4 * half + ct][:, 0:TH], fn,
                                                    bias=PR(name)[:, ct:ct + 1]))
                                else:
                                    ac(S.activation(dst[:, ct, hs], pb[4 * half + ct][:, 0:TH], fn))
                            S.sem_inc(act_for_pe, 1)
                        S.sem_inc(act_for_dve, 1)

                    s.wait_ge(dve_for_act, c["act_from_dve"].next())
                    ac(S.activation(wdad[0:64], wdad[0:64], ACT.Tanh))
                    S.sem_inc(act_for_pe, 1)
                    s.wait_ge(dve_for_act, c["act_from_dve"].next())
                    tiles(z0, ACT.Sigmoid, "w0")
                    s.wait_ge(dve_for_act, c["act_from_dve"].next())
                    tiles(z1, ACT.Sigmoid, "a0")
                    tiles(work, ACT.Sqrt)
                    s.wait_ge(dve_for_act, c["act_from_dve"].next())
                    s.wait_ge(pe_for_act, c["act_from_pe"].next())
                    for half in range(2):
                        ac(S.activation(vdn[0:32, half * TH:(half + 1) * TH], pb[4 * half][0:32, 0:TH], ACT.Copy))
                    S.sem_inc(act_for_pe, 1)
                    tiles(z2, ACT.Sigmoid, "v0")
                    ac(S.activation(gd[:, 0], gd[:, 0], ACT.Sigmoid))
                    ac(S.activation(gd[0:32, 1], gd[0:32, 1], ACT.Sigmoid))
                    s.wait_ge(dve_for_act, c["act_from_dve"].next())
                    ac(S.activation(dvec[:, 0], dvec[:, 0], ACT.Exp))
                    ac(S.activation(z0, z0, ACT.Exp))
                    S.sem_inc(act_for_dve, 1)
                    s.wait_ge(dve_for_act, c["act_from_dve"].next())
                    ac(S.activation(z0, work, ACT.Exp, scale=-1.0))
                    S.sem_inc(act_for_dve, 1)
                    ac(S.activation(work, work, ACT.Exp))
                    S.sem_inc(act_for_dve, 1)

                @block.vector
                def _(v):
                    dv = c["dve"]
                    vm = C("vmix", DEPTH)[:, bass.ds(l, 1)]

                    def shift(t0, t1):
                        for t in range(t0, t1):
                            mc = P if t < 14 else 32
                            t_ = V.scalar_tensor_tensor(zs[0:mc, t, :], zs[0:mc, t, :], PR("mu")[0:mc, t:t + 1], z[0:mc, t, :], mult, add)
                        dv(t_)

                    for lo, hi, mc in ((0, 14, P), (14, 15, 32)):
                        V.tensor_tensor(zs[0:mc, lo:hi, 1:SEQ], z[0:mc, lo:hi, 0:SEQ - 1], z[0:mc, lo:hi, 1:SEQ], sub)
                        V.tensor_scalar(zs[0:mc, lo:hi, 0:1], z[0:mc, lo:hi, 0:1], -1.0, None, mult)
                    v.wait_ge(pe_for_dve, c["dve_from_pe"].next())
                    V.tensor_copy(prevT[:, 0:14], at(pb[0], 0, 14, DEC))
                    dv(V.tensor_copy(prevT[0:32, 14], pb[0][0:32, 14 * DEC:15 * DEC]))
                    V.tensor_tensor(zs[0:32, 14:15, SEQ:T], prevT[0:32, 14:15], z[0:32, 14:15, SEQ:T], sub)
                    dv(V.tensor_tensor(zs[:, 0:14, SEQ:T], prevT[:, 0:14], z[:, 0:14, SEQ:T], sub))
                    for g in range(4):
                        w_ = 512 if g < 3 else RW - 1536
                        t_ = V.tensor_copy(last_rows[:, g * 512:g * 512 + w_], pb[1 + g][0:9, 0:w_])
                    dv(t_)
                    V.sem_inc(dve_for_sp, 1)
                    shift(12, 13)
                    V.sem_inc(dve_for_act, 1)
                    shift(0, 4)
                    V.sem_inc(dve_for_act, 1)
                    shift(4, 8)
                    V.sem_inc(dve_for_act, 1)
                    for ct in range(HP):
                        t_ = V.tensor_scalar(kk[:, ct], k_[:, ct], PR("k_k")[:, ct:ct + 1], None, mult)
                    dv(t_)
                    dv(V.tensor_tensor(work, kk, kk, mult))
                    V.sem_inc(dve_for_pe, 1)
                    shift(8, 12)
                    V.sem_inc(dve_for_pe, 1)
                    shift(13, 15)
                    V.sem_inc(dve_for_act, 1)
                    v.wait_ge(loaded, c["loaded"].base + 128)
                    dv(V.tensor_tensor(y3, y3, v_, sub))
                    dv(V.scalar_tensor_tensor(vkeep, y3, vm, v_, mult, add))
                    V.sem_inc(dve_for_sp, 1)
                    v.wait_ge(act_for_dve, c["dve_from_act"].next())
                    dv(V.tensor_scalar(z0, z0, -math.exp(-0.5), None, mult))
                    v.wait_ge(act_for_dve, c["dve_from_act"].next())
                    for ct in range(HP):
                        ka = PR("k_a")[:, ct:ct + 1]
                        dv(V.tensor_scalar(rstd, z1[:, ct], ka, ka, mult, sub))
                        dv(V.scalar_tensor_tensor(k_[:, ct], rstd, 1.0, k_[:, ct], add, mult))
                    v.wait_ge(act_for_dve, c["dve_from_act"].next())
                    dv(V.tensor_scalar(work, work, 1e-12, None, amax))
                    dv(V.reciprocal(work, work))
                    dv(V.tensor_tensor(kk, kk, work, mult))
                    for ct in range(HP):
                        t_ = V.tensor_tensor_scan(work[:, ct], C("scan"), z0[:, ct], 0.0, mult, add)
                    dv(t_)
                    dv(V.tensor_copy(dvec[:, 0], z0[:, :, SEQ:T]))
                    dv(V.tensor_tensor(z0, work, z0, sub))
                    V.sem_inc(dve_for_act, 1)
                    dv(V.tensor_tensor(z1, z1, kk, mult))
                    v.wait_ge(act_for_dve, c["dve_from_act"].next())
                    dv(V.scalar_tensor_tensor(y3, z2, vm, y3, mult, mult))
                    dv(V.tensor_tensor(v_, v_, y3, add))
                    for ct in range(HP):
                        t_ = V.scalar_tensor_tensor(y3[:, ct], r_[:, ct], PR("r_k")[:, ct:ct + 1], k_[:, ct], mult, mult)
                    dv(t_)
                    V.sem_inc(dve_for_pe, 1)
                    V.tensor_copy(dvec[:, 1], k_[:, :, SEQ:T])
                    V.tensor_scalar(dvec[:, 2], kk[:, :, SEQ:T], -1.0, None, mult)
                    V.tensor_copy(dvec[:, 3], z1[:, :, SEQ:T])
                    dv(V.tensor_copy(dvec[:, 4], r_[:, :, SEQ:T]))
                    v.wait_ge(act_for_dve, c["dve_from_act"].next())
                    V.sem_inc(dve_for_pe, 1)
                    dv(V.scalar_tensor_tensor(z2, kk, -1.0, z0, mult, mult))
                    V.sem_inc(dve_for_act, 1)
                    v.wait_ge(pe_for_dve, c["dve_from_pe"].next())
                    V.tensor_copy(bonus[:, 0:MT], at(pb[5], 0, MT, HC))
                    dv(V.tensor_copy(bonus[0:DEC, MT], pb[5][0:DEC, MT * 8:MT * 8 + 8]))
                    v.wait_ge(act_for_dve, c["dve_from_act"].next())
                    V.tensor_tensor(z1, z1, z0, mult)
                    dv(V.tensor_tensor(k_, k_, z0, mult))
                    v.wait_ge(act_for_dve, c["dve_from_act"].next())
                    V.tensor_copy(dend, work[:, :, CH - 1:SEQ:CH])
                    dv(V.tensor_tensor(r_, r_, work, mult))
                    v.wait_ge(pe_for_dve, c["dve_from_pe"].next())
                    for n in (2, 0, 3, 1, 4):
                        dv(V.tensor_copy(tokv[0][0:DEC, n], pb[n][0:DEC, :]))
                        dv(V.tensor_tensor(tokv[1][0:DEC, n], pb[n][0:DEC, :], tokv[0][0:DEC, n].bitcast(F32), sub))
            c["loaded"].skip(128)

            ytok = at(x_raw, 0, 5, 512)
            vtok = at(arena, 15600, 5, 512)
            btok = at(arena, 0, MT, 512)
            ktok = at(arena, 11960, MT, 512)
            stb = at(arena, 14040, HP, P)
            turns = ([(v_, m * P, vtok[:, m]) for m in range(MT)] + [(v_, SEQ, vtok[0:DEC, MT])]
                     + [(z1, m * P, btok[:, m]) for m in range(MT)] + [(k_, m * P, ktok[:, m]) for m in range(MT)])
            with nc.Block() as block:
                t1 = at(ring[0], 2048, 2, HP, DC)
                u = at(small, 320, 2, HP)

                def spread(b, n):
                    return pb[3 * (b % 2) + n // 2][:, n % 2 * 256:(n % 2 + 1) * 256]

                @block.sync
                def _(sp):
                    so = Lo(rwkv_s).rearrange("b (q g) i j -> g i b q j", g=2)
                    for b in range(DEC):
                        sp.wait_ge(dve_for_sp, c["sp_from_dve"].next())
                        for g in range(2):
                            sp.dma_start(so[g, :, b], ds_[g * 64:(g + 1) * 64, b]).then_inc(stored, 16)

                @block.tensor
                def _(pe):
                    def turn_tile(n):
                        src, first, dst = turns[n]
                        if n >= 2:
                            pe.wait_ge(act_for_pe, c["pe_from_act"].next())
                        for hp in range(HP):
                            t = tr(pb[6 + n % 2][0:dst.shape[0], hp * P:(hp + 1) * P], src[:, hp, first:first + dst.shape[0]])
                        t.then_inc(pe_for_act, 1)

                    pe.wait_ge(act_for_pe, c["pe_from_act"].next())
                    for b in range(DEC):
                        if b >= 2:
                            pe.wait_ge(dve_for_pe, c["pe_from_dve"].next())
                        for n in (2, 0, 3, 1, 4):
                            for g in (1, 0):
                                for x in range(2):
                                    row = tokv[x][0:DEC, n, :].rearrange("b (q g j) -> b g q j", g=2, j=DC)
                                    t = mm(spread(b, n)[0:(g + 1) * 64],
                                           tok_place[0:DEC, b, (1 - g) * 64:P], row[:, g],
                                           start=(g == 1 and x == 0), stop=(g == 0 and x == 1))
                        t.then_inc(pe_for_dve, 1)
                        turn_tile(b)
                    turn_tile(DEC)
                    pe.wait_ge(dve_for_pe, c["pe_from_dve"].next(3))
                    for hp in range(HP):
                        t = tr(pb[0][0:DEC, hp * P:(hp + 1) * P], yd[:, hp, :])
                    t.then_inc(pe_for_dve, 1)
                    for n in range(DEC + 1, len(turns)):
                        turn_tile(n)
                    c["pe_from_act"].skip(2)

                @block.scalar
                def _(s):
                    S.activation(tok_place[0:DEC, :, 0:64], bc(ident[0:DEC, 0:DEC], [DEC, DEC, 64], 2), ACT.Copy, scale=0.0)
                    c["act"](S.activation(tok_place[0:DEC, :, 64:P], bc(ident[0:DEC, 0:DEC], [DEC, DEC, 64], 2), ACT.Copy))
                    S.sem_inc(act_for_pe, 1)
                    c["act"](S.activation(at(vtok[:, MT], 0, 4, P), bc(ident, [P, 4, P], 1), ACT.Copy, scale=0.0))
                    for n, (src, first, dst) in enumerate(turns):
                        s.wait_ge(pe_for_act, c["act_from_pe"].next())
                        if n == DEC + 1:
                            s.wait_ge(dve_for_act, c["act_from_dve"].next())
                        c["act"](S.activation(dst, pb[6 + n % 2][0:dst.shape[0]], ACT.Copy))
                        S.sem_inc(act_for_pe, 1)

                @block.vector
                def _(v):
                    dv = c["dve"]
                    dv(V.memset(stb, 0.0))
                    v.wait_ge(states_loaded, 256)
                    for b in range(DEC):
                        st = ds_[:, b]
                        w3, k3, a3, b3, r3 = (spread(b, n).rearrange("p (q j) -> p q j", q=HP) for n in range(5))
                        ub = u[:, b % 2]
                        vv = v_[:, :, SEQ + b:SEQ + b + 1].rearrange("p q o -> p (q o)")
                        v.wait_ge(pe_for_dve, c["dve_from_pe"].next())
                        V.tensor_tensor(t1[:, 1], k3, bc(vv, [P, HP, DC], 2), mult)
                        dv(V.tensor_tensor(t1[:, 0], st, a3, mult))
                        V.tensor_tensor(st, st, w3, mult)
                        dv(V.tensor_reduce(ub, t1[:, 0], AX.X, add))
                        dv(V.tensor_tensor(t1[:, 0], b3, bc(ub, [P, HP, DC], 2), mult))
                        dv(V.tensor_tensor(t1[:, 0], t1[:, 0], t1[:, 1], add))
                        dv(V.tensor_tensor(st, st, t1[:, 0], add))
                        V.sem_inc(dve_for_sp, 1)
                        dv(V.tensor_tensor(t1[:, 0], st, r3, mult))
                        V.sem_inc(dve_for_pe, 1)
                        dv(V.tensor_reduce(yd[:, :, b:b + 1].rearrange("p q o -> p (q o)"), t1[:, 0], AX.X, add))
                    V.sem_inc(dve_for_pe, 1)
                    V.sem_inc(dve_for_act, 1)
                    v.wait_ge(pe_for_dve, c["dve_from_pe"].next())
                    dv(V.tensor_copy(ytok[0:DEC, MT], pb[0][0:DEC, :]))

            m_ba, m_br, m_ka, m_kr = (at(ring[0], n * 1024, 2, HP, P) for n in range(4))
            xt = at(arena, 6240, 2, HP, P)
            xm = at(y_raw, 8 * T, 2, HP, P)
            m1 = at(y_raw, 8 * T + 1024, 2, HP, P)
            rhs1 = ring[1][:, 3200:3712]
            uu = arena[:, 7264:7776]
            keep = C("keep", 2, P)
            level = C("level", 6, P)
            states_stored = c["stored"].next(256)
            with nc.Block() as block:
                @block.tensor
                def _(pe):
                    turn = c["pe_from_dve"]

                    def products(left, right, m, bank, g):
                        gs, tok = slice(g * 64, (g + 1) * 64), slice(m * P, (m + 1) * P)
                        for hp in range(HP):
                            t = mm(pb[bank + g][:, hp * P:(hp + 1) * P], left[gs, hp, tok], right[gs, hp, tok])
                        return t

                    for left, right, bank in ((z1, z2, 4), (z1, r_, 6)):
                        products(left, right, 0, bank, 0)
                        products(left, right, 0, bank, 1).then_inc(pe_for_dve, 1)
                    pe.wait_ge(dve_for_pe, turn.next())
                    for m in range(MT):
                        for lv in range(6):
                            for g in range(2):
                                if lv:
                                    pe.wait_ge(dve_for_pe, turn.next())
                                for hp in range(HP):
                                    t = mm(pb[g][:, hp * P:(hp + 1) * P], m_ba[:, g, hp, :],
                                           ident if lv == 0 else xm[:, g, hp, :])
                                t.then_inc(pe_for_dve, 1)
                            if lv == 0:
                                if m:
                                    pe.wait_ge(dve_for_pe, turn.next())
                                    pe.wait_ge(act_for_pe, c["pe_from_act"].next())
                                products(k_, z2, m, 2, 0)
                                products(k_, z2, m, 2, 1).then_inc(pe_for_dve, 1)
                            for g in range(2):
                                pe.wait_ge(dve_for_pe, turn.next())
                                for hp in range(HP):
                                    hs = slice(hp * P, (hp + 1) * P)
                                    t = mm(pb[4 + g][:, hs], m1[:, g, hp, :], ident if lv == 0 else xt[:, g, hp, :])
                                    if 0 < lv < 5:
                                        t = mm(pb[2 + g][:, hs], xt[:, g, hp, :], m1[:, g, hp, :])
                                t.then_inc(pe_for_dve, 1)
                            if lv == 0:
                                pe.wait_ge(dve_for_pe, turn.next())
                                products(k_, r_, m, 6, 0)
                                products(k_, r_, m, 6, 1).then_inc(pe_for_dve, 1)
                        for cc in range(2):
                            r = slice(cc * 64, (cc + 1) * 64)
                            tk = slice(m * P + cc * 64, m * P + (cc + 1) * 64)
                            hsl = [slice(h * 64, (h + 1) * 64) for h in range(HC)]
                            ahead = (z1, (z2, r_)[cc], m + 1, 4 + 2 * cc)
                            pe.wait_ge(dve_for_pe, turn.next())
                            for hp in range(HP):
                                mm(pb[0][r, hp * P:(hp + 1) * P], z2[:, hp, tk], stb[:, hp, :], start=(hp == 0), stop=False)
                            for h in range(HC):
                                t = mm(pb[0][r, hsl[h]], m_ka[r, h % 2, h // 2, r], vtok[r, m, hsl[h]], start=False)
                            t.then_inc(pe_for_dve, 1)
                            if m + 1 < MT:
                                products(*ahead, 0)
                            pe.wait_ge(dve_for_pe, turn.next())
                            for h in range(HC):
                                t = mm(pb[1][r, hsl[h]], xt[r, h % 2, h // 2, r], rhs1[r, hsl[h]])
                            t.then_inc(pe_for_dve, 1)
                            if m + 1 < MT:
                                products(*ahead, 1).then_inc(pe_for_dve, 1)
                            pe.wait_ge(dve_for_pe, turn.next())
                            for hp in range(HP):
                                hs = slice(hp * P, (hp + 1) * P)
                                mm(pb[3][:, hs], btok[r, m, hs], uu[r, hs], stop=False)
                                t = mm(pb[3][:, hs], ktok[r, m, hs], vtok[r, m, hs], start=False)
                            if cc:
                                pe.wait_ge(act_for_pe, c["pe_from_act"].next())
                            for hp in range(HP):
                                t = mm(pb[2][r, hp * P:(hp + 1) * P], r_[:, hp, tk], stb[:, hp, :], start=(hp == 0), stop=False)
                            t.then_inc(pe_for_dve, 1)
                            for h in range(HC):
                                mm(pb[2][r, hsl[h]], m_br[r, h % 2, h // 2, r], uu[r, hsl[h]], start=False, stop=False)
                                t = mm(pb[2][r, hsl[h]], m_kr[r, h % 2, h // 2, r], vtok[r, m, hsl[h]], start=False)
                            t.then_inc(pe_for_act, 1)
                    pe.wait_ge(dve_for_pe, turn.next())
                    for hp in range(HP):
                        t = tr(pb[0][:, hp * P:(hp + 1) * P], stb[:, hp, :])
                    t.then_inc(pe_for_dve, 1)
                    c["pe_from_act"].skip(1)

                @block.vector
                def _(v):
                    dv = c["dve"]
                    done = c["dve_from_pe"]
                    v.wait_ge(stored, states_stored)

                    def mask(dst, kp, bank):
                        for g in range(2):
                            t = V.tensor_tensor(dst[:, g], at(pb[bank + g], 0, HP, P), bc(keep[:, kp], [P, HP, P], 1), mult)
                        dv(t)

                    v.wait_ge(pe_for_dve, done.next())
                    mask(m_ba, 0, 4)
                    V.sem_inc(dve_for_pe, 1)
                    for m in range(MT):
                        for lv in range(6):
                            for g in range(2):
                                v.wait_ge(pe_for_dve, done.next(2 if m == lv == g == 0 else 1))
                                dv(V.tensor_tensor(m1[:, g], at(pb[g], 0, HP, P), bc(level[:, lv], [P, HP, P], 1), mult))
                                V.sem_inc(dve_for_pe, 1)
                            if lv == 0:
                                mask(m_br, 1, 6)
                                V.sem_inc(dve_for_pe, 1)
                                v.wait_ge(pe_for_dve, done.next())
                                mask(m_ka, 0, 2)
                            for g in range(2):
                                v.wait_ge(pe_for_dve, done.next())
                                if lv == 0:
                                    V.tensor_tensor(xm[:, g], m1[:, g], bc(ident, [P, HP, P], 1), add)
                                elif lv < 5:
                                    V.tensor_tensor(xm[:, g], xm[:, g], at(pb[2 + g], 0, HP, P), add)
                                dv(V.tensor_tensor(xt[:, g], bc(ident, [P, HP, P], 1) if lv == 0 else xt[:, g],
                                                   at(pb[4 + g], 0, HP, P), add))
                                if lv < 5:
                                    V.sem_inc(dve_for_pe, 1)
                            if lv == 0:
                                v.wait_ge(pe_for_dve, done.next())
                                mask(m_kr, 1, 6)
                        for cc in range(2):
                            r = slice(cc * 64, (cc + 1) * 64)
                            V.sem_inc(dve_for_pe, 1)
                            v.wait_ge(pe_for_dve, done.next())
                            dv(V.tensor_copy(rhs1[r], pb[0][r]))
                            V.sem_inc(dve_for_pe, 1)
                            v.wait_ge(pe_for_dve, done.next())
                            dv(V.tensor_copy(uu[r], pb[1][r]))
                            V.sem_inc(dve_for_pe, 1)
                            if m + 1 < MT:
                                v.wait_ge(pe_for_dve, done.next())
                                if cc == 0:
                                    mask(m_ba, 0, 4)
                            v.wait_ge(pe_for_dve, done.next())
                            upd = at(m1.rearrange("p g q t -> p (g q t)"), 0, HP, P)
                            dv(V.tensor_tensor(upd, at(pb[3], 0, HP, P), bc(blk, [P, HP, P], 1), mult))
                            dv(V.tensor_tensor(stb, stb, upd, add))
                            dv(V.tensor_tensor(stb, stb, bc(dend[:, :, 2 * m + cc], [P, HP, P], 2), mult))
                        V.sem_inc(dve_for_pe, 1)
                    v.wait_ge(pe_for_dve, done.next())
                    dv(V.tensor_copy(uu, pb[0]))
                    V.sem_inc(dve_for_sp, 1)

                @block.scalar
                def _(s):
                    for n in range(2 * MT):
                        r = slice(n % 2 * 64, (n % 2 + 1) * 64)
                        s.wait_ge(pe_for_act, c["act_from_pe"].next())
                        c["act"](S.activation(ytok[r, n // 2], pb[2][r], ACT.Copy))
                        S.sem_inc(act_for_pe, 1)

                @block.sync
                def _(sp):
                    sp.wait_ge(dve_for_sp, c["sp_from_dve"].next())
                    o = Lo(rwkv_p).rearrange("o (q g) i j -> g i (o q) j", g=2)
                    for g in range(2):
                        sp.dma_start(o[g], at(arena, 7264, HP, P)[g * 64:(g + 1) * 64, :, g * 64:(g + 1) * 64]).then_inc(stored, 16)
                    sp.wait_ge(stored, c["stored"].next(32))

            with nc.Block() as block:
                sq = at(arena, 0, 5, 512)
                ms = small[:, 160:200]
                mu_ = small[:, 330:370]
                pe_part, dve_part = heads_to_columns(None, [ytok], yT[:, 8:12, :])

                @block.sync
                def _(sp):
                    load_w(sp, 0, w_in[:, GATE0:GATE0 + 512])

                @block.scalar
                def _(s):
                    s.wait_ge(dve_for_act, c["act_from_dve"].next())
                    c["act"](S.activation(ms, ms, ACT.Sqrt, bias=eps_ln, scale=1.0 / DC))
                    S.sem_inc(act_for_dve, 1)

                @block.tensor
                def _(pe):
                    for m in range(5):
                        r = P if m < MT else DEC
                        mm(pb[m][0:r], gd[:, 0, m * P:m * P + r], w_g1, stop=False)
                        t = mm(pb[m][0:r], gd[0:32, 1, m * P:m * P + r], w_g2, start=False)
                    t.then_inc(pe_for_dve, 1)
                    pe_part(pe)

                @block.vector
                def _(v):
                    dv = c["dve"]
                    yg = ytok.rearrange("p m (g d) -> p (m g) d", d=DC)
                    vg = vtok.rearrange("p m (g d) -> p (m g) d", d=DC)
                    sg_ = sq.rearrange("p m (g d) -> p (m g) d", d=DC)
                    dv(V.tensor_reduce(mu_, yg, AX.X, add))
                    dv(V.tensor_scalar(mu_, mu_, 1.0 / DC, None, mult))
                    dv(V.tensor_tensor(yg, yg, bc(mu_, [P, 40, DC], 2), sub))
                    dv(V.tensor_tensor(sq, ytok, ytok, mult))
                    dv(V.tensor_reduce(ms, sg_, AX.X, add))
                    V.sem_inc(dve_for_act, 1)
                    v.wait_ge(act_for_dve, c["dve_from_act"].next())
                    dv(V.reciprocal(ms, ms))
                    dv(V.tensor_tensor(yg, yg, bc(ms, [P, 40, DC], 2), mult))
                    dv(V.tensor_tensor(ytok, ytok, bc(BR("lnx_g"), [P, 5, 512], 1), mult))
                    dv(V.tensor_tensor(ytok, ytok, bc(BR("lnx_b"), [P, 5, 512], 1), add))
                    dv(V.tensor_tensor(sg_, vg, bc(bonus.rearrange("p m h -> p (m h)"), [P, 40, DC], 2), mult))
                    dv(V.tensor_tensor(ytok, ytok, sq, add))
                    v.wait_ge(pe_for_dve, c["dve_from_pe"].next())
                    for m in range(5):
                        r = P if m < MT else DEC
                        dv(V.tensor_tensor(ytok[0:r, m], ytok[0:r, m], pb[m][0:r], mult))
                    dve_part(v)

            merged = at(arena, 0, KD, T)
            ysp = [x.rearrange("p (k t) -> p k t", k=HP) for x in y_split]
            msp = [x.rearrange("p (k t) -> p k t", k=KD) for x in m_split]
            fsp = [x.rearrange("p (k t) -> p k t", k=KD) for x in (h_raw[0][:, 0:KD * T], h_raw[1][:, 0:KD * T])]
            with nc.Block() as block:
                sgb = at(arena, 4160, 4, T)
                tmp = at(arena, 6240, 2, T)
                names = ("w_up_a", "w_up_b", "w_up_c")

                @block.sync
                def _(sp):
                    for q in range(6):
                        n, og = q // 2, q % 2
                        g0 = GATE0 + n * D + og * 512
                        if q:
                            load_w(sp, 0, w_in[:, g0:g0 + 512])
                        load_w4(sp, 1, L(names[n])[:, og * 512:(og + 1) * 512])
                    prefetch(sp, L("w_out")[:, 0:512], L("w_out")[:, 512:1024])

                @block.tensor
                def _(pe):
                    for q in range(6):
                        for u in range(2):
                            fm_unit(pe, w_split, 3 * q + u, hT[0], hT[1], 4 * u, c["pe_from_dve"], pe_for_act,
                                    first=(u == 0), last=(u == 1))
                        if q % 2 == 0:
                            pe.wait_ge(y_split_ready, q // 2 + 1)
                        fm_unit(pe, w_split, 3 * q + 2, ysp[0], ysp[1], 0, c["pe_from_act"], pe_for_dve)
                    c["pe_from_dve"].skip(4)

                @block.scalar
                def _(s):
                    split_hi(s, w_split, 0, 0, 0)
                    split_hi(s, w_split, 1, 0, 1, first=False)
                    for q in range(6):
                        s.wait_ge(split_free, c["split_free"].next())
                        split_hi(s, w_split, 3 * q + 2, 1)
                        for ct in range(4):
                            s.wait_ge(pe_for_act, c["act_from_pe"].next())
                            for half in range(2):
                                c["act"](S.activation(sgb[:, ct, half * TH:(half + 1) * TH], pb[4 * half + ct][:, 0:TH],
                                                      ACT.Sigmoid))
                            S.sem_inc(act_for_pe, 1)
                            S.sem_inc(act_for_dve, 1)
                        split_hi(s, w_split, 3 * q + 3, 0, 0)
                        s.wait_ge(dve_for_act, c["act_from_dve"].next())
                        if q < 5:
                            split_hi(s, w_split, 3 * q + 4, 0, 1, first=False)

                @block.vector
                def _(v):
                    dv = c["dve"]

                    def split_y(n):
                        ys = yT[:, 4 * n:4 * n + 4]
                        dv(V.tensor_copy(ysp[0], ys))
                        dv(V.tensor_tensor(ysp[1], ys, ysp[0].bitcast(F32), sub))
                        V.sem_inc(y_split_ready, 1)

                    V.sem_inc(dve_for_pe, 4)
                    split_lo(v, w_split, 0, 0, 0, last=False)
                    split_lo(v, w_split, 1, 0, 1)
                    split_y(0)
                    for q in range(6):
                        n, og = q // 2, q % 2
                        split_lo(v, w_split, 3 * q + 2, 1)
                        split_lo(v, w_split, 3 * q + 3, 0, 0, last=False)
                        for ct in range(4):
                            b = ct % 2
                            mg = merged[:, og * 4 + ct, :]
                            dst = mg if n == 0 else tmp[:, b]
                            v.wait_ge(act_for_dve, c["dve_from_act"].next())
                            v.wait_ge(pe_for_dve, c["dve_from_pe"].next())
                            for half in range(2):
                                hs = slice(half * TH, (half + 1) * TH)
                                dv(V.tensor_tensor(dst[:, hs], sgb[:, ct, hs], pb[4 * half + ct][:, 0:TH], mult))
                            V.sem_inc(dve_for_pe, 1)
                            if ct == 3:
                                V.sem_inc(dve_for_act, 1)
                            if n:
                                dv(V.tensor_tensor(mg, mg, tmp[:, b], add))
                        if q < 5:
                            split_lo(v, w_split, 3 * q + 4, 0, 1)
                        if q in (1, 3):
                            split_y(n + 1)

            def residual(v, dv, kt, bank, gate0, tmp8):
                g = modT[:, gate0 + kt, 0:1]
                dv(V.scalar_tensor_tensor(xT[:, kt, 0:TH], pb[bank][:, 0:TH], g, xT[:, kt, 0:TH], mult, add))
                dv(V.scalar_tensor_tensor(xT[:, kt, TH:SEQ], pb[4 + bank][:, 0:SEQ - TH], g, xT[:, kt, TH:SEQ], mult, add))
                dv(V.tensor_tensor(tmp8, pb[4 + bank][:, SEQ - TH:TH], modT[:, gate0 + kt, 1:9], mult))
                V.sem_inc(dve_for_pe, 1)
                dv(V.tensor_tensor(xT[:, kt, SEQ:T], xT[:, kt, SEQ:T], tmp8, add))

            tmp8 = small[:, 400:408]
            with nc.Block() as block:
                @block.sync
                def _(sp):
                    sp.dma_start(x_raw, x_spill).then_inc(loaded, 16)
                    w1 = L("w_ff1")
                    prefetch(sp, w1[:, 0:512], w1[:, 512:1024])

                @block.tensor
                def _(pe):
                    for n in range(4):
                        if n < 2:
                            pe.wait_ge(dve_for_pe, c["pe_from_dve"].next())
                        fm_unit(pe, w_split, n, msp[0], msp[1], n % 2 * 4, c["pe_from_dve"] if n else None, pe_for_dve,
                                first=(n % 2 == 0), last=(n % 2 == 1))
                    c["pe_from_dve"].skip(4)

                @block.scalar
                def _(s):
                    for n in range(2):
                        if n:
                            split_hi(s, w_split, n, 0, n, first=False)
                        c["act"](S.activation(msp[0][:, 4 * n:4 * n + 4], merged[:, 4 * n:4 * n + 4], ACT.Copy))
                        S.sem_inc(act_for_dve, 1)
                    s.wait_ge(split_free, c["split_free"].next())
                    split_hi(s, w_split, 2, 1, 0)
                    s.wait_ge(dve_for_act, c["act_from_dve"].next())
                    split_hi(s, w_split, 3, 1, 1, first=False)
                    s.wait_ge(split_free, c["split_free"].next())

                @block.vector
                def _(v):
                    dv = c["dve"]
                    for n in range(2):
                        if n:
                            split_lo(v, w_split, n, 0, n, last=True)
                        v.wait_ge(act_for_dve, c["dve_from_act"].next())
                        dv(V.tensor_tensor(msp[1][:, 4 * n:4 * n + 4], merged[:, 4 * n:4 * n + 4],
                                           msp[0][:, 4 * n:4 * n + 4].bitcast(F32), sub))
                        V.sem_inc(dve_for_pe, 1)
                    split_lo(v, w_split, 2, 1, 0, last=False)
                    v.wait_ge(loaded, c["loaded"].next(16))
                    for b in range(2):
                        for ct in range(4):
                            v.wait_ge(pe_for_dve, c["dve_from_pe"].next())
                            if b == 0 and ct == 3:
                                V.sem_inc(dve_for_act, 1)
                            residual(v, c["dve"], 4 * b + ct, ct, 16, tmp8)
                        if b == 0:
                            split_lo(v, w_split, 3, 1, 1)

            norm_stage("norm2", 24, 32, False, f_split)

            ff = at(arena, 0, KF, T)
            with nc.Block() as block:
                @block.sync
                def _(sp):
                    w1 = L("w_ff1")
                    with sp.Fori(0, 3) as i:
                        for s in range(2):
                            c["sp_free"][s].enter(i, 1)
                            load_w(sp, s, w1[:, bass.ds(i * 1024 + (s + 2) * 512, 512)])
                    for s in range(2):
                        c["sp_free"][s].leave(3)
                    w2 = L("w_ff2")
                    prefetch(sp, w2[0:1024, 0:512], w2[1024:2048, 0:512])

                @block.tensor
                def _(pe):
                    for n in range(16):
                        fm_unit(pe, f_split, n, hT[0], hT[1], n % 2 * 4, c["pe_from_act"], pe_for_act,
                                first=(n % 2 == 0), last=(n % 2 == 1))
                    c["pe_from_act"].skip(4)

                @block.scalar
                def _(s):
                    S.sem_inc(act_for_pe, 4)
                    split_hi(s, f_split, 1, 0, 1, first=False)
                    for b in range(8):
                        s.wait_ge(split_free, c["split_free"].next())
                        if b < 7:
                            split_hi(s, f_split, 2 * b + 2, (b + 1) % 2, 0)
                        for ct in range(4):
                            f = ff[:, 4 * b + ct]
                            s.wait_ge(pe_for_act, c["act_from_pe"].next())
                            for half in range(2):
                                c["act"](S.activation(f[:, half * TH:(half + 1) * TH], pb[4 * half + ct][:, 0:TH], ACT.Relu))
                            S.sem_inc(act_for_pe, 1)
                            S.sem_inc(act_for_dve, 1)
                        if b < 7:
                            split_hi(s, f_split, 2 * b + 3, (b + 1) % 2, 1, first=False)

                @block.vector
                def _(v):
                    split_lo(v, f_split, 1, 0, 1)
                    for b in range(8):
                        if b < 7:
                            split_lo(v, f_split, 2 * b + 2, (b + 1) % 2, 0, last=False)
                        for ct in range(4):
                            f = ff[:, 4 * b + ct]
                            v.wait_ge(act_for_dve, c["dve_from_act"].next())
                            c["dve"](V.tensor_tensor(f, f, f, mult))
                        if b < 7:
                            split_lo(v, f_split, 2 * b + 3, (b + 1) % 2, 1)

            with nc.Block() as block:
                def ffu(n):
                    ks = slice(n % 2 * 4, n % 2 * 4 + 4)
                    return fsp[0][:, ks], fsp[1][:, ks], ff[:, n % 8 * 4:n % 8 * 4 + 4]

                @block.sync
                def _(sp):
                    w2 = L("w_ff2")
                    for og in range(2):
                        for kg in range(0 if og else 2, 4):
                            load_w(sp, kg % 2, w2[kg * 1024:(kg + 1) * 1024, og * 512:(og + 1) * 512])

                @block.tensor
                def _(pe):
                    for n in range(16):
                        fm_unit(pe, f_split, n, fsp[0], fsp[1], n % 2 * 4, c["pe_from_dve"], pe_for_dve,
                                first=(n % 8 == 0), last=(n % 8 == 7))
                    c["pe_from_dve"].skip(4)

                @block.scalar
                def _(s):
                    for n in range(16):
                        if n == 9:
                            s.wait_ge(dve_for_act, c["act_from_dve"].next())
                        elif n >= 2:
                            s.wait_ge(split_free, c["split_free"].next())
                        split_hi(s, f_split, n, n // 2 % 2, n % 2, first=(n % 2 == 0), acts=ffu(n))
                    s.wait_ge(split_free, c["split_free"].next())

                @block.vector
                def _(v):
                    V.sem_inc(dve_for_pe, 4)
                    for n in range(9):
                        split_lo(v, f_split, n, n // 2 % 2, n % 2, last=(n % 2 == 1), acts=ffu(n))
                    for og in range(2):
                        for ct in range(4):
                            v.wait_ge(pe_for_dve, c["dve_from_pe"].next())
                            if og == 0 and ct == 3:
                                V.sem_inc(dve_for_act, 1)
                            residual(v, c["dve"], 4 * og + ct, ct, 40, tmp8)
                        if og == 0:
                            for n in range(9, 16):
                                split_lo(v, f_split, n, n // 2 % 2, n % 2, last=(n % 2 == 1), acts=ffu(n))
            clear()

        c = counts()
        with nc.Block() as block:
            @block.tensor
            def _(pe):
                for m in range(5):
                    if m >= 3:
                        pe.wait_ge(dve_for_pe, c["pe_from_dve"].next())
                    r = P if m < MT else DEC
                    for k in range(KD):
                        t = tr(pb[2 * (m % 3) + k // 4][0:r, (k % 4) * P:(k % 4 + 1) * P], xT[:, k, m * P:m * P + r])
                    t.then_inc(pe_for_dve, 1)

            @block.vector
            def _(v):
                for m in range(5):
                    r = P if m < MT else DEC
                    v.wait_ge(pe_for_dve, c["dve_from_pe"].next())
                    for j in range(2):
                        c["dve"](V.tensor_copy(arena[0:r, m * D + j * 512:m * D + (j + 1) * 512], pb[2 * (m % 3) + j][0:r]))
                    V.sem_inc(dve_for_pe, 1)
                    V.sem_inc(dve_for_sp, 1)

            @block.sync
            def _(sp):
                for m in range(5):
                    sp.wait_ge(dve_for_sp, c["sp_from_dve"].next())
                    if m < MT:
                        sp.dma_start(y_p[0, m * P:(m + 1) * P, :], arena[:, m * D:(m + 1) * D]).then_inc(stored, 16)
                    else:
                        sp.dma_start(y_s.rearrange("b o d -> b (o d)"), arena[0:DEC, m * D:(m + 1) * D]).then_inc(stored, 16)
                sp.wait_ge(stored, c["stored"].next(80))


_INS = ['x_prompt', 'x_sample', 'c_prompt', 'c_sample', 'cache_k_diff', 'cache_v_diff', 'page_table', 'state_ret',
        'state_rwkv', 'state_shift', 'rel_bias', 'w_ada', 'b_ada', 'norm1', 'norm2', 'w_in', 'qk_norm_q', 'qk_norm_k',
        'lambda_q1', 'lambda_k1', 'lambda_q2', 'lambda_k2', 'subln_diff', 'mu_shift', 'w0', 'w_decay_up', 'a0',
        'w_a_up', 'w_g_up', 'v0', 'w_v_down', 'w_v_up', 'k_k', 'k_a', 'r_k', 'lnx_g', 'lnx_b', 'w_up_a', 'w_up_b',
        'w_up_c', 'w_out', 'w_ff1', 'w_ff2']
_OUTS = [(1, SEQ, D), (DEC, 1, D), (DEPTH, 1, SEQ, HB, 2 * DB), (DEPTH, 1, SEQ, HB, DVB), (DEPTH, DEC, 1, HB, 2 * DB),
         (DEPTH, DEC, 1, HB, DVB), (DEPTH, 1, HA, DA, DA), (DEPTH, DEC, HA, DA, DA), (DEPTH, 1, HC, DC, DC),
         (DEPTH, DEC, HC, DC, DC), (DEPTH, 1, 1, RW), (DEPTH, DEC, 1, RW)]


def kernel(**inputs):
    import numpy as _np
    import concourse.bacc as _bacc
    from concourse import mybir as _mybir
    from concourse.bass_utils import run_bass_kernel_spmd as _run

    nc = _bacc.Bacc("TRN2", target_bir_lowering=False, num_devices=1)
    arrays, args = {}, {}
    for name in _INS:
        v = _np.ascontiguousarray(inputs[name])
        arrays[f"in_{name}_dram"] = v
        args[name] = nc.dram_tensor(f"in_{name}_dram", v.shape, _mybir.dt.from_np(v.dtype), kind="ExternalInput").ap()
    table = shape_constants()
    arrays["shape_constants_dram"] = table
    consts = nc.dram_tensor("shape_constants_dram", table.shape, F32, kind="ExternalInput").ap()
    outs = [nc.dram_tensor(f"out_{i}_dram", shape, F32, kind="ExternalOutput").ap() for i, shape in enumerate(_OUTS)]
    build(nc, args, consts, outs)
    r = _run(nc, [arrays], core_ids=[0])
    return tuple(r.results[0][f"out_{i}_dram"] for i in range(len(_OUTS)))
```
